# Optimizing a Trainium2 kernel written in Bass

```python
import math
import jax
import jax.numpy as jnp
from jax import lax
import numpy as np

D_MODEL = 1024
BATCH = 1
SEQ = 256
DEPTH = 2

CTX_LEN = 256
GRID_W = 64
HEAD_DIM = 64
ROPE_THETA = 10000.0
Q_BLOCK = 128
A_HEADS = 8
A_KV_HEADS = 2
W_HEADS = 8
W_KV_HEADS = 2
WINDOW = 128
SSM_HEADS = 16
SSM_HEAD_DIM = 64
SSM_INNER = SSM_HEADS * SSM_HEAD_DIM
SSM_GROUPS = 2
SSM_STATE = 128
SSM_CONV = 3
SSM_CONV_CH = SSM_INNER + 2 * SSM_GROUPS * SSM_STATE
SSM_CHUNK = 128
N_BRANCH = 3
IN_SPLITS = (A_HEADS * HEAD_DIM, A_KV_HEADS * HEAD_DIM, A_KV_HEADS * HEAD_DIM,
             W_HEADS * HEAD_DIM, W_KV_HEADS * HEAD_DIM, W_KV_HEADS * HEAD_DIM,
             SSM_INNER, SSM_CONV_CH, 2 * SSM_HEADS, N_BRANCH * D_MODEL)
IN_PROJ_WIDTH = sum(IN_SPLITS)
N_EXPERTS = 64
TOP_K = 8
N_EXPERT_GROUPS = 8
TOPK_GROUPS = 4
D_EXPERT = 256
D_SHARED = 256
ROUTED_SCALE = 2.5
MOE_BLOCK = 128
EPS = 1e-6

kernel_name = 'hybrid_gqa_ssd_swa_moe_dit'

def rmsnorm(x, g):
    xf = x.astype(jnp.float32)
    y = xf * lax.rsqrt(jnp.mean(xf * xf, axis=-1, keepdims=True) + EPS)
    return (y * g.astype(jnp.float32)).astype(x.dtype)

def modulate(h, shift, scale):
    return h * (1 + scale) + shift

def split_in_proj(p):
    points = [int(s) for s in np.cumsum(IN_SPLITS)[:-1]]
    return jnp.split(p, points, axis=-1)

def to_heads(t):
    return t.reshape(t.shape[:-1] + (t.shape[-1] // HEAD_DIM, HEAD_DIM))

def axial_rope_tables(n):
    ROWS = n // GRID_W
    row = jnp.repeat(jnp.arange(ROWS, dtype=jnp.float32), GRID_W)
    col = jnp.tile(jnp.arange(GRID_W, dtype=jnp.float32), ROWS)
    axis_dim = HEAD_DIM // 2
    inv_freq = ROPE_THETA ** (-jnp.arange(0, axis_dim, 2, dtype=jnp.float32) / axis_dim)
    ang_r = row[:, None] * inv_freq[None, :]
    ang_c = col[:, None] * inv_freq[None, :]
    return (jnp.cos(ang_r), jnp.sin(ang_r), jnp.cos(ang_c), jnp.sin(ang_c))

def rope_1d(t, cos, sin):
    m = t.shape[-1] // 2
    t1, t2 = t[..., :m], t[..., m:]
    cos = cos[:, None, :].astype(t.dtype)
    sin = sin[:, None, :].astype(t.dtype)
    return jnp.concatenate([t1 * cos - t2 * sin, t2 * cos + t1 * sin], axis=-1)

def apply_axial_rope(t, tables):
    cr, sr, cc, sc = tables
    a = HEAD_DIM // 2
    return jnp.concatenate([rope_1d(t[..., :a], cr, sr), rope_1d(t[..., a:], cc, sc)], axis=-1)

def dense_block_attn(q, k, v, sink=None):
    bsz, n, h, hd = q.shape
    hkv = k.shape[2]
    g = h // hkv
    nb = n // Q_BLOCK
    scale = hd ** -0.5
    qb = jnp.swapaxes(q.reshape(bsz, nb, Q_BLOCK, hkv, g, hd), 0, 1)

    def one(qblk):
        s = jnp.einsum('bqkgd,bmkd->bkgqm', qblk, k).astype(jnp.float32) * scale
        if sink is not None:
            sk = jnp.broadcast_to(sink.astype(jnp.float32).reshape(1, hkv, g, 1, 1), s.shape[:-1] + (1,))
            s = jnp.concatenate([s, sk], axis=-1)
        p = jax.nn.softmax(s, axis=-1)
        if sink is not None:
            p = p[..., :-1]
        o = jnp.einsum('bkgqm,bmkd->bqkgd', p.astype(v.dtype), v)
        return o.reshape(bsz, Q_BLOCK, h * hd)

    o = lax.map(one, qb)
    return jnp.swapaxes(o, 0, 1).reshape(bsz, n, h * hd)

def window_block_attn(q, k, v, kc, vc, sink):
    bsz, n, h, hd = q.shape
    hkv = k.shape[2]
    g = h // hkv
    nb = n // Q_BLOCK
    span = Q_BLOCK + 2 * WINDOW
    scale = hd ** -0.5
    pad = ((0, 0), (WINDOW, WINDOW), (0, 0), (0, 0))
    kp = jnp.pad(k, pad)
    vp = jnp.pad(v, pad)
    sink_l = sink.astype(jnp.float32).reshape(1, hkv, g, 1, 1)

    def one(b):
        q0 = b * Q_BLOCK
        qb = lax.dynamic_slice_in_dim(q, q0, Q_BLOCK, axis=1).reshape(bsz, Q_BLOCK, hkv, g, hd)
        kb = lax.dynamic_slice_in_dim(kp, q0, span, axis=1)
        vb = lax.dynamic_slice_in_dim(vp, q0, span, axis=1)
        qpos = q0 + jnp.arange(Q_BLOCK)
        kpos = q0 - WINDOW + jnp.arange(span)
        ok = (jnp.abs(qpos[:, None] - kpos[None, :]) <= WINDOW) & (kpos[None, :] >= 0) & (kpos[None, :] < n)
        s_loc = jnp.einsum('bqkgd,bmkd->bkgqm', qb, kb).astype(jnp.float32) * scale
        s_loc = jnp.where(ok, s_loc, -jnp.inf)
        s_ctx = jnp.einsum('bqkgd,bmkd->bkgqm', qb, kc).astype(jnp.float32) * scale
        s_snk = jnp.broadcast_to(sink_l, s_loc.shape[:-1] + (1,))
        p = jax.nn.softmax(jnp.concatenate([s_loc, s_ctx, s_snk], axis=-1), axis=-1).astype(v.dtype)
        o = (jnp.einsum('bkgqm,bmkd->bqkgd', p[..., :span], vb)
             + jnp.einsum('bkgqm,bmkd->bqkgd', p[..., span:span + kc.shape[1]], vc))
        return o.reshape(bsz, Q_BLOCK, h * hd)

    o = lax.map(one, jnp.arange(nb))
    return jnp.swapaxes(o, 0, 1).reshape(bsz, n, h * hd)

def dwconv_centred(u, w, b):
    kw = w.shape[0]
    out = lax.conv_general_dilated(u, w[:, None, :].astype(u.dtype), window_strides=(1,),
                                   padding=[(kw // 2, kw // 2)], dimension_numbers=('NWC', 'WIO', 'NWC'),
                                   feature_group_count=u.shape[-1])
    return out + b.astype(u.dtype)

def ssm_prep(xbc, dt, conv_w, conv_b, dt_bias):
    u = jax.nn.silu(dwconv_centred(xbc, conv_w, conv_b))
    xs, bm, cm = jnp.split(u, [SSM_INNER, SSM_INNER + SSM_GROUPS * SSM_STATE], axis=-1)
    shp = xs.shape[:-1]
    xs = xs.reshape(shp + (SSM_HEADS, SSM_HEAD_DIM))
    bm = bm.reshape(shp + (SSM_GROUPS, SSM_STATE))
    cm = cm.reshape(shp + (SSM_GROUPS, SSM_STATE))
    dt = jax.nn.softplus(dt.astype(jnp.float32) + dt_bias.reshape(-1).astype(jnp.float32))
    return xs, bm, cm, dt[..., :SSM_HEADS], dt[..., SSM_HEADS:]

def ssd_scan(x, dt, a_neg, bm, cm, s0):
    bsz, seq, nh, hp = x.shape
    ng, ns = bm.shape[2], bm.shape[3]
    r = nh // ng
    q = SSM_CHUNK
    nc = seq // q
    a = (dt * a_neg).reshape(bsz, nc, q, ng, r)
    ac = jnp.cumsum(a, axis=2).transpose(0, 1, 3, 4, 2)
    xd = (x.astype(jnp.float32) * dt[..., None]).reshape(bsz, nc, q, ng, r, hp)
    bc = bm.astype(jnp.float32).reshape(bsz, nc, q, ng, ns)
    cc = cm.astype(jnp.float32).reshape(bsz, nc, q, ng, ns)
    tri = jnp.tril(jnp.ones((q, q), dtype=bool))
    decay = jnp.exp(jnp.where(tri, ac[..., :, None] - ac[..., None, :], -jnp.inf))
    cb = jnp.einsum('bcign,bcjgn->bcgij', cc, bc)
    y_diag = jnp.einsum('bcgrij,bcjgrp->bcigrp', cb[:, :, :, None] * decay, xd)
    end_decay = jnp.exp(ac[..., -1:] - ac).transpose(0, 1, 4, 2, 3)
    chunk_states = jnp.einsum('bcjgn,bcjgrp->bcgrpn', bc, xd * end_decay[..., None])
    chunk_decay = jnp.exp(ac[..., -1])

    def step(s, inp):
        st, dec = inp
        return s * dec[..., None, None] + st, s

    s_fin, s_start = lax.scan(step, s0, (jnp.moveaxis(chunk_states, 1, 0), jnp.moveaxis(chunk_decay, 1, 0)))
    s_start = jnp.moveaxis(s_start, 0, 1)
    in_decay = jnp.exp(ac).transpose(0, 1, 4, 2, 3)[..., None]
    y_off = jnp.einsum('bcign,bcgrpn->bcigrp', cc, s_start) * in_decay
    y = (y_diag + y_off).reshape(bsz, seq, nh, hp)
    return y.astype(x.dtype), s_fin

def flip_seq(t):
    return jnp.flip(t, axis=1)

def ssd_bidir(xs, dt_f, dt_b, bm, cm, a_neg, d_skip, s0_f, s0_b):
    y_f, s_f = ssd_scan(xs, dt_f, a_neg[0], bm, cm, s0_f)
    y_b, s_b = ssd_scan(flip_seq(xs), flip_seq(dt_b), a_neg[1], flip_seq(bm), flip_seq(cm), s0_b)
    y = y_f + flip_seq(y_b) + d_skip.astype(xs.dtype)[:, None] * xs
    return y, s_f, s_b

def gated_group_rmsnorm(y, z, g):
    u = (y * jax.nn.silu(z)).astype(jnp.float32)
    shp = u.shape
    ug = u.reshape(shp[:-1] + (SSM_GROUPS, shp[-1] // SSM_GROUPS))
    ug = ug * lax.rsqrt(jnp.mean(ug * ug, axis=-1, keepdims=True) + EPS)
    return (ug.reshape(shp) * g.astype(jnp.float32)).astype(y.dtype)

def merge_branches(oa, ow, ys, gates, w_br_a, w_br_w, w_br_s, w_out):
    ga, gw, gs = jnp.split(jax.nn.sigmoid(gates), N_BRANCH, axis=-1)
    return (ga * (oa @ w_br_a) + gw * (ow @ w_br_w) + gs * (ys @ w_br_s)) @ w_out

def hybrid_mixer(hl, hc, rope, w_in, g_q, g_k, sink, conv_w, conv_b, dt_bias, a_log, d_skip, norm_w,
                 w_br_a, w_br_w, w_br_s, w_out, with_ctx_out):
    pl = split_in_proj(hl @ w_in)
    pc = split_in_proj(hc @ w_in)
    qa = apply_axial_rope(rmsnorm(to_heads(pl[0]), g_q), rope)
    ka = apply_axial_rope(rmsnorm(to_heads(pl[1]), g_k), rope)
    va = to_heads(pl[2])
    ka_c = rmsnorm(to_heads(pc[1]), g_k)
    va_c = to_heads(pc[2])
    oa = dense_block_attn(qa, jnp.concatenate([ka, ka_c], axis=1), jnp.concatenate([va, va_c], axis=1))
    qw = apply_axial_rope(to_heads(pl[3]), rope)
    kw = apply_axial_rope(to_heads(pl[4]), rope)
    vw = to_heads(pl[5])
    kw_c = to_heads(pc[4])
    vw_c = to_heads(pc[5])
    ow = window_block_attn(qw, kw, vw, kw_c, vw_c, sink)
    a_neg = -jnp.exp(a_log.astype(jnp.float32))
    bsz = hl.shape[0]
    s0 = jnp.zeros((bsz, SSM_GROUPS, SSM_HEADS // SSM_GROUPS, SSM_HEAD_DIM, SSM_STATE), jnp.float32)
    xs_c, bm_c, cm_c, dtf_c, dtb_c = ssm_prep(pc[7], pc[8], conv_w, conv_b, dt_bias)
    ys_c, s_f, s_b = ssd_bidir(xs_c, dtf_c, dtb_c, bm_c, cm_c, a_neg, d_skip, s0, s0)
    xs_l, bm_l, cm_l, dtf_l, dtb_l = ssm_prep(pl[7], pl[8], conv_w, conv_b, dt_bias)
    ys_l, _, _ = ssd_bidir(xs_l, dtf_l, dtb_l, bm_l, cm_l, a_neg, d_skip, s_f, s_b)
    ys = gated_group_rmsnorm(ys_l.reshape(ys_l.shape[:2] + (SSM_INNER,)), pl[6], norm_w)
    ml = merge_branches(oa, ow, ys, pl[9], w_br_a, w_br_w, w_br_s, w_out)
    if not with_ctx_out:
        return ml, None
    qa_c = rmsnorm(to_heads(pc[0]), g_q)
    oa_c = dense_block_attn(qa_c, ka_c, va_c)
    ow_c = dense_block_attn(to_heads(pc[3]), kw_c, vw_c, sink)
    ysc = gated_group_rmsnorm(ys_c.reshape(ys_c.shape[:2] + (SSM_INNER,)), pc[6], norm_w)
    mc = merge_branches(oa_c, ow_c, ysc, pc[9], w_br_a, w_br_w, w_br_s, w_out)
    return ml, mc

def moe_ffn(x, w_router, b_router, we_gate, we_up, we_down, ws_gate, ws_up, ws_down):
    t_count, d = x.shape
    scores = jax.nn.sigmoid((x @ w_router).astype(jnp.float32))
    sel = scores + b_router.astype(jnp.float32)
    per_group = N_EXPERTS // N_EXPERT_GROUPS
    group_score = lax.top_k(sel.reshape(t_count, N_EXPERT_GROUPS, per_group), 2)[0].sum(-1)
    _, gidx = lax.top_k(group_score, TOPK_GROUPS)
    gmask = jnp.any(gidx[:, :, None] == jnp.arange(N_EXPERT_GROUPS)[None, None, :], axis=1)
    sel = jnp.where(jnp.repeat(gmask, per_group, axis=1), sel, -jnp.inf)
    _, eidx = lax.top_k(sel, TOP_K)
    wts = jnp.take_along_axis(scores, eidx, axis=1)
    wts = wts / jnp.sum(wts, axis=-1, keepdims=True) * ROUTED_SCALE
    tk = t_count * TOP_K
    flat_e = eidx.reshape(-1)
    order = jnp.argsort(flat_e)
    se = flat_e[order]
    st = (order // TOP_K).astype(jnp.int32)
    sw = wts.reshape(-1)[order]
    counts = jnp.bincount(flat_e, length=N_EXPERTS)
    padded = (counts + MOE_BLOCK - 1) // MOE_BLOCK * MOE_BLOCK
    pad_end = jnp.cumsum(padded)
    pad_start = pad_end - padded
    start = jnp.cumsum(counts) - counts
    dest = pad_start[se] + jnp.arange(tk) - start[se]
    n_blocks = -(-(tk + N_EXPERTS * (MOE_BLOCK - 1)) // MOE_BLOCK)
    cap = n_blocks * MOE_BLOCK
    buf_t = jnp.zeros((cap,), jnp.int32).at[dest].set(st)
    buf_w = jnp.zeros((cap,), jnp.float32).at[dest].set(sw)
    blk_e = jnp.minimum(jnp.searchsorted(pad_end, jnp.arange(n_blocks) * MOE_BLOCK, side='right'), N_EXPERTS - 1)

    def body(acc, inp):
        t_blk, w_blk, e = inp
        xb = x[t_blk]
        hb = jax.nn.silu(xb @ we_gate[e]) * (xb @ we_up[e])
        yb = (hb @ we_down[e]).astype(jnp.float32) * w_blk[:, None]
        return acc.at[t_blk].add(yb), None

    routed, _ = lax.scan(body, jnp.zeros((t_count, d), jnp.float32),
                         (buf_t.reshape(n_blocks, MOE_BLOCK), buf_w.reshape(n_blocks, MOE_BLOCK), blk_e))
    shared = (jax.nn.silu(x @ ws_gate) * (x @ ws_up)) @ ws_down
    return (routed + shared.astype(jnp.float32)).astype(x.dtype)

def setup_inputs(seed: int = 0) -> dict:
    key = jax.random.key(seed)
    ks = iter(jax.random.split(key, 40))
    f32 = jnp.float32
    D = D_MODEL
    L = DEPTH

    def nrm(shape, scale):
        return scale * jax.random.normal(next(ks), shape, f32)

    x = nrm((BATCH, SEQ, D), 1.0)
    c = nrm((BATCH, D), 1.0)
    ctx = nrm((BATCH, CTX_LEN, D), 1.0)
    c_ctx = nrm((D,), 1.0)
    w_ada = nrm((L, D, 6 * D), 0.5 * D ** -0.5)
    b_ada = nrm((L, 6 * D), 0.02)
    g_mix_pre = 1.0 + nrm((L, D), 0.05)
    g_mix_post = 1.0 + nrm((L, D), 0.05)
    g_ffn_pre = 1.0 + nrm((L, D), 0.05)
    g_ffn_post = 1.0 + nrm((L, D), 0.05)
    w_in = nrm((L, D, IN_PROJ_WIDTH), D ** -0.5)
    g_q_a = 1.0 + nrm((L, HEAD_DIM), 0.05)
    g_k_a = 1.0 + nrm((L, HEAD_DIM), 0.05)
    sink_w = nrm((L, W_HEADS), 0.5)
    ssm_conv_w = nrm((L, SSM_CONV, SSM_CONV_CH), SSM_CONV ** -0.5)
    ssm_conv_b = nrm((L, SSM_CONV_CH), 0.02)
    dt0 = jnp.exp(jax.random.uniform(next(ks), (L, 2, SSM_HEADS), f32, math.log(1e-3), math.log(1e-1)))
    ssm_dt_bias = dt0 + jnp.log(-jnp.expm1(-dt0))
    ssm_a_log = jnp.log(jax.random.uniform(next(ks), (L, 2, SSM_HEADS), f32, 1.0, 16.0))
    ssm_d = 1.0 + nrm((L, SSM_HEADS), 0.1)
    ssm_norm = 1.0 + nrm((L, SSM_INNER), 0.05)
    w_br_a = nrm((L, A_HEADS * HEAD_DIM, D), (A_HEADS * HEAD_DIM) ** -0.5)
    w_br_w = nrm((L, W_HEADS * HEAD_DIM, D), (W_HEADS * HEAD_DIM) ** -0.5)
    w_br_s = nrm((L, SSM_INNER, D), SSM_INNER ** -0.5)
    w_out = nrm((L, D, D), D ** -0.5)
    w_router = nrm((L, D, N_EXPERTS), D ** -0.5)
    b_router = nrm((L, N_EXPERTS), 0.01)
    we_gate = nrm((L, N_EXPERTS, D, D_EXPERT), D ** -0.5)
    we_up = nrm((L, N_EXPERTS, D, D_EXPERT), D ** -0.5)
    we_down = nrm((L, N_EXPERTS, D_EXPERT, D), D_EXPERT ** -0.5)
    ws_gate = nrm((L, D, D_SHARED), D ** -0.5)
    ws_up = nrm((L, D, D_SHARED), D ** -0.5)
    ws_down = nrm((L, D_SHARED, D), D_SHARED ** -0.5)
    return {'x': x, 'c': c, 'ctx': ctx, 'c_ctx': c_ctx, 'w_ada': w_ada, 'b_ada': b_ada,
            'g_mix_pre': g_mix_pre, 'g_mix_post': g_mix_post, 'g_ffn_pre': g_ffn_pre, 'g_ffn_post': g_ffn_post,
            'w_in': w_in, 'g_q_a': g_q_a, 'g_k_a': g_k_a, 'sink_w': sink_w,
            'ssm_conv_w': ssm_conv_w, 'ssm_conv_b': ssm_conv_b, 'ssm_dt_bias': ssm_dt_bias,
            'ssm_a_log': ssm_a_log, 'ssm_d': ssm_d, 'ssm_norm': ssm_norm,
            'w_br_a': w_br_a, 'w_br_w': w_br_w, 'w_br_s': w_br_s, 'w_out': w_out,
            'w_router': w_router, 'b_router': b_router, 'we_gate': we_gate, 'we_up': we_up, 'we_down': we_down,
            'ws_gate': ws_gate, 'ws_up': ws_up, 'ws_down': ws_down}

def reference(x, c, ctx, c_ctx, w_ada, b_ada, g_mix_pre, g_mix_post, g_ffn_pre, g_ffn_post,
              w_in, g_q_a, g_k_a, sink_w, ssm_conv_w, ssm_conv_b, ssm_dt_bias, ssm_a_log, ssm_d, ssm_norm,
              w_br_a, w_br_w, w_br_s, w_out, w_router, b_router, we_gate, we_up, we_down,
              ws_gate, ws_up, ws_down):
    d = x.shape[-1]
    rope = axial_rope_tables(x.shape[1])
    xl, xc = x, ctx
    for i in range(DEPTH):
        last = i == DEPTH - 1
        mod_l = jnp.split((jax.nn.silu(c) @ w_ada[i] + b_ada[i])[:, None, :], 6, axis=-1)
        mod_c = jnp.split(jax.nn.silu(c_ctx) @ w_ada[i] + b_ada[i], 6, axis=-1)
        hl = modulate(rmsnorm(xl, g_mix_pre[i]), mod_l[0], mod_l[1])
        hc = modulate(rmsnorm(xc, g_mix_pre[i]), mod_c[0], mod_c[1])
        ml, mc = hybrid_mixer(hl, hc, rope, w_in[i], g_q_a[i], g_k_a[i], sink_w[i],
                              ssm_conv_w[i], ssm_conv_b[i], ssm_dt_bias[i], ssm_a_log[i], ssm_d[i], ssm_norm[i],
                              w_br_a[i], w_br_w[i], w_br_s[i], w_out[i], not last)
        xl = xl + mod_l[2] * rmsnorm(ml, g_mix_post[i])
        hl = modulate(rmsnorm(xl, g_ffn_pre[i]), mod_l[3], mod_l[4])
        moe_w = (w_router[i], b_router[i], we_gate[i], we_up[i], we_down[i], ws_gate[i], ws_up[i], ws_down[i])
        if last:
            fl = moe_ffn(hl.reshape(-1, d), *moe_w).reshape(hl.shape)
        else:
            xc = xc + mod_c[2] * rmsnorm(mc, g_mix_post[i])
            hc = modulate(rmsnorm(xc, g_ffn_pre[i]), mod_c[3], mod_c[4])
            n_lat = hl.shape[0] * hl.shape[1]
            f = moe_ffn(jnp.concatenate([hl.reshape(-1, d), hc.reshape(-1, d)], axis=0), *moe_w)
            fl = f[:n_lat].reshape(hl.shape)
            xc = xc + mod_c[5] * rmsnorm(f[n_lat:].reshape(hc.shape), g_ffn_post[i])
        xl = xl + mod_l[5] * rmsnorm(fl, g_ffn_post[i])
    return xl


_drawn_inputs = setup_inputs


def setup_inputs(seed=0):
    import zlib

    import numpy as np

    out = dict(_drawn_inputs(seed))
    spreads = {}
    factors = {'g_q_a': 2.98, 'g_k_a': 5.211, 'sink_w': 8.0}
    for name, (base, spread) in spreads.items():
        noise = np.random.default_rng([zlib.crc32(name.encode()), seed]).standard_normal(out[name].shape)
        drawn = base * np.exp(spread * noise) if base else spread * noise
        out[name] = jnp.asarray(drawn.astype(out[name].dtype))
    for name, factor in factors.items():
        out[name] = (out[name] * factor).astype(out[name].dtype)
    return out
```

```python
import numpy as np
from contextlib import ExitStack
import concourse.bass as bass
from concourse import mybir

F32 = mybir.dt.float32
ALU = mybir.AluOpType
ACT = mybir.ActivationFunctionType
AX = mybir.AxisListType

P = 128
D = 1024
KD = D // P
DEPTH = 2
LAT_TILES, CTX_TILES = 2, 2
TILES = LAT_TILES + CTX_TILES
TOK = TILES * P
SEG = LAT_TILES * P
HD = 64
HEADS, KV = 8, 2
GQ = HEADS // KV
SH, SP_, SG, SN = 16, 64, 2, 128
SI = SH * SP_
CONV_T = 12
N_EXP, D_EXP = 64, 256
EPS = 1e-6
NEG = -1.0e30
SCALE = HD ** -0.5
ROUTED_SCALE = 2.5
NCH = 512
COL_XBC, COL_DT, COL_QKV, COL_Z, COL_GATE = 2560, 4096, 0, 1536, 4128
RING = 3
EXP_SLOTS = 2

LOOP_SEMS = ("mm_gu", "mm_hT", "mm_down", "hidden", "ev_hT", "ev_down", "silu")

C_ID, C_UT, C_LT, C_NA, C_NB, C_ONE, C_COS, C_SIN, C_SEL, C_TRI8, C_END = (
    0, 128, 256, 384, 512, 640, 768, 896, 1024, 1280, 1344)


def constants():
    c = np.zeros((P, C_END), np.float32)
    i = np.arange(P)
    c[:, C_ID:C_ID + P] = np.eye(P)
    c[:, C_UT:C_UT + P] = i[:, None] <= i[None, :]
    c[:, C_LT:C_LT + P] = i[:, None] >= i[None, :]
    c[:, C_NA:C_NA + P] = np.where(i[None, :] > i[:, None], NEG, 0)
    c[:, C_NB:C_NB + P] = np.where(i[None, :] < i[:, None], NEG, 0)
    c[:, C_ONE:C_ONE + P] = 1
    half = HD // 2
    inv = np.float32(10000.0) ** (-np.arange(0, half, 2, dtype=np.float32) / np.float32(half))
    for t in range(LAT_TILES):
        tok = t * P + i
        ang = np.stack([(tok // 64).astype(np.float32)[:, None] * inv, (tok % 64).astype(np.float32)[:, None] * inv], 1)
        co, si = np.cos(ang), np.sin(ang)
        c[:, C_COS + t * HD:C_COS + (t + 1) * HD] = np.stack([co, co], 2).reshape(P, HD)
        c[:, C_SIN + t * HD:C_SIN + (t + 1) * HD] = np.stack([-si, si], 2).reshape(P, HD)
    c[0, C_SEL:C_SEL + P] = 1
    c[1, C_SEL + P:C_SEL + 2 * P] = 1
    g = np.arange(8)
    c[:, C_TRI8:C_TRI8 + 64] = (g[None, :] < g[:, None]).reshape(1, 64)
    return c


def ring_jobs():
    jobs = []
    for l in range(DEPTH):
        jobs += [(l, "ada0", n) for n in range(6)]
        jobs += [(l, "xbc", n) for n in range(3)]
        jobs += [(l, "qkv", n) for n in range(3)]
        jobs += [(l, "z", n) for n in range(2)]
        for b in range(3):
            for n in range(2):
                jobs += [(l, "gate", b * 2 + n), (l, "br", b * 2 + n)]
        jobs += [(l, "out", n) for n in range(2)]
        jobs += [(l, "ada1", n) for n in range(6)]
    return jobs


def build(nc, a, cst_d, out):
    jobs = ring_jobs()
    job_at = {j: i for i, j in enumerate(jobs)}
    per_layer = len(jobs) // DEPTH
    out_tiles = [TILES, LAT_TILES]
    before = BEFORE
    ctx = ExitStack()
    with ctx:
        top = [nc.sbuf_base + 31 & ~31]

        def at(name, shape, offset, dt=F32):
            return nc.alloc_sbuf_tensor_at(name, shape, dt, offset=offset)

        def region(nbytes):
            o = top[0]
            top[0] += nbytes + 31 & ~31
            return o

        sems = {}

        def sem(name):
            stem = name[:-2]
            if name[-2:] in ("_0", "_1") and stem not in LOOP_SEMS:
                name = stem
            if name not in sems:
                sems[name] = ctx.enter_context(nc.semaphore(name))
            return sems[name]

        def stage(name, value):
            base = before[name[:-2]] if name.endswith("_1") and name[:-2] not in LOOP_SEMS else 0
            return sem(name), base + value

        x = at("x", [P, TILES, D], region(TILES * D * 4))
        hT = at("hT", [P, KD, TOK], region(KD * TOK * 4))
        r_ring = region(RING * KD * NCH * 4)
        ring = at("ring", [P, RING, KD, NCH], r_ring)
        esl = at("esl", [P, EXP_SLOTS, 3, 2048], r_ring)
        r_bc = region(6 * D * 4)
        bc = at("bc", [P, 3, 2, D], r_bc)
        zs = at("zs", [P, TILES, D], r_bc)
        mT = at("mT", [P, KD, TOK], r_bc)
        cst = at("cst", [P, C_END], region(C_END * 4))
        r_qk = region(TILES * 1536 * 4)
        qk = at("qk", [P, TILES, 1536], r_qk)
        modrow = at("modrow", [2, 3, D], r_qk)
        bada = at("bada", [2, 3 * D], r_qk + 3 * D * 4)
        y = at("y", [P, TILES, D], r_qk)
        st = at("st", [P, 2, SI], r_qk + TILES * D * 4)
        acc = at("acc", [P, TILES, D], r_qk)
        r_qT = region(10 * TOK * 4)
        qT = at("qT", [P, 2, GQ, TOK], r_qT)
        kT = at("kT", [P, 2, TOK], r_qT + 2 * GQ * TOK * 4)
        oT = at("oT", [P, KD, TOK], r_qT)
        XPB = (2 * (SEG + 2) * 4 + 31) & ~31
        xp = [at(f"xp{i}", [P, 2, SEG + 2], r_qT + i * XPB) for i in range(2)]
        cacc = at("cacc", [P, 2, TOK], r_qT + 2 * XPB)
        cu = at("cu", [P, 2, TOK], r_qT + 2 * XPB + 2 * TOK * 4)
        gnorm = at("gnorm", [2, 2, D], r_qT)
        r_xs = region(TILES * SI * 4)
        xs = at("xs", [P, TILES, SI], r_xs)
        ysT = at("ysT", [P, KD, TOK], r_xs)
        ml = at("ml", [P, TILES, D], r_xs)
        bcc = at("bcc", [P, 4, TOK], region(4 * TOK * 4))
        btok = at("btok", [P, TILES, 2 * SN], region(TILES * 2 * SN * 4))
        r_t = region(3 * D * 4)
        hn = at("hn", [P, 2, D], r_t)
        pr = at("pr", [P, 2, NCH], r_t)
        pT = at("pT", [P, 2, NCH], r_t + 2 * NCH * 4)
        rt = at("rt", [P, 640], r_t)
        rq = at("rq", [P, 2, 640], r_t + 640 * 4)
        mt = at("mt", [P, 3, 8, P], r_t)
        tmp = at("tmp", [P, D], r_t + 2 * D * 4)
        gs = at("gs", [P, 2, NCH], r_t)
        junk = at("junk", [P, D], r_t + 2 * D * 4)
        hsg = at("hsg", [P, 2, D_EXP], r_t)
        hgT = at("hgT", [P, 2, 2, P], r_t + 2 * D_EXP * 4)
        gqk = at("gqk", [P, 640], r_t + 3 * 640 * 4)
        nsink = at("nsink", [P, HEADS], region(HEADS * 4))
        dtb = at("dtb", [P, 32], region(128))
        alog = at("alog", [P, 32], region(128))
        dsk = at("dsk", [P, SH], region(64))
        nw = at("nw", [P, SI], region(SI * 4))
        brt = at("brt", [P, N_EXP], region(256))
        crow = at("crow", [4 * CONV_T, P], region(512))
        ccol = at("ccol", [P, 4 * CONV_T], region(4 * CONV_T * 4))
        wdt = at("wdt", [P, KD, 32], region(KD * 32 * 4))
        r_small = region(9 * P * 4)
        dts = at("dts", [P, 9, 2, TILES, SH], r_small)
        wr = at("wr", [P, KD, N_EXP], r_xs)
        rtr = at("rtr", [P, 12, TILES, N_EXP], r_xs + KD * N_EXP * 4)
        stat = at("stat", [P, 8, 64], region(8 * 64 * 4))
        cT = at("cT", [P, 16], region(64))
        crw = at("crw", [16, P], region(512))
        cbm = at("cbm", [P, 2, P], region(2 * P * 4))
        print("SBUF used", top[0], "of", nc.sbuf_usable_end) if top[0] > nc.sbuf_usable_end else None

        ps = ctx.enter_context(nc.psum_tensor("ps", [P, 8, NCH], F32))

        ident = cst[:, C_ID:C_ID + P]
        UT, LT = cst[:, C_UT:C_UT + P], cst[:, C_LT:C_LT + P]
        tri = [UT, LT]
        cond = sem("cond_loaded")
        param = sem("params_loaded")
        phase = sem("phase_done")
        full = [sem(f"ring_full{i}") for i in range(RING)]
        efull = [sem(f"expert_full{i}") for i in range(EXP_SLOTS)]

        def qkv_units(l):
            return [(n, t) for n in range(3) for t in range(TILES) if n > 0 or t < out_tiles[l]]

        def attn_units(l):
            return [(t, ty, g, h) for t in range(out_tiles[l]) for ty in range(2) for g in range(KV) for h in range(GQ)]

        def scan_order(d):
            ctx_t, lat_t = [2, 3], [0, 1]
            return ctx_t + lat_t if d == 0 else ctx_t[::-1] + lat_t[::-1]

        def scan_steps(l):
            return [(s, d, scan_order(d)[s]) for s in range(4) for d in range(2)]

        def tr_units(l):
            return [(t, ty) for t in range(TILES) for ty in range(2)]

        def has_q(l, t):
            return t < out_tiles[l]

        def last_use(j):
            l, kind, n = jobs[j]
            if kind in ("ada0", "ada1"):
                return stage(f"mm_{kind}_{l}", n + 1)
            if kind == "xbc":
                return stage(f"mm_xbc_{l}", 4 * (n + 1))
            if kind == "qkv":
                u = qkv_units(l)
                return stage(f"mm_qkv_{l}", max(i for i, (m, _) in enumerate(u) if m == n) + 1)
            if kind == "z":
                return stage(f"mm_z_{l}", (n + 1) * out_tiles[l])
            if kind == "gate":
                return stage(f"mm_gate_{l}", (n + 1) * out_tiles[l])
            if kind == "br":
                return stage(f"mm_br_{l}", (n + 1) * out_tiles[l])
            return stage(f"mm_out_{l}", (n + 1) * out_tiles[l])

        def ring_source(j):
            l, kind, n = jobs[j]
            rows = lambda w, c: w[:, c:c + NCH].rearrange("(k p) n -> p k n", p=P)
            if kind in ("ada0", "ada1"):
                return rows(a["w_ada"][l], (3 * D if kind == "ada1" else 0) + n * NCH)
            if kind in ("xbc", "qkv", "z", "gate"):
                base = {"xbc": COL_XBC, "qkv": COL_QKV, "z": COL_Z, "gate": COL_GATE}[kind]
                return rows(a["w_in"][l], base + n * NCH)
            if kind == "br":
                return rows(a[("w_br_a", "w_br_w", "w_br_s")[n // 2]][l], (n % 2) * NCH)
            return rows(a["w_out"][l], n * NCH)

        def chunk(l, kind, n):
            j = job_at[(l, kind, n)]
            return ring[:, j % RING], (full[j % RING], 16 * (j // RING + 1))

        PH = ["ada0", "norm0", "inproj", "attn", "ssd", "gn", "merge", "out", "ada1", "norm1", "router", "moe", "post"]

        def phase_start(l, name):
            return 2 * (l * len(PH) + PH.index(name))

        class Steps:

            def __init__(self, eng, own):
                self.eng, self.own, self.n = eng, own, {}

            def mark(self, ins, s=None):
                s = s if s is not None else self.own
                self.n[s.name] = self.n.get(s.name, 0) + 1
                ins.then_inc(s, 1)

            def run(self, ins, s=None):
                s = s if s is not None else self.own
                self.mark(ins, s)
                self.eng.wait_ge(s, self.n[s.name])

        block = ctx.enter_context(nc.Block())

        @block.sync
        def _(sp):
            def load_ring(j):
                if j % per_layer == 0 and j:
                    l = j // per_layer
                    sp.wait_ge(phase, phase_start(l, "ada0"))
                if j >= RING:
                    sp.wait_ge(*last_use(j - RING))
                src = ring_source(j)
                sp.dma_start(ring[:, j % RING, 0:src.shape[1], :], src).then_inc(full[j % RING], 16)

            def load_expert(slot, wg, wu, wd):
                sp.dma_start(esl[:, slot, 0, :].rearrange("p (k n) -> p k n", n=D_EXP),
                             wg.rearrange("(k p) n -> p k n", p=P)).then_inc(efull[slot], 16)
                sp.dma_start(esl[:, slot, 1, :].rearrange("p (k n) -> p k n", n=D_EXP),
                             wu.rearrange("(k p) n -> p k n", p=P)).then_inc(efull[slot], 16)
                sp.dma_start(esl[:, slot, 2, :].rearrange("p (k n) -> p k n", n=D),
                             wd.rearrange("(k p) n -> p k n", p=P)).then_inc(efull[slot], 16)

            sp.dma_start(x[:, 0:LAT_TILES, :], a["x"][0].rearrange("(t p) d -> p t d", p=P)).then_inc(sem("x_loaded"), 16)
            sp.dma_start(x[:, LAT_TILES:, :], a["ctx"][0].rearrange("(t p) d -> p t d", p=P)).then_inc(sem("x_loaded"), 16)
            for l in range(DEPTH):
                for j in range(l * per_layer, (l + 1) * per_layer):
                    load_ring(j)
                nt = out_tiles[l]
                down = sem(f"mm_down_{l}")
                for j in range((l + 1) * per_layer - RING, (l + 1) * per_layer):
                    sp.wait_ge(*last_use(j))
                for s in range(EXP_SLOTS):
                    load_expert(s, a["we_gate"][l, s], a["we_up"][l, s], a["we_down"][l, s])
                with sp.Fori(0, N_EXP // EXP_SLOTS - 1) as r:
                    i = r * EXP_SLOTS
                    for s in range(EXP_SLOTS):
                        sp.wait_ge(down, (i + (s + 1)) * nt)
                        load_expert(s, a["we_gate"][l, bass.ds(i + (s + EXP_SLOTS), 1)].rearrange("o r n -> (o r) n"),
                                    a["we_up"][l, bass.ds(i + (s + EXP_SLOTS), 1)].rearrange("o r n -> (o r) n"),
                                    a["we_down"][l, bass.ds(i + (s + EXP_SLOTS), 1)].rearrange("o r n -> (o r) n"))
                sp.wait_ge(down, (N_EXP - EXP_SLOTS + 1) * nt)
                load_expert(0, a["ws_gate"][l], a["ws_up"][l], a["ws_down"][l])
            sp.wait_ge(phase, phase_start(DEPTH, "ada0"))
            sp.dma_start(out[0].rearrange("(t p) d -> p t d", p=P), x[:, 0:LAT_TILES, :]).then_inc(sem("out_written"), 16)
            sp.wait_ge(sem("out_written"), 16)

        @block.gpsimd
        def _(pool):
            def rows(dst, src):
                pool.dma_start(dst, src).then_inc(param, 16)

            pool.dma_start(cst[:, :], cst_d).then_inc(cond, 16)
            pool.dma_start(crw[0:8, :], a["c"].rearrange("o (k p) -> (o k) p", p=P)).then_inc(cond, 16)
            pool.dma_start(crw[8:16, :], a["c_ctx"].rearrange("(k p) -> k p", p=P)).then_inc(cond, 16)
            for l in range(DEPTH):
                if l:
                    pool.wait_ge(phase, phase_start(l, "ada0"))
                for half in range(2):
                    if half:
                        pool.wait_ge(phase, phase_start(l, "ada1"))
                    rows(bada[:, :], a["b_ada"][l, half * 3 * D:(half + 1) * 3 * D].partition_broadcast(2))
                    rows(gnorm[:, 0, :], a[("g_mix_pre", "g_ffn_pre")[half]][l].partition_broadcast(2))
                    rows(gnorm[:, 1, :], a[("g_mix_post", "g_ffn_post")[half]][l].partition_broadcast(2))
                    if half == 0:
                        rows(dtb[:, :], a["ssm_dt_bias"][l].rearrange("d h -> (d h)").partition_broadcast(P))
                        rows(alog[:, :], a["ssm_a_log"][l].rearrange("d h -> (d h)").partition_broadcast(P))
                        rows(dsk[:, :], a["ssm_d"][l].partition_broadcast(P))
                        rows(nw[:, :], a["ssm_norm"][l].partition_broadcast(P))
                        rows(nsink[:, :], a["sink_w"][l].partition_broadcast(P))
                        rows(brt[:, :], a["b_router"][l].partition_broadcast(P))
                        rows(crow[0:36, :], a["ssm_conv_w"][l].rearrange("w (c p) -> (w c) p", p=P))
                        rows(crow[36:48, :], a["ssm_conv_b"][l].rearrange("(c p) -> c p", p=P))
                        rows(wdt[:, :, :], a["w_in"][l][:, COL_DT:COL_DT + 32].rearrange("(k p) n -> p k n", p=P))
                        pool.wait_ge(phase, phase_start(l, "inproj"))
                        for h in range(HEADS + KV):
                            pool.dma_start(gqk[:, h * HD:(h + 1) * HD],
                                           a["g_q_a" if h < HEADS else "g_k_a"][l].partition_broadcast(P)).then_inc(sem("gqk_loaded"), 16)
                    else:
                        rows(wr[:, :, :], a["w_router"][l].rearrange("(k p) n -> p k n", p=P))

        HALF_LOADS = [3 + 6 + 3, 3 + 1]

        def params_at(l, half):
            return 16 * (l * sum(HALF_LOADS) + HALF_LOADS[0] + (HALF_LOADS[1] if half else 0))

        @block.tensor
        def _(pe):
            def mms(o, pairs, start=True, stop=True):
                for i, (lt, rh) in enumerate(pairs):
                    last = nc.tensor.matmul(o, lt, rh, start=start and i == 0, stop=stop and i == len(pairs) - 1)
                return last

            def transposes(bank, ins):
                for i, blk in enumerate(ins):
                    last = nc.tensor.transpose(ps[:, bank, i * P:(i + 1) * P], blk, ident)
                return last

            pe.wait_ge(cond, 16 * 3)
            nc.tensor.transpose(ps[:, 0, 0:16], crw[:, :], cst[0:16, C_ID:C_ID + 16]).then_inc(sem("mm_cond"), 1)
            pe.wait_ge(sem("cond_silu"), 2)
            for l in range(DEPTH):
                nt = out_tiles[l]

                def ada(half):
                    kind = f"ada{half}"
                    pe.wait_ge(phase, phase_start(l, kind)) if phase_start(l, kind) else None
                    if half == 0:
                        pe.wait_ge(param, params_at(l, 0))
                        nc.tensor.transpose(ps[:, 6, 0:48], crow[:, :], cst[0:48, C_ID:C_ID + 48]).then_inc(sem(f"mm_ccol_{l}"), 1)
                    for n in range(6):
                        w, ready = chunk(l, kind, n)
                        pe.wait_ge(*ready)
                        if n >= 2:
                            pe.wait_ge(*stage(f"ev_{kind}_{l}", n - 1))
                        mms(ps[0:2, n % 2, :], [(cT[:, k::8], w[:, k, :]) for k in range(KD)]).then_inc(sem(f"mm_{kind}_{l}"), 1)
                    pe.wait_ge(*stage(f"modrow_{kind}_{l}", 2))
                    for i in range(12):
                        v, s, n2 = i // 4, i // 2 % 2, i % 2
                        if i >= 4:
                            pe.wait_ge(*stage(f"bc_{kind}_{l}", i - 3))
                        mms(ps[:, 2 + i % 4, :], [(cst[0:2, C_SEL + s * P:C_SEL + (s + 1) * P], modrow[:, v, n2 * NCH:(n2 + 1) * NCH])])\
                            .then_inc(sem(f"mm_bc_{kind}_{l}"), 1)

                def norm(half, tiles):
                    kind = f"norm{half}"
                    pe.wait_ge(phase, phase_start(l, kind))
                    for t in range(tiles):
                        pe.wait_ge(*stage(f"hn_{kind}_{l}", t + 1))
                        for b in range(2):
                            u = 2 * t + b
                            if u >= 4:
                                pe.wait_ge(*stage(f"ev_{kind}_{l}", u - 3))
                            transposes(u % 4, [hn[:, t % 2, (4 * b + i) * P:(4 * b + i + 1) * P] for i in range(4)])\
                                .then_inc(sem(f"mm_{kind}_{l}"), 1)

                ada(0)
                norm(0, TILES)

                pe.wait_ge(phase, phase_start(l, "inproj"))

                def conv_transposes(ct):
                    pe.wait_ge(*stage(f"conv_u_{l}", ct + 1))
                    if ct >= 2:
                        pe.wait_ge(*stage(f"ev_uT_{l}", ct - 1))
                    src = cu[:, ct % 2, :] if ct < 8 else bcc[:, ct - 8, :]
                    transposes(2 + ct % 2, [src[:, t * P:(t + 1) * P] for t in range(TILES)]).then_inc(sem(f"mm_uT_{l}"), 1)

                for ct in range(CONV_T):
                    w, ready = chunk(l, "xbc", ct // 4)
                    pe.wait_ge(*ready)
                    if ct >= 2:
                        pe.wait_ge(*stage(f"conv_in_{l}", ct - 1))
                    mms(ps[:, ct % 2, :], [(w[:, k, (ct % 4) * P:(ct % 4 + 1) * P], hT[:, k, :]) for k in range(KD)])\
                        .then_inc(sem(f"mm_xbc_{l}"), 1)
                    if ct >= 2:
                        conv_transposes(ct - 2)
                for t in range(TILES):
                    last = mms(ps[:, 4, t * 32:(t + 1) * 32], [(hT[:, k, t * P:(t + 1) * P], wdt[:, k, :]) for k in range(KD)])
                last.then_inc(sem(f"mm_dt_{l}"), 1)
                u = 0
                for kind, units in (("qkv", qkv_units(l)), ("z", [(n, t) for n in range(2) for t in range(nt)])):
                    for n, t in units:
                        w, ready = chunk(l, kind, n)
                        pe.wait_ge(*ready)
                        if u >= 3:
                            pe.wait_ge(*stage(f"ev_proj_{l}", u - 2))
                        mms(ps[:, 5 + u % 3, :], [(hT[:, k, t * P:(t + 1) * P], w[:, k, :]) for k in range(KD)])\
                            .then_inc(sem(f"mm_{kind}_{l}"), 1)
                        u += 1

                pe.wait_ge(phase, phase_start(l, "attn"))
                e = 0
                for i, (t, ty) in enumerate(tr_units(l)):
                    pe.wait_ge(*stage(f"roped_{l}", i + 1))
                    for part in range(2):
                        if part == 0 and not has_q(l, t):
                            continue
                        if e >= 4:
                            pe.wait_ge(*stage(f"ev_qT_{l}", e - 3))
                        ins = [rq[:, i % 2, h * P:(h + 1) * P] for h in range(GQ)] if part == 0 else [rq[:, i % 2, 512:640]]
                        transposes(e % 4, ins).then_inc(sem(f"mm_qT_{l}"), 1)
                        e += 1
                pe.wait_ge(*stage(f"ev_qT_{l}", e))
                units = attn_units(l)

                def keys(t):
                    return (0, TILES) if t < LAT_TILES else (LAT_TILES, TILES)

                for i in range(len(units) + 2):
                    if i < len(units):
                        t, ty, g, h = units[i]
                        k0, k1 = keys(t)
                        if i >= 3:
                            pe.wait_ge(*stage(f"prob_{l}", i - 2))
                        o = ps[:, i % 3, 0:(k1 - k0) * P]
                        part = slice(g * HD, (g + 1) * HD)
                        masked = ty == 1 and t < LAT_TILES
                        m = nc.tensor.matmul(o, qT[part, ty, h, t * P:(t + 1) * P], kT[part, ty, k0 * P:k1 * P], start=True, stop=not masked)
                        if masked:
                            neg = cst[:, C_NA:C_NA + P] if t == 0 else cst[:, C_NB:C_NB + P]
                            m = nc.tensor.matmul(ps[:, i % 3, (1 - t) * P:(2 - t) * P], ident, neg, start=False, stop=True)
                        m.then_inc(sem(f"mm_score_{l}"), 1)
                    if 1 <= i <= len(units):
                        j = i - 1
                        t = units[j][0]
                        k0, k1 = keys(t)
                        pe.wait_ge(*stage(f"prob_{l}", j + 1))
                        if j >= 2:
                            pe.wait_ge(*stage(f"ev_pT_{l}", j - 1))
                        transposes(3 + j % 2, [pr[:, j % 2, c * P:(c + 1) * P] for c in range(k1 - k0)]).then_inc(sem(f"mm_pT_{l}"), 1)
                    if i >= 2:
                        j = i - 2
                        t, ty, g, h = units[j]
                        k0, k1 = keys(t)
                        pe.wait_ge(*stage(f"ev_pT_{l}", j + 1))
                        grp, hh = j // HEADS, j % HEADS
                        if hh == 0 and grp >= 2:
                            pe.wait_ge(*stage(f"ev_o_{l}", grp - 1))
                        v0 = ty * 768 + 640 + g * HD
                        mms(ps[:, 5 + grp % 2, hh * HD:(hh + 1) * HD],
                            [(pT[:, j % 2, c * P:(c + 1) * P], qk[:, k0 + c, v0:v0 + HD]) for c in range(k1 - k0)])\
                            .then_inc(sem(f"mm_pv_{l}"), 1)
                for t in range(nt):
                    pe.wait_ge(*stage(f"ev_o_{l}", 2 * (t + 1)))
                    for ty in range(2):
                        u = 2 * t + ty
                        if u >= 2:
                            pe.wait_ge(*stage(f"ev_oT_{l}", u - 1))
                        if u == 0:
                            pe.wait_ge(*stage(f"ev_pT_{l}", len(units)))
                        transposes(3 + u % 2, [qk[:, t, ty * 768 + c * P:ty * 768 + (c + 1) * P] for c in range(4)])\
                            .then_inc(sem(f"mm_oT_{l}"), 1)

                pe.wait_ge(phase, phase_start(l, "ssd"))
                pe.wait_ge(*stage(f"a_ready_{l}", 1))
                for d in range(2):
                    mms(ps[:, 7, d * 64:(d + 1) * 64], [(tri[d], dts[:, 1, d])])
                mms(ps[:, 7, 128:256], [(cst[:, C_ONE:C_ONE + P], dts[:, 1])]).then_inc(sem(f"mm_cum_{l}"), 1)
                ny = ns = 0
                for s, d, t in scan_steps(l):
                    if s > 0 and t < nt:
                        pe.wait_ge(*stage(f"state_{l}", 2 * (s - 1) + d + 1))
                        if ny >= 2:
                            pe.wait_ge(*stage(f"ev_yoff_{l}", ny - 1))
                        for g in range(SG):
                            m = mms(ps[:, 2 * (ny % 2) + g, :], [(bcc[:, 2 + g, t * P:(t + 1) * P], st[:, d, g * NCH:(g + 1) * NCH])])
                        m.then_inc(sem(f"mm_yoff_{l}"), 1)
                        ny += 1
                    if s < 3:
                        pe.wait_ge(*stage(f"xw_{l}", ns + 1))
                        for g in range(SG):
                            m = mms(ps[:, 4 + g, :], [(btok[:, t, g * SN:(g + 1) * SN], tmp[:, g * NCH:(g + 1) * NCH])])
                        m.then_inc(sem(f"mm_state_{l}"), 1)
                        ns += 1
                pe.wait_ge(*stage(f"scan_done_{l}", 1))
                q = 0
                for u in range(nt * SG + 1):
                    for d in range(2):
                        if u < nt * SG:
                            t, g = u // SG, u % SG
                            if d == 0:
                                if u >= 1:
                                    pe.wait_ge(*stage(f"cbm_{l}", 2 * u))
                                mms(ps[:, 0, 0:P], [(bcc[:, g, t * P:(t + 1) * P], bcc[:, 2 + g, t * P:(t + 1) * P])]).then_inc(sem(f"mm_cb_{l}"), 1)
                            if q >= 2:
                                pe.wait_ge(*stage(f"diff_{l}", q - 1))
                            for h in range(8):
                                last = mms(ps[:, 1 + 2 * (q % 2) + h // 4, (h % 4) * P:(h % 4 + 1) * P],
                                           [(dts[:, 1, d, t, g * 8 + h:g * 8 + h + 1].to_broadcast([P, P]), tri[d])])
                            last.then_inc(sem(f"mm_r_{l}"), 1)
                            q += 1
                    if u >= 1:
                        pu = u - 1
                        t, g = pu // SG, pu % SG
                        pe.wait_ge(*stage(f"m_ready_{l}", 2 * u))
                        if pu >= 2:
                            pe.wait_ge(*stage(f"ev_y_{l}", pu - 1))
                        for h in range(8):
                            for d in range(2):
                                hh = g * 8 + h
                                last = nc.tensor.matmul(ps[:, 5 + pu % 2, h * HD:(h + 1) * HD], mt[:, (2 * pu + d) % 3, h, :],
                                                        xs[:, t, hh * HD:(hh + 1) * HD], start=d == 0, stop=d == 1)
                        last.then_inc(sem(f"mm_y_{l}"), 1)

                def row_transposes(name, tiles, src):
                    for t in range(tiles):
                        pe.wait_ge(*stage(f"{name}_rows_{l}", t + 1))
                        for b in range(2):
                            u = 2 * t + b
                            if u >= 4:
                                pe.wait_ge(*stage(f"ev_{name}_{l}", u - 3))
                            transposes(4 + u % 4, [src[:, t, (4 * b + i) * P:(4 * b + i + 1) * P] for i in range(4)])\
                                .then_inc(sem(f"mm_{name}_{l}"), 1)

                pe.wait_ge(phase, phase_start(l, "gn"))
                row_transposes("gn", nt, y)

                pe.wait_ge(phase, phase_start(l, "merge"))
                u = 0
                for bn in range(6):
                    b, n = bn // 2, bn % 2
                    wg, g_ready = chunk(l, "gate", bn)
                    wb, b_ready = chunk(l, "br", bn)
                    pe.wait_ge(*g_ready)
                    pe.wait_ge(*b_ready)
                    src = [(oT, 0, 4), (oT, 4, 4), (ysT, 0, 8)][b]
                    for t in range(nt):
                        if u >= 2:
                            pe.wait_ge(*stage(f"gated_{l}", u - 1))
                        mms(ps[:, u % 2, :], [(hT[:, k, t * P:(t + 1) * P], wg[:, k, :]) for k in range(KD)]).then_inc(sem(f"mm_gate_{l}"), 1)
                        mms(ps[:, 2 + u % 2, :], [(src[0][:, src[1] + k, t * P:(t + 1) * P], wb[:, k, :]) for k in range(src[2])])\
                            .then_inc(sem(f"mm_br_{l}"), 1)
                        u += 1
                row_transposes("mg", nt, acc)

                pe.wait_ge(phase, phase_start(l, "out"))
                for u, (n, t) in enumerate([(n, t) for n in range(2) for t in range(nt)]):
                    w, ready = chunk(l, "out", n)
                    pe.wait_ge(*ready)
                    if u >= 2:
                        pe.wait_ge(*stage(f"ev_out_{l}", u - 1))
                    mms(ps[:, u % 2, :], [(mT[:, k, t * P:(t + 1) * P], w[:, k, :]) for k in range(KD)]).then_inc(sem(f"mm_out_{l}"), 1)

                ada(1)
                norm(1, nt)

                pe.wait_ge(phase, phase_start(l, "router"))
                pe.wait_ge(param, params_at(l, 1))
                for t in range(nt):
                    last = mms(ps[:, 0, t * N_EXP:(t + 1) * N_EXP], [(hT[:, k, t * P:(t + 1) * P], wr[:, k, :]) for k in range(KD)])
                last.then_inc(sem(f"mm_router_{l}"), 1)

                pe.wait_ge(phase, phase_start(l, "moe"))
                gu, hid_t, down = sem(f"mm_gu_{l}"), sem(f"mm_hT_{l}"), sem(f"mm_down_{l}")
                act_h, ev_h, ev_d = sem(f"hidden_{l}"), sem(f"ev_hT_{l}"), sem(f"ev_down_{l}")

                def unit(slot, t, u, first):
                    b = t % 2
                    wgu = esl[:, slot, 0:2, :].rearrange("p a (k n) -> p k a n", n=D_EXP)
                    if not first or t >= 2:
                        pe.wait_ge(act_h, u - 1)
                    mms(ps[:, b, :].rearrange("p (a n) -> p a n", a=2), [(hT[:, k, t * P:(t + 1) * P], wgu[:, k]) for k in range(KD)]).then_inc(gu, 1)
                    pe.wait_ge(act_h, u + 1)
                    if not first or t >= 2:
                        pe.wait_ge(ev_h, u - 1)
                    transposes(2 + b, [hsg[:, b, c * P:(c + 1) * P] for c in range(2)]).then_inc(hid_t, 1)
                    pe.wait_ge(ev_h, u + 1)
                    if not first or t >= 2:
                        pe.wait_ge(ev_d, u - 1)
                    for n in range(2):
                        m = mms(ps[:, 4 + 2 * b + n, :], [(hgT[:, b, c, :], esl[:, slot, 2, c * D + n * NCH:c * D + (n + 1) * NCH]) for c in range(2)])
                    m.then_inc(down, 1)

                for e in range(EXP_SLOTS):
                    pe.wait_ge(efull[e], EXP_BASE[l][e] + 48)
                    for t in range(nt):
                        unit(e, t, e * nt + t, e == 0)
                with pe.Fori(EXP_SLOTS, N_EXP, EXP_SLOTS) as i:
                    for e in range(EXP_SLOTS):
                        pe.wait_ge(efull[e], (i // EXP_SLOTS) * 48 + (EXP_BASE[l][e] + 48))
                        for t in range(nt):
                            unit(e, t, i * nt + (e * nt + t), False)
                pe.wait_ge(efull[0], EXP_BASE[l][0] + 48 * (N_EXP // EXP_SLOTS + 1))
                for t in range(nt):
                    unit(0, t, N_EXP * nt + t, False)

        @block.scalar
        def _(act):
            do = Steps(act, sem("act_order"))
            nc_a = nc.scalar
            act.wait_ge(sem("mm_cond"), 1)
            act.wait_ge(sem("x_loaded"), 32)
            do.run(nc_a.activation(cT[:, :], ps[:, 0, 0:16], ACT.Silu))
            nc_a.activation(cT[:, :], cT[:, :], ACT.Copy).then_inc(sem("cond_silu"), 1)
            act.sem_inc(sem("cond_silu"), 1)
            for l in range(DEPTH):
                nt = out_tiles[l]

                def end():
                    act.wait_ge(do.own, do.n.get(do.own.name, 0))
                    act.sem_inc(phase, 1)

                def ada(half):
                    kind = f"ada{half}"
                    act.wait_ge(phase, phase_start(l, kind)) if phase_start(l, kind) else None
                    if half == 0:
                        act.wait_ge(*stage(f"mm_ccol_{l}", 1))
                        do.run(nc_a.activation(ccol[:, :], ps[:, 6, 0:48], ACT.Copy))
                    for i in range(12):
                        v, s, n2 = i // 4, i // 2 % 2, i % 2
                        act.wait_ge(*stage(f"mm_bc_{kind}_{l}", i + 1))
                        do.run(nc_a.activation(bc[:, v, s, n2 * NCH:(n2 + 1) * NCH], ps[:, 2 + i % 4, :], ACT.Copy), sem(f"bc_{kind}_{l}"))
                    act.sem_inc(phase, 1)

                def rstd(src, n, waits, ready):
                    act.wait_ge(*waits)
                    do.run(nc_a.activation(stat[:, 2, 0:n], stat[:, 1, 0:n], ACT.Sqrt), ready)

                def norm(half, tiles):
                    kind = f"norm{half}"
                    act.wait_ge(phase, phase_start(l, kind))
                    for t in range(tiles):
                        do.run(nc_a.activation(junk[:, :], x[:, t, :], ACT.Square, accum_out=stat[:, 0, t:t + 1]), sem(f"sq_{kind}_{l}"))
                    rstd(None, tiles, stage(f"inv_{kind}_{l}", 1), sem(f"rstd_{kind}_{l}"))
                    for u in range(2 * tiles):
                        t, b = u // 2, u % 2
                        act.wait_ge(*stage(f"mm_{kind}_{l}", u + 1))
                        do.run(nc_a.activation(hT[:, 4 * b:4 * b + 4, t * P:(t + 1) * P],
                                               ps[:, u % 4, :].rearrange("p (k n) -> p k n", n=P), ACT.Copy), sem(f"ev_{kind}_{l}"))
                    act.sem_inc(phase, 1)

                ada(0)
                norm(0, TILES)

                act.wait_ge(phase, phase_start(l, "inproj"))
                act.wait_ge(*stage(f"xp_zero_{l}", 2))
                for ct in range(CONV_T + 1):
                    if ct < CONV_T:
                        act.wait_ge(*stage(f"mm_xbc_{l}", ct + 1))
                        if ct >= 2:
                            act.wait_ge(*stage(f"conv_{l}", ct - 1))
                        do.run(nc_a.activation(xp[ct % 2][:, :, 1:SEG + 1], ps[:, ct % 2, :].rearrange("p (s n) -> p s n", s=2), ACT.Copy),
                               sem(f"conv_in_{l}"))
                    if ct >= 1:
                        c = ct - 1
                        act.wait_ge(*stage(f"conv_{l}", c + 1))
                        if c >= 2 and c < 8:
                            act.wait_ge(*stage(f"mm_uT_{l}", c - 1))
                        dst = cu[:, c % 2, :] if c < 8 else bcc[:, c - 8, :]
                        do.run(nc_a.activation(dst, cacc[:, c % 2, :], ACT.Silu), sem(f"conv_u_{l}"))
                u = 0
                for kind, units in (("qkv", qkv_units(l)), ("z", [(n, t) for n in range(2) for t in range(nt)])):
                    for i, (n, t) in enumerate(units):
                        act.wait_ge(*stage(f"mm_{kind}_{l}", i + 1))
                        dst = (qk if kind == "qkv" else zs)[:, t, n * NCH:(n + 1) * NCH]
                        do.run(nc_a.activation(dst, ps[:, 5 + u % 3, :], ACT.Copy if kind == "qkv" else ACT.Silu), sem(f"ev_proj_{l}"))
                        u += 1
                act.sem_inc(phase, 1)

                act.wait_ge(phase, phase_start(l, "attn"))
                rstd(None, TILES * 10, stage(f"inv_qk_{l}", 1), sem(f"rstd_qk_{l}"))
                e = 0
                for t, ty in tr_units(l):
                    for part in range(2):
                        if part == 0 and not has_q(l, t):
                            continue
                        act.wait_ge(*stage(f"mm_qT_{l}", e + 1))
                        if part == 0:
                            ins = nc_a.activation(qT[:, ty, :, t * P:(t + 1) * P], ps[:, e % 4, :].rearrange("p (h n) -> p h n", n=P), ACT.Copy)
                        else:
                            ins = nc_a.activation(kT[:, ty, t * P:(t + 1) * P], ps[:, e % 4, 0:P], ACT.Copy)
                        do.run(ins, sem(f"ev_qT_{l}"))
                        e += 1
                units = attn_units(l)
                for i in range(len(units) + 1):
                    if i < len(units):
                        t = units[i][0]
                        n = (TILES if t < LAT_TILES else CTX_TILES) * P
                        act.wait_ge(*stage(f"negmax_{l}", i + 1))
                        if i >= 2:
                            act.wait_ge(*stage(f"mm_pT_{l}", i - 1))
                        col = i % 16
                        if i >= 16 and i % 8 == 0:
                            act.wait_ge(*stage(f"ev_o_{l}", i // 8 - 1))
                        do.run(nc_a.activation(pr[:, i % 2, 0:n], ps[:, i % 3, 0:n], ACT.Exp, bias=stat[:, 3, col:col + 1], scale=SCALE,
                                               accum_out=stat[:, 4, col:col + 1]), sem(f"prob_{l}"))
                        if i % 8 == 7 and units[i][1] == 1:
                            g8 = slice(col - 7, col + 1)
                            act.wait_ge(*stage(f"sinkarg_{l}", i // 16 + 1))
                            do.run(nc_a.activation(stat[:, 5, g8], stat[:, 5, g8], ACT.Exp), sem(f"sinkexp_{l}"))
                    if i >= 1:
                        j = i - 1
                        t = units[j][0]
                        n = (TILES if t < LAT_TILES else CTX_TILES) * P
                        act.wait_ge(*stage(f"mm_pT_{l}", j + 1))
                        if j >= 2:
                            act.wait_ge(*stage(f"mm_pv_{l}", j - 1))
                        do.run(nc_a.activation(pT[:, j % 2, 0:n], ps[:, 3 + j % 2, 0:n], ACT.Copy), sem(f"ev_pT_{l}"))
                for u in range(2 * nt):
                    t, ty = u // 2, u % 2
                    act.wait_ge(*stage(f"mm_oT_{l}", u + 1))
                    do.run(nc_a.activation(oT[:, 4 * ty:4 * ty + 4, t * P:(t + 1) * P], ps[:, 3 + u % 2, :].rearrange("p (k n) -> p k n", n=P), ACT.Copy),
                           sem(f"ev_oT_{l}"))
                act.sem_inc(phase, 1)

                act.wait_ge(phase, phase_start(l, "ssd"))
                do.run(nc_a.activation(alog[:, :], alog[:, :], ACT.Exp), sem(f"expA_{l}"))
                act.wait_ge(*stage(f"nabs_{l}", 1))
                do.run(nc_a.activation(dts[:, 7], dts[:, 7], ACT.Exp), sem(f"softexp_{l}"))
                act.wait_ge(*stage(f"onep_{l}", 1))
                do.run(nc_a.activation(dts[:, 3], dts[:, 8], ACT.Ln), sem(f"softln_{l}"))
                act.wait_ge(*stage(f"cum_{l}", 1))
                do.mark(nc_a.activation(dts[:, 4], dts[:, 2], ACT.Exp))
                do.mark(nc_a.activation(dts[:, 5], dts[:, 5], ACT.Exp))
                do.mark(nc_a.activation(dts[:, 6], dts[:, 3], ACT.Exp), sem(f"decays_{l}"))
                for q in range(2 * SG * nt):
                    act.wait_ge(*stage(f"diff_{l}", q + 1))
                    m3 = mt[:, q % 3]
                    do.run(nc_a.activation(m3, m3, ACT.Exp), sem(f"expd_{l}"))
                act.sem_inc(phase, 1)

                act.wait_ge(phase, phase_start(l, "gn"))
                for t in range(nt):
                    act.wait_ge(*stage(f"yz_{l}", t + 1))
                    for g in range(SG):
                        do.run(nc_a.activation(junk[:, 0:NCH], y[:, t, g * NCH:(g + 1) * NCH], ACT.Square,
                                               accum_out=stat[:, 0, 2 * t + g:2 * t + g + 1]), sem(f"sq_gn_{l}"))
                rstd(None, 2 * nt, stage(f"inv_gn_{l}", 1), sem(f"rstd_gn_{l}"))

                def evac_rows(name, dst):
                    for u in range(2 * nt):
                        t, b = u // 2, u % 2
                        act.wait_ge(*stage(f"mm_{name}_{l}", u + 1))
                        do.run(nc_a.activation(dst[:, 4 * b:4 * b + 4, t * P:(t + 1) * P],
                                               ps[:, 4 + u % 4, :].rearrange("p (k n) -> p k n", n=P), ACT.Copy), sem(f"ev_{name}_{l}"))

                evac_rows("gn", ysT)
                act.sem_inc(phase, 1)

                act.wait_ge(phase, phase_start(l, "merge"))
                for u in range(6 * nt):
                    act.wait_ge(*stage(f"mm_gate_{l}", u + 1))
                    if u >= 2:
                        act.wait_ge(*stage(f"gated_{l}", u - 1))
                    do.run(nc_a.activation(gs[:, u % 2, :], ps[:, u % 2, :], ACT.Sigmoid), sem(f"gate_{l}"))
                evac_rows("mg", mT)
                act.sem_inc(phase, 1)

                act.wait_ge(phase, phase_start(l, "out"))
                for u, (n, t) in enumerate([(n, t) for n in range(2) for t in range(nt)]):
                    act.wait_ge(*stage(f"mm_out_{l}", u + 1))
                    do.run(nc_a.activation(ml[:, t, n * NCH:(n + 1) * NCH], ps[:, u % 2, :], ACT.Copy), sem(f"ev_out_{l}"))

                def post(name, src):
                    for t in range(nt):
                        do.run(nc_a.activation(junk[:, :], src[:, t, :], ACT.Square, accum_out=stat[:, 0, t:t + 1]), sem(f"sq_{name}_{l}"))
                    rstd(None, nt, stage(f"inv_{name}_{l}", 1), sem(f"rstd_{name}_{l}"))
                    act.sem_inc(phase, 1)

                post("out", ml)
                ada(1)
                norm(1, nt)

                act.wait_ge(phase, phase_start(l, "router"))
                act.wait_ge(*stage(f"mm_router_{l}", 1))
                do.run(nc_a.activation(rtr[:, 0, 0:nt, :], ps[:, 0, 0:nt * N_EXP].rearrange("p (t n) -> p t n", n=N_EXP), ACT.Sigmoid), sem(f"scores_{l}"))
                act.sem_inc(phase, 1)

                act.wait_ge(phase, phase_start(l, "moe"))
                gu, hid_t, down = sem(f"mm_gu_{l}"), sem(f"mm_hT_{l}"), sem(f"mm_down_{l}")
                act_h, ev_h, silu = sem(f"hidden_{l}"), sem(f"ev_hT_{l}"), sem(f"silu_{l}")

                def unit(t, u, first):
                    b = t % 2
                    act.wait_ge(gu, u + 1)
                    if not first or t >= 2:
                        act.wait_ge(hid_t, u - 1)
                    nc_a.activation(hsg[:, b, :], ps[:, b, 0:D_EXP], ACT.Silu).then_inc(silu, 1)
                    act.wait_ge(hid_t, u + 1)
                    if not first or t >= 2:
                        act.wait_ge(down, u - 1)
                    nc_a.activation(hgT[:, b, :, :], ps[:, 2 + b, 0:2 * P].rearrange("p (c n) -> p c n", n=P), ACT.Copy).then_inc(ev_h, 1)

                for t in range(nt):
                    unit(t, t, True)
                with act.Fori(nt, (N_EXP + 1) * nt, nt) as i:
                    for t in range(nt):
                        unit(t, i + t, False)
                act.wait_ge(ev_h, (N_EXP + 1) * nt)
                act.sem_inc(phase, 1)

                act.wait_ge(phase, phase_start(l, "post"))
                post("post", acc)

        @block.vector
        def _(dve):
            do = Steps(dve, sem("dve_order"))
            v = nc.vector
            dve.wait_ge(sem("x_loaded"), 32)
            for l in range(DEPTH):
                nt = out_tiles[l]

                def end():
                    dve.sem_inc(phase, 1)

                def ada(half):
                    kind = f"ada{half}"
                    dve.wait_ge(phase, phase_start(l, kind)) if phase_start(l, kind) else None
                    dve.wait_ge(param, params_at(l, half))
                    if half == 0:
                        do.run(v.tensor_scalar(nsink[:, :], nsink[:, :], -1.0, None, ALU.mult))
                    for n in range(6):
                        dve.wait_ge(*stage(f"mm_{kind}_{l}", n + 1))
                        o = modrow[:, n // 2, (n % 2) * NCH:(n % 2 + 1) * NCH]
                        do.run(v.tensor_tensor(o, ps[0:2, n % 2, :], bada[:, n * NCH:(n + 1) * NCH], ALU.add), sem(f"ev_{kind}_{l}"))
                    do.run(v.scalar_tensor_tensor(modrow[:, 1, :], modrow[:, 1, :], 1.0, gnorm[:, 0, :], ALU.add, ALU.mult), sem(f"modrow_{kind}_{l}"))
                    do.run(v.tensor_tensor(modrow[:, 2, :], modrow[:, 2, :], gnorm[:, 1, :], ALU.mult), sem(f"modrow_{kind}_{l}"))
                    end()

                def inverse_ms(n, width, ready):
                    do.run(v.tensor_scalar(stat[:, 0, 0:n], stat[:, 0, 0:n], 1.0 / width, EPS, ALU.mult, ALU.add))
                    do.run(v.reciprocal(stat[:, 1, 0:n], stat[:, 0, 0:n]), ready)

                def norm(half, tiles):
                    kind = f"norm{half}"
                    dve.wait_ge(phase, phase_start(l, kind))
                    dve.wait_ge(*stage(f"sq_{kind}_{l}", tiles))
                    inverse_ms(tiles, D, sem(f"inv_{kind}_{l}"))
                    dve.wait_ge(*stage(f"rstd_{kind}_{l}", 1))
                    for t in range(tiles):
                        s = 0 if t < LAT_TILES else 1
                        if t >= 2:
                            dve.wait_ge(*stage(f"mm_{kind}_{l}", 2 * (t - 1)))
                        do.run(v.scalar_tensor_tensor(hn[:, t % 2, :], x[:, t, :], stat[:, 2, t:t + 1], bc[:, 1, s, :], ALU.mult, ALU.mult))
                        do.run(v.tensor_tensor(hn[:, t % 2, :], hn[:, t % 2, :], bc[:, 0, s, :], ALU.add), sem(f"hn_{kind}_{l}"))
                    end()

                ada(0)
                norm(0, TILES)

                dve.wait_ge(phase, phase_start(l, "inproj"))
                for i in range(2):
                    do.run(v.memset(xp[i][:, :, :], 0.0), sem(f"xp_zero_{l}"))

                def evac_uT(ct):
                    dve.wait_ge(*stage(f"mm_uT_{l}", ct + 1))
                    dst = xs[:, :, ct * P:(ct + 1) * P] if ct < 8 else btok[:, :, (ct - 8) * P:(ct - 7) * P]
                    do.run(v.tensor_copy(dst, ps[:, 2 + ct % 2, :].rearrange("p (t n) -> p t n", n=P)), sem(f"ev_uT_{l}"))

                for ct in range(CONV_T):
                    dve.wait_ge(*stage(f"conv_in_{l}", ct + 1))
                    if ct >= 2:
                        dve.wait_ge(*stage(f"conv_u_{l}", ct - 1))
                    src = xp[ct % 2]
                    o = cacc[:, ct % 2, :].rearrange("p (s n) -> p s n", s=2)
                    wcol = lambda w: ccol[:, w * CONV_T + ct:w * CONV_T + ct + 1]
                    do.run(v.tensor_scalar(o, src[:, :, 1:SEG + 1], wcol(1), wcol(3), ALU.mult, ALU.add))
                    do.run(v.scalar_tensor_tensor(o, src[:, :, 0:SEG], wcol(0), o, ALU.mult, ALU.add))
                    do.run(v.scalar_tensor_tensor(o, src[:, :, 2:SEG + 2], wcol(2), o, ALU.mult, ALU.add), sem(f"conv_{l}"))
                    if ct >= 2:
                        evac_uT(ct - 2)
                dve.wait_ge(*stage(f"mm_dt_{l}", 1))
                for d in range(2):
                    do.run(v.tensor_tensor(dts[:, 0, d], ps[:, 4, 0:TILES * 32].rearrange("p (t d h) -> p d t h", d=2, h=SH)[:, d],
                                           dtb[:, d * SH:(d + 1) * SH].unsqueeze(1).to_broadcast([P, TILES, SH]), ALU.add))
                end()

                dve.wait_ge(phase, phase_start(l, "attn"))
                for t in range(TILES):
                    h0 = 0 if has_q(l, t) else HEADS
                    w = (10 - h0) * HD
                    src = qk[:, t, h0 * HD:640]
                    do.run(v.tensor_tensor(rt[:, 0:w], src, src, ALU.mult))
                    do.run(v.tensor_reduce(stat[:, 0, t * 10 + h0:(t + 1) * 10], rt[:, 0:w].rearrange("p (h d) -> p h d", d=HD), AX.X, ALU.add))
                    if h0:
                        do.run(v.memset(stat[:, 0, t * 10:t * 10 + h0], 1.0))
                inverse_ms(TILES * 10, HD, sem(f"inv_qk_{l}"))
                dve.wait_ge(*stage(f"rstd_qk_{l}", 1))
                dve.wait_ge(sem("gqk_loaded"), 16 * (HEADS + KV) * (l + 1))
                for t, ty in tr_units(l):
                    h0 = 0 if has_q(l, t) else HEADS
                    nh = 10 - h0
                    cur = qk[:, t, ty * 768 + h0 * HD:ty * 768 + 640]
                    heads = cur.rearrange("p (h d) -> p h d", d=HD)
                    if ty == 0:
                        r = stat[:, 2, t * 10 + h0:(t + 1) * 10].unsqueeze(2).to_broadcast([P, nh, HD])
                        do.run(v.tensor_tensor(heads, heads, r, ALU.mult))
                        do.run(v.tensor_tensor(cur, cur, gqk[:, h0 * HD:640], ALU.mult))
                    if t < LAT_TILES:
                        cosb = cst[:, C_COS + t * HD:C_COS + (t + 1) * HD].unsqueeze(1).to_broadcast([P, nh, HD])
                        sv = cst[:, C_SIN + t * HD:C_SIN + (t + 1) * HD].rearrange("p (x f j) -> p x f j", x=2, f=2)
                        hv = cur.rearrange("p (h x f j) -> p h x f j", x=2, f=2, j=16)
                        mv = rt[:, :].rearrange("p (h x f j) -> p h x f j", x=2, f=2, j=16)
                        for f in range(2):
                            for ax in range(2):
                                do.mark(v.tensor_tensor(mv[:, :, ax, f, :], hv[:, :, ax, 1 - f, :],
                                                        sv[:, ax, f, :].unsqueeze(1).to_broadcast([P, nh, 16]), ALU.mult))
                        dve.wait_ge(do.own, do.n[do.own.name])
                        do.run(v.tensor_tensor(heads, heads, cosb, ALU.mult))
                    u = tr_units(l).index((t, ty))
                    if u >= 2:
                        dve.wait_ge(*stage(f"mm_qT_{l}", sum(1 + has_q(l, tt) for tt, _ in tr_units(l)[:u - 1])))
                    if has_q(l, t):
                        qd = rq[:, u % 2, 0:512].rearrange("p (h g d) -> p g h d", g=KV, d=HD)
                        q4 = lambda z: z.rearrange("p (g h d) -> p g h d", g=KV, d=HD)
                        qs = q4(cur[:, 0:512])
                        do.mark(v.tensor_tensor(qd, qs, q4(rt[:, 0:512]), ALU.add) if t < LAT_TILES else v.tensor_copy(qd, qs))
                    ks, kd = cur[:, nh * HD - P:nh * HD], rq[:, u % 2, 512:640]
                    do.run(v.tensor_tensor(kd, ks, rt[:, 512:640], ALU.add) if t < LAT_TILES else v.tensor_copy(kd, ks), sem(f"roped_{l}"))

                units = attn_units(l)

                def finish_group(grp):
                    t, ty = grp // 2, grp % 2
                    c0 = (grp % 2) * 8
                    dve.wait_ge(*stage(f"mm_pv_{l}", 8 * (grp + 1)))
                    den = stat[:, 4, c0:c0 + 8]
                    if ty == 1:
                        dve.wait_ge(*stage(f"sinkexp_{l}", t + 1))
                        do.run(v.tensor_tensor(den, den, stat[:, 5, c0:c0 + 8], ALU.add))
                    do.run(v.reciprocal(stat[:, 6, 0:8], den))
                    o = qk[:, t, ty * 768:ty * 768 + 512].rearrange("p (h d) -> p h d", d=HD)
                    do.run(v.tensor_tensor(o, ps[:, 5 + grp % 2, :].rearrange("p (h d) -> p h d", d=HD),
                                           stat[:, 6, 0:8].unsqueeze(2).to_broadcast([P, HEADS, HD]), ALU.mult), sem(f"ev_o_{l}"))

                for i, (t, ty, g, h) in enumerate(units):
                    n = (TILES if t < LAT_TILES else CTX_TILES) * P
                    col = i % 16
                    dve.wait_ge(*stage(f"mm_score_{l}", i + 1))
                    do.run(v.tensor_reduce(stat[:, 7, col:col + 1], ps[:, i % 3, 0:n], AX.X, ALU.max, negate=True))
                    if ty == 0:
                        ins = v.tensor_scalar(stat[:, 3, col:col + 1], stat[:, 7, col:col + 1], SCALE, None, ALU.mult)
                    else:
                        ins = v.tensor_scalar(stat[:, 3, col:col + 1], stat[:, 7, col:col + 1], SCALE, nsink[:, i % 8:i % 8 + 1], ALU.mult, ALU.min)
                    do.run(ins, sem(f"negmax_{l}"))
                    if i % 8 == 7 and ty == 1:
                        do.run(v.tensor_tensor(stat[:, 5, 8:16], stat[:, 3, 8:16], nsink[:, :], ALU.subtract), sem(f"sinkarg_{l}"))
                    if i >= 3 and (i - 3) % 8 == 7:
                        finish_group((i - 3) // 8)
                finish_group(len(units) // 8 - 1)
                end()

                dve.wait_ge(phase, phase_start(l, "ssd"))
                dt, aa, cum, tot, ein, eend, edec = (dts[:, i] for i in range(7))
                flat = lambda z: z.rearrange("p d t h -> p (d t h)")
                do.run(v.scalar_tensor_tensor(flat(dts[:, 7]), flat(dt), -1.0, flat(dt), ALU.mult, ALU.min), sem(f"nabs_{l}"))
                dve.wait_ge(*stage(f"softexp_{l}", 1))
                do.run(v.tensor_scalar(flat(dts[:, 8]), flat(dts[:, 7]), 1.0, None, ALU.add), sem(f"onep_{l}"))
                do.run(v.scalar_tensor_tensor(flat(dts[:, 4]), flat(dts[:, 8]), 1.0, flat(dts[:, 7]), ALU.subtract, ALU.subtract))
                do.run(v.reciprocal(flat(dts[:, 5]), flat(dts[:, 8])))
                do.run(v.scalar_tensor_tensor(flat(dts[:, 4]), flat(dts[:, 4]), -1.0, flat(dts[:, 5]), ALU.mult, ALU.mult))
                do.run(v.scalar_tensor_tensor(flat(dt), flat(dt), 0.0, flat(dts[:, 4]), ALU.max, ALU.add))
                dve.wait_ge(*stage(f"softln_{l}", 1))
                do.run(v.tensor_tensor(flat(dt), flat(dt), flat(tot), ALU.add))
                dve.wait_ge(*stage(f"expA_{l}", 1))
                for d in range(2):
                    do.run(v.tensor_tensor(aa[:, d], dt[:, d], alog[:, d * SH:(d + 1) * SH].unsqueeze(1).to_broadcast([P, TILES, SH]), ALU.mult))
                do.run(v.tensor_scalar(flat(aa), flat(aa), -1.0, None, ALU.mult), sem(f"a_ready_{l}"))
                dve.wait_ge(*stage(f"mm_cum_{l}", 1))
                do.run(v.tensor_copy(dts[:, 2:4].rearrange("p a d t h -> p (a d t h)"), ps[:, 7, 0:256]))
                do.run(v.tensor_tensor(flat(eend), flat(tot), flat(cum), ALU.subtract), sem(f"cum_{l}"))
                dve.wait_ge(*stage(f"decays_{l}", 1))
                do.run(v.tensor_tensor(flat(eend), flat(eend), flat(dt), ALU.mult))
                perhead = lambda z: z.rearrange("p (h d) -> p h d", d=HD)
                hb = lambda z: z.unsqueeze(2).to_broadcast([P, SH, HD])
                for t in range(nt):
                    do.run(v.tensor_tensor(perhead(y[:, t, :]), perhead(xs[:, t, :]), hb(dsk[:, :]), ALU.mult))
                ny = ns = 0
                for s, d, t in scan_steps(l):
                    if s > 0 and t < nt:
                        dve.wait_ge(*stage(f"mm_yoff_{l}", ny + 1))
                        bank = 2 * (ny % 2)
                        yo = mt[:, 0].rearrange("p a n -> p (a n)")
                        do.run(v.tensor_tensor(perhead(yo), ps[:, bank:bank + 2, :].rearrange("p a (h d) -> p (a h) d", d=HD), hb(ein[:, d, t, :]), ALU.mult),
                               sem(f"ev_yoff_{l}"))
                        do.run(v.tensor_tensor(y[:, t, :], y[:, t, :], yo, ALU.add))
                        ny += 1
                    if s < 3:
                        if ns:
                            dve.wait_ge(*stage(f"mm_state_{l}", ns))
                        do.run(v.tensor_tensor(perhead(tmp[:, :]), perhead(xs[:, t, :]), hb(eend[:, d, t, :]), ALU.mult), sem(f"xw_{l}"))
                        dve.wait_ge(*stage(f"mm_state_{l}", ns + 1))
                        add = ps[:, 4:6, :].rearrange("p a n -> p (a n)")
                        if s == 0:
                            do.run(v.tensor_copy(st[:, d, :], add), sem(f"state_{l}"))
                        else:
                            if ny and t < nt:
                                dve.wait_ge(*stage(f"mm_yoff_{l}", ny))
                            do.run(v.tensor_tensor(perhead(st[:, d, :]), perhead(st[:, d, :]), hb(edec[:, d, t, :]), ALU.mult))
                            do.run(v.tensor_tensor(st[:, d, :], st[:, d, :], add, ALU.add), sem(f"state_{l}"))
                        ns += 1
                do.run(v.memset(stat[:, 6, 0:1], 0.0), sem(f"scan_done_{l}"))

                def decayed(q):
                    u, d = q // 2, q % 2
                    t, g = u // SG, u % SG
                    dve.wait_ge(*stage(f"expd_{l}", q + 1))
                    for h in range(8):
                        ins = v.scalar_tensor_tensor(mt[:, q % 3, h, :], mt[:, q % 3, h, :], dt[:, d, t, g * 8 + h:g * 8 + h + 1], cbm[:, d, :], ALU.mult, ALU.mult)
                        do.mark(ins, sem(f"m_ready_{l}")) if h == 7 else None

                def add_y(u):
                    t, g = u // SG, u % SG
                    dve.wait_ge(*stage(f"mm_y_{l}", u + 1))
                    yy = y[:, t, g * NCH:(g + 1) * NCH]
                    do.run(v.tensor_tensor(yy, yy, ps[:, 5 + u % 2, :], ALU.add), sem(f"ev_y_{l}"))

                NQ = 2 * SG * nt
                for q in range(NQ + 1):
                    if q < NQ:
                        u, d = q // 2, q % 2
                        t, g = u // SG, u % SG
                        dve.wait_ge(*stage(f"mm_r_{l}", q + 1))
                        if q >= 3:
                            dve.wait_ge(*stage(f"mm_y_{l}", (q - 3) // 2 + 1))
                        for h in range(8):
                            ins = v.tensor_scalar(mt[:, q % 3, h, :], ps[:, 1 + 2 * (q % 2) + h // 4, (h % 4) * P:(h % 4 + 1) * P],
                                                  cum[:, d, t, g * 8 + h:g * 8 + h + 1], 0.0, ALU.subtract, ALU.min)
                        do.mark(ins, sem(f"diff_{l}"))
                    if q >= 1:
                        if (q - 1) % 2 == 0:
                            pu = (q - 1) // 2
                            dve.wait_ge(*stage(f"mm_cb_{l}", pu + 1))
                            for dd in range(2):
                                do.run(v.tensor_tensor(cbm[:, dd, :], ps[:, 0, 0:P], tri[dd], ALU.mult), sem(f"cbm_{l}"))
                        decayed(q - 1)
                        if (q - 1) % 2 == 1:
                            add_y((q - 1) // 2)
                end()

                dve.wait_ge(phase, phase_start(l, "gn"))
                for t in range(nt):
                    do.run(v.tensor_tensor(y[:, t, :], y[:, t, :], zs[:, t, :], ALU.mult), sem(f"yz_{l}"))
                dve.wait_ge(*stage(f"sq_gn_{l}", SG * nt))
                inverse_ms(SG * nt, NCH, sem(f"inv_gn_{l}"))
                dve.wait_ge(*stage(f"rstd_gn_{l}", 1))
                for t in range(nt):
                    for g in range(SG):
                        yy = y[:, t, g * NCH:(g + 1) * NCH]
                        ins = v.scalar_tensor_tensor(yy, yy, stat[:, 2, 2 * t + g:2 * t + g + 1], nw[:, g * NCH:(g + 1) * NCH], ALU.mult, ALU.mult)
                    do.run(ins, sem(f"gn_rows_{l}"))
                end()

                dve.wait_ge(phase, phase_start(l, "merge"))
                for u in range(6 * nt):
                    bn, t = u // nt, u % nt
                    b, n = bn // 2, bn % 2
                    dve.wait_ge(*stage(f"gate_{l}", u + 1))
                    dve.wait_ge(*stage(f"mm_br_{l}", u + 1))
                    dst = acc[:, t, n * NCH:(n + 1) * NCH]
                    if b == 0:
                        do.run(v.tensor_tensor(dst, ps[:, 2 + u % 2, :], gs[:, u % 2, :], ALU.mult), sem(f"gated_{l}"))
                    else:
                        do.run(v.tensor_tensor(tmp[:, 0:NCH], ps[:, 2 + u % 2, :], gs[:, u % 2, :], ALU.mult), sem(f"gated_{l}"))
                        do.run(v.tensor_tensor(dst, dst, tmp[:, 0:NCH], ALU.add), sem(f"mg_rows_{l}") if bn == 5 else None)
                end()

                def post(name, src):
                    dve.wait_ge(phase, phase_start(l, name))
                    dve.wait_ge(*stage(f"sq_{name}_{l}", nt))
                    inverse_ms(nt, D, sem(f"inv_{name}_{l}"))
                    dve.wait_ge(*stage(f"rstd_{name}_{l}", 1))
                    for t in range(nt):
                        s = 0 if t < LAT_TILES else 1
                        do.run(v.scalar_tensor_tensor(tmp[:, :], src[:, t, :], stat[:, 2, t:t + 1], bc[:, 2, s, :], ALU.mult, ALU.mult))
                        do.run(v.tensor_tensor(x[:, t, :], x[:, t, :], tmp[:, :], ALU.add))
                    end()

                post("out", ml)
                ada(1)
                norm(1, nt)

                dve.wait_ge(phase, phase_start(l, "router"))
                dve.wait_ge(*stage(f"scores_{l}", 1))
                for t in range(nt):
                    R = lambda i: rtr[:, i, t, :]
                    do.run(v.tensor_tensor(R(1), R(0), brt[:, :], ALU.add))
                    for g in range(8):
                        do.mark(v.max(R(2)[:, g * 8:(g + 1) * 8], R(1)[:, g * 8:(g + 1) * 8]))
                    dve.wait_ge(do.own, do.n[do.own.name])
                    top2 = R(2).rearrange("p (g e) -> p g e", e=8)
                    gsum = R(3)[:, 0:8]
                    do.run(v.tensor_tensor(gsum.unsqueeze(2), top2[:, :, 0:1], top2[:, :, 1:2], ALU.add))
                    mine = gsum.unsqueeze(2).to_broadcast([P, 8, 8])
                    other = gsum.unsqueeze(1).to_broadcast([P, 8, 8])
                    g88 = lambda i: R(i).rearrange("p (g e) -> p g e", e=8)
                    do.run(v.tensor_tensor(g88(4), other, mine, ALU.is_equal))
                    do.run(v.tensor_tensor(R(4), R(4), cst[:, C_TRI8:C_TRI8 + 64], ALU.mult))
                    do.run(v.tensor_tensor(g88(5), other, mine, ALU.is_gt))
                    do.run(v.tensor_tensor(R(5), R(5), R(4), ALU.add))
                    do.run(v.tensor_reduce(R(3)[:, 8:16], g88(5), AX.X, ALU.add))
                    do.run(v.tensor_scalar(R(3)[:, 16:24], R(3)[:, 8:16], 3.5, None, ALU.is_lt))
                    gm = R(3)[:, 16:24].unsqueeze(2).to_broadcast([P, 8, 8])
                    do.run(v.tensor_tensor(g88(6), g88(1), gm, ALU.mult))
                    do.run(v.tensor_scalar(R(3)[:, 24:32], R(3)[:, 16:24], 1.0, -NEG, ALU.subtract, ALU.mult))
                    do.run(v.tensor_tensor(g88(6), g88(6), R(3)[:, 24:32].unsqueeze(2).to_broadcast([P, 8, 8]), ALU.add))
                    do.run(v.max(R(7)[:, 0:8], R(6)))
                    do.run(v.match_replace(R(8), R(7)[:, 0:8], R(6), 3 * NEG))
                    do.run(v.tensor_tensor(R(8), R(8), R(6), ALU.not_equal))
                    do.run(v.tensor_tensor(R(9), R(8), R(0), ALU.mult))
                    do.run(v.tensor_reduce(R(7)[:, 8:9], R(9), AX.X, ALU.add))
                    do.run(v.reciprocal(R(7)[:, 9:10], R(7)[:, 8:9]))
                    do.run(v.tensor_scalar(R(10), R(9), R(7)[:, 9:10], ROUTED_SCALE, ALU.mult, ALU.mult))
                do.run(v.memset(acc[:, 0:nt, :], 0.0))
                end()

                dve.wait_ge(phase, phase_start(l, "moe"))
                down, act_h, ev_d, silu = (sem(f"{n}_{l}") for n in ("mm_down", "hidden", "ev_down", "silu"))

                def unit(t, u, w):
                    b = t % 2
                    dve.wait_ge(silu, u + 1)
                    v.tensor_tensor(hsg[:, b, :], hsg[:, b, :], ps[:, b, D_EXP:2 * D_EXP], ALU.mult).then_inc(act_h, 1)
                    dve.wait_ge(down, u + 1)
                    o = acc[:, t, :]
                    p2 = ps[:, 4 + 2 * b:6 + 2 * b, :].rearrange("p a n -> p (a n)")
                    if w is None:
                        v.tensor_tensor(o, p2, o, ALU.add).then_inc(ev_d, 1)
                    else:
                        v.scalar_tensor_tensor(o, p2, w, o, ALU.mult, ALU.add).then_inc(ev_d, 1)
                    dve.wait_ge(ev_d, u + 1)

                with dve.Fori(0, N_EXP) as i:
                    for t in range(nt):
                        unit(t, i * nt + t, rtr[:, 10, t, bass.ds(i, 1)])
                for t in range(nt):
                    unit(t, N_EXP * nt + t, None)
                end()
                post("post", acc)


BEFORE = {'x_loaded': 32,
 'mm_ccol': 1,
 'mm_ada0': 6,
 'mm_bc_ada0': 12,
 'mm_norm0': 8,
 'mm_xbc': 12,
 'mm_uT': 10,
 'mm_dt': 1,
 'mm_qkv': 12,
 'mm_z': 8,
 'mm_qT': 16,
 'mm_score': 64,
 'mm_pT': 64,
 'mm_pv': 64,
 'mm_oT': 8,
 'mm_cum': 1,
 'mm_state': 6,
 'mm_yoff': 6,
 'mm_cb': 8,
 'mm_r': 16,
 'mm_y': 8,
 'mm_gn': 8,
 'mm_gate': 24,
 'mm_br': 24,
 'mm_mg': 8,
 'mm_out': 8,
 'mm_ada1': 6,
 'mm_bc_ada1': 12,
 'mm_norm1': 8,
 'mm_router': 1,
 'bc_ada0': 12,
 'sq_norm0': 4,
 'rstd_norm0': 1,
 'ev_norm0': 8,
 'conv_in': 12,
 'conv_u': 12,
 'ev_proj': 20,
 'rstd_qk': 1,
 'ev_qT': 16,
 'prob': 64,
 'ev_pT': 64,
 'sinkexp': 4,
 'ev_oT': 8,
 'expA': 1,
 'softexp': 1,
 'softln': 1,
 'decays': 1,
 'expd': 16,
 'sq_gn': 8,
 'rstd_gn': 1,
 'ev_gn': 8,
 'gate': 24,
 'ev_mg': 8,
 'ev_out': 8,
 'sq_out': 4,
 'rstd_out': 1,
 'bc_ada1': 12,
 'sq_norm1': 4,
 'rstd_norm1': 1,
 'ev_norm1': 8,
 'scores': 1,
 'sq_post': 4,
 'rstd_post': 1,
 'ev_ada0': 6,
 'modrow_ada0': 2,
 'inv_norm0': 1,
 'hn_norm0': 4,
 'xp_zero': 2,
 'conv': 12,
 'ev_uT': 10,
 'inv_qk': 1,
 'roped': 8,
 'negmax': 64,
 'ev_o': 8,
 'sinkarg': 4,
 'nabs': 1,
 'onep': 1,
 'a_ready': 1,
 'cum': 1,
 'xw': 6,
 'state': 6,
 'ev_yoff': 6,
 'scan_done': 1,
 'diff': 16,
 'cbm': 16,
 'm_ready': 16,
 'ev_y': 8,
 'yz': 4,
 'inv_gn': 1,
 'gn_rows': 4,
 'gated': 24,
 'mg_rows': 4,
 'inv_out': 1,
 'ev_ada1': 6,
 'modrow_ada1': 2,
 'inv_norm1': 1,
 'hn_norm1': 4,
 'inv_post': 1}
EXP_BASE = [[l * 48 * (N_EXP // EXP_SLOTS + (1 if s == 0 else 0)) for s in range(EXP_SLOTS)] for l in range(DEPTH)]

_NAMES = ['x', 'c', 'ctx', 'c_ctx', 'w_ada', 'b_ada', 'g_mix_pre', 'g_mix_post', 'g_ffn_pre', 'g_ffn_post', 'w_in', 'g_q_a', 'g_k_a',
          'sink_w', 'ssm_conv_w', 'ssm_conv_b', 'ssm_dt_bias', 'ssm_a_log', 'ssm_d', 'ssm_norm', 'w_br_a', 'w_br_w', 'w_br_s', 'w_out',
          'w_router', 'b_router', 'we_gate', 'we_up', 'we_down', 'ws_gate', 'ws_up', 'ws_down']


def kernel(**inputs):
    import concourse.bacc as bacc
    from concourse.bass_utils import run_bass_kernel_spmd

    nc = bacc.Bacc("TRN2", target_bir_lowering=False, num_devices=1)
    arrays, aps = {}, {}
    for name in _NAMES:
        v = np.ascontiguousarray(inputs[name])
        arrays[f"in_{name}"] = v
        aps[name] = nc.dram_tensor(f"in_{name}", v.shape, mybir.dt.from_np(v.dtype), kind="ExternalInput").ap()
    arrays["in_constants"] = constants()
    cst_d = nc.dram_tensor("in_constants", (P, C_END), F32, kind="ExternalInput").ap()
    out = nc.dram_tensor("out", (1, SEG, D), F32, kind="ExternalOutput").ap()
    build(nc, aps, cst_d, out)
    r = run_bass_kernel_spmd(nc, [arrays], core_ids=[0])
    return r.results[0]["out"]
```

```python
import numpy as np
from contextlib import ExitStack
import concourse.bass as bass
from concourse import mybir

F32 = mybir.dt.float32
ALU = mybir.AluOpType
ACT = mybir.ActivationFunctionType
AX = mybir.AxisListType

P = 128
D = 1024
KD = D // P
DEPTH = 2
LAT_TILES, CTX_TILES = 2, 2
TILES = LAT_TILES + CTX_TILES
TOK = TILES * P
SEG = LAT_TILES * P
HD = 64
HEADS, KV = 8, 2
GQ = HEADS // KV
SH, SP_, SG, SN = 16, 64, 2, 128
SI = SH * SP_
CONV_T = 12
N_EXP, D_EXP = 64, 256
EPS = 1e-6
NEG = -1.0e30
SCALE = HD ** -0.5
ROUTED_SCALE = 2.5
TOP_K = 8
I32, U32 = mybir.dt.int32, mybir.dt.uint32
BLOCKS = TOK // P
CAP = TOK
NOROW = float(1 << 20)
XSTEPS = 11
X0 = 3
NCH = 512
COL_XBC, COL_DT, COL_QKV, COL_Z, COL_GATE = 2560, 4096, 0, 1536, 4128
RING = 3
EXP_SLOTS = 4

LOOP_SEMS = ("x_step", "x_gath", "x_scat", "x_weights")

C_ID, C_UT, C_LT, C_NA, C_NB, C_COS, C_SIN, C_SEL, C_TRI8, C_IOTA, C_PAY, C_THR, C_EID, C_COL, C_ONE, C_END = (
    0, 128, 256, 384, 512, 640, 768, 896, 1152, 1216, 1280, 1312, 1315, 1316, 1319, 1320)


def constants():
    c = np.zeros((P, C_END), np.float32)
    i = np.arange(P)
    c[:, C_ID:C_ID + P] = np.eye(P)
    c[:, C_UT:C_UT + P] = i[:, None] <= i[None, :]
    c[:, C_LT:C_LT + P] = i[:, None] >= i[None, :]
    c[:, C_NA:C_NA + P] = np.where(i[None, :] > i[:, None], NEG, 0)
    c[:, C_NB:C_NB + P] = np.where(i[None, :] < i[:, None], NEG, 0)
    c[:, C_ONE] = 1
    c[:, C_IOTA:C_IOTA + 64] = np.arange(64)
    for t in range(TILES):
        for k in range(TOP_K):
            c[:, C_PAY + t * TOP_K + k] = (t * P + i) * TOP_K + k
    for b in range(BLOCKS - 1):
        c[:, C_THR + b] = (b + 1) * P
        c[:, C_COL + b] = (b + 1) * N_EXP + i
    c[:, C_EID] = i
    half = HD // 2
    inv = np.float32(10000.0) ** (-np.arange(0, half, 2, dtype=np.float32) / np.float32(half))
    for t in range(LAT_TILES):
        tok = t * P + i
        ang = np.stack([(tok // 64).astype(np.float32)[:, None] * inv, (tok % 64).astype(np.float32)[:, None] * inv], 1)
        co, si = np.cos(ang), np.sin(ang)
        c[:, C_COS + t * HD:C_COS + (t + 1) * HD] = np.stack([co, co], 2).reshape(P, HD)
        c[:, C_SIN + t * HD:C_SIN + (t + 1) * HD] = np.stack([-si, si], 2).reshape(P, HD)
    c[0, C_SEL:C_SEL + P] = 1
    c[1, C_SEL + P:C_SEL + 2 * P] = 1
    g = np.arange(8)
    c[:, C_TRI8:C_TRI8 + 64] = (g[None, :] < g[:, None]).reshape(1, 64)
    return c


def ring_jobs():
    jobs = []
    for l in range(DEPTH):
        jobs += [(l, "ada0", n) for n in range(6)]
        jobs += [(l, "xbc", n) for n in range(3)]
        jobs += [(l, "qkv", n) for n in range(3)]
        jobs += [(l, "z", n) for n in range(2)]
        for b in range(3):
            for n in range(2):
                jobs += [(l, "gate", b * 2 + n), (l, "br", b * 2 + n)]
        jobs += [(l, "out", n) for n in range(2)]
        jobs += [(l, "ada1", n) for n in range(6)]
    return jobs


def build(nc, a, cst_d, out):
    jobs = ring_jobs()
    job_at = {j: i for i, j in enumerate(jobs)}
    per_layer = len(jobs) // DEPTH
    out_tiles = [TILES, LAT_TILES]
    before = BEFORE
    ctx = ExitStack()
    with ctx:
        top = [nc.sbuf_base + 31 & ~31]

        def at(name, shape, offset, dt=F32):
            return nc.alloc_sbuf_tensor_at(name, shape, dt, offset=offset)

        def region(nbytes):
            o = top[0]
            top[0] += nbytes + 31 & ~31
            return o

        sems = {}

        def instance(name):
            stem, l = name[:-2], name[-2:]
            if l not in ("_0", "_1") or stem in LOOP_SEMS:
                return name, 0
            for shared, members in SHARED.items():
                names = [m for m, _ in members]
                if stem in names:
                    here = sum(n[int(l[1])] for _, n in members[:names.index(stem)])
                    return shared, here + (sum(n[0] for _, n in members) if l == "_1" else 0)
            if stem[:-1].endswith(("ada", "norm")):
                both = before[stem[:-1]]
                return stem[:-1], (both if l == "_1" else 0) + (both // 2 if stem[-1] == "1" else 0)
            return stem, before[stem] if l == "_1" else 0

        def sem(name):
            name = instance(name)[0]
            if name not in sems:
                sems[name] = ctx.enter_context(nc.semaphore(name))
            return sems[name]

        def stage(name, value):
            return sem(name), value + instance(name)[1]

        x = at("x", [P, TILES, D], region(TILES * D * 4))
        r_ring = region(RING * KD * NCH * 4)
        ring = at("ring", [P, RING, KD, NCH], r_ring)
        r_qT = region(10 * TOK * 4)
        bcc = at("bcc", [P, 4, TOK], region(4 * TOK * 4))
        btok = at("btok", [P, TILES, 2 * SN], region(TILES * 2 * SN * 4))
        hT = at("hT", [P, KD, TOK], region(KD * TOK * 4))
        esl = at("esl", [P, EXP_SLOTS, 3, 2048], r_ring)
        comb = at("comb", [P, 4, 2, D], r_ring + RING * KD * NCH * 4)
        assert top[0] - r_ring >= EXP_SLOTS * 3 * 2048 * 4
        r_bc = region(6 * D * 4)
        bc = at("bc", [P, 3, 2, D], r_bc)
        zs = at("zs", [P, TILES, D], r_bc)
        mT = at("mT", [P, KD, TOK], r_bc)
        cst = at("cst", [P, C_END], region(C_END * 4))
        r_qk = region(TILES * 1536 * 4)
        qk = at("qk", [P, TILES, 1536], r_qk)
        modrow = at("modrow", [2, 3, D], r_qk)
        bada = at("bada", [2, 3 * D], r_qk + 3 * D * 4)
        y = at("y", [P, TILES, D], r_qk)
        st = at("st", [P, 2, SI], r_qk + TILES * D * 4)
        acc = at("acc", [P, TILES, D], r_qk)
        qT = at("qT", [P, 2, GQ, TOK], r_qT)
        kT = at("kT", [P, 2, TOK], r_qT + 2 * GQ * TOK * 4)
        oT = at("oT", [P, KD, TOK], r_qT)
        XPB = (2 * (SEG + 2) * 4 + 31) & ~31
        xp = [at(f"xp{i}", [P, 2, SEG + 2], r_qT + i * XPB) for i in range(2)]
        cacc = at("cacc", [P, 2, TOK], r_qT + 2 * XPB)
        cu = at("cu", [P, 2, TOK], r_qT + 2 * XPB + 2 * TOK * 4)
        gnorm = at("gnorm", [2, 2, D], r_qT)
        r_xs = region(TILES * SI * 4)
        xs = at("xs", [P, TILES, SI], r_xs)
        ysT = at("ysT", [P, KD, TOK], r_xs)
        ml = at("ml", [P, TILES, D], r_xs)
        r_t = region(3 * D * 4)
        hn = at("hn", [P, 2, D], r_t)
        pr = at("pr", [P, 2, NCH], r_t)
        pT = at("pT", [P, 2, NCH], r_t + 2 * NCH * 4)
        rt = at("rt", [P, 640], r_t)
        rq = at("rq", [P, 2, 640], r_t + 640 * 4)
        mt = at("mt", [P, 3, 8, P], r_t)
        tmp = at("tmp", [P, D], r_t + 2 * D * 4)
        gs = at("gs", [P, 2, NCH], r_t)
        junk = at("junk", [P, D], r_t + 2 * D * 4)
        hsg = at("hsg", [P, 2, D_EXP], r_t)
        hgT = at("hgT", [P, 2, 2, P], r_t + 2 * D_EXP * 4)
        r_nw = region(SI * 4)
        nw = at("nw", [P, SI], r_nw)
        xg = [at(f"xg{i}", [P, D], o) for i, o in enumerate((r_t + D * 4, r_t + 2 * D * 4, r_xs + 2 * D * 4, r_nw))]
        ysb = [at(f"ysb{i}", [P, D], o) for i, o in enumerate((r_bc + 2 * D * 4, r_bc + 3 * D * 4, r_xs, r_xs + D * 4))]
        xgT = at("xgT", [P, 2, KD, P], r_bc)
        r_rt = r_qk + TILES * D * 4
        oneh = at("oneh", [P, TOP_K, N_EXP], r_rt)
        onet = at("onet", [P, TOP_K, N_EXP], r_rt + 2048)
        tsb = at("tsb", [N_EXP, CAP], r_rt + 4096)
        nor = at("nor", [P, N_EXP * CAP // P], r_rt + 6144)
        eiu = at("eiu", [P, TILES, TOP_K], r_rt + 7168, U32)
        eif = at("eif", [P, TILES, TOP_K], r_rt + 7296)
        rnk = at("rnk", [P, TILES, TOP_K], r_rt + 7424)
        wk = at("wk", [P, TILES, TOP_K], r_rt + 7552)
        dst_i = at("dst_i", [P, TILES, TOP_K], r_rt + 7680, I32)
        xl = at("xl", [1, 72], r_rt + 7808, I32)
        gqk = at("gqk", [P, 640], r_t + 3 * 640 * 4)
        nsink = at("nsink", [P, HEADS], region(HEADS * 4))
        dtb = at("dtb", [P, 32], region(128))
        alog = at("alog", [P, 32], region(128))
        dsk = at("dsk", [P, SH], region(64))
        brt = at("brt", [P, N_EXP], region(256))
        crow = at("crow", [4 * CONV_T, P], region(512))
        ccol = at("ccol", [P, 4 * CONV_T], region(4 * CONV_T * 4))
        wdt = at("wdt", [P, KD, 32], region(KD * 32 * 4))
        r_small = region(9 * P * 4)
        dts = at("dts", [P, 9, 2, TILES, SH], r_small)
        wr = at("wr", [P, KD, N_EXP], r_xs)
        rtr = at("rtr", [P, 12, TILES, N_EXP], r_xs + KD * N_EXP * 4)
        gi = at("gi", [P, BLOCKS * N_EXP], r_xs + 14336, I32)
        si = at("si", [P, BLOCKS * N_EXP], r_xs + 15360, I32)
        gstg = at("gstg", [P, EXP_SLOTS], region(32), I32)
        sstg = at("sstg", [P, EXP_SLOTS], region(32), I32)
        stat = at("stat", [P, 8, 64], region(8 * 64 * 4))
        cT = at("cT", [P, 16], region(64))
        crw = at("crw", [16, P], region(512))
        cbm = at("cbm", [P, 2, P], region(2 * P * 4))

        ps = ctx.enter_context(nc.psum_tensor("ps", [P, 8, NCH], F32))

        h_d = nc.dram_tensor("h_rows", (TOK, D), F32, kind="Internal").ap()
        tab_d = nc.dram_tensor("slot_table", (N_EXP * CAP, 1), F32, kind="Internal").ap()
        y_d = nc.dram_tensor("routed_rows", (TOK * TOP_K, D), F32, kind="Internal").ap()

        ident = cst[:, C_ID:C_ID + P]
        UT, LT = cst[:, C_UT:C_UT + P], cst[:, C_LT:C_LT + P]
        tri = [UT, LT]
        ones = cst[:, C_ONE:C_ONE + 1].to_broadcast([P, P])
        cond = sem("cond_loaded")
        param = sem("params_loaded")
        phase = sem("phase_done")
        full = [sem(f"ring_full{i}") for i in range(RING)]
        efull = [sem(f"weights{i}_0") for i in range(EXP_SLOTS)]

        def max_extra(l):
            return out_tiles[l] * P * TOP_K // (P + 1)

        def qkv_units(l):
            return [(n, t) for n in range(3) for t in range(TILES) if n > 0 or t < out_tiles[l]]

        def attn_units(l):
            return [(t, ty, g, h) for t in range(out_tiles[l]) for ty in range(2) for g in range(KV) for h in range(GQ)]

        def scan_order(d):
            ctx_t, lat_t = [2, 3], [0, 1]
            return ctx_t + lat_t if d == 0 else ctx_t[::-1] + lat_t[::-1]

        def scan_steps(l):
            return [(s, d, scan_order(d)[s]) for s in range(4) for d in range(2)]

        def tr_units(l):
            return [(t, ty) for t in range(TILES) for ty in range(2)]

        def has_q(l, t):
            return t < out_tiles[l]

        def last_use(j):
            l, kind, n = jobs[j]
            if kind in ("ada0", "ada1"):
                return stage(f"mm_{kind}_{l}", n + 1)
            if kind == "xbc":
                return stage(f"mm_xbc_{l}", 4 * (n + 1))
            if kind == "qkv":
                u = qkv_units(l)
                return stage(f"mm_qkv_{l}", max(i for i, (m, _) in enumerate(u) if m == n) + 1)
            if kind == "z":
                return stage(f"mm_z_{l}", (n + 1) * out_tiles[l])
            if kind == "gate":
                return stage(f"mm_gate_{l}", (n + 1) * out_tiles[l])
            if kind == "br":
                return stage(f"mm_br_{l}", (n + 1) * out_tiles[l])
            return stage(f"mm_out_{l}", (n + 1) * out_tiles[l])

        def ring_source(j):
            l, kind, n = jobs[j]
            rows = lambda w, c: w[:, c:c + NCH].rearrange("(k p) n -> p k n", p=P)
            if kind in ("ada0", "ada1"):
                return rows(a["w_ada"][l], (3 * D if kind == "ada1" else 0) + n * NCH)
            if kind in ("xbc", "qkv", "z", "gate"):
                base = {"xbc": COL_XBC, "qkv": COL_QKV, "z": COL_Z, "gate": COL_GATE}[kind]
                return rows(a["w_in"][l], base + n * NCH)
            if kind == "br":
                return rows(a[("w_br_a", "w_br_w", "w_br_s")[n // 2]][l], (n % 2) * NCH)
            return rows(a["w_out"][l], n * NCH)

        def chunk(l, kind, n):
            j = job_at[(l, kind, n)]
            return ring[:, j % RING], (full[j % RING], 16 * (j // RING + 1))

        PH = ["ada0", "norm0", "inproj", "attn", "ssd", "gn", "merge", "out", "ada1", "norm1", "router", "moe", "post"]

        def phase_start(l, name):
            return 2 * (l * len(PH) + PH.index(name))

        class Steps:

            def __init__(self, eng, own):
                self.eng, self.own, self.n = eng, own, {}

            def mark(self, ins, s=None):
                s = s if s is not None else self.own
                self.n[s.name] = self.n.get(s.name, 0) + 1
                ins.then_inc(s, 1)

            def run(self, ins, s=None):
                s = s if s is not None else self.own
                self.mark(ins, s)
                self.eng.wait_ge(s, self.n[s.name])

        block = ctx.enter_context(nc.Block())

        @block.sync
        def _(sp):
            def load_ring(j):
                if j >= RING:
                    sp.wait_ge(*last_use(j - RING))
                src = ring_source(j)
                sp.dma_start(ring[:, j % RING, 0:src.shape[1], :], src).then_inc(full[j % RING], 16)

            def load_expert(slot, wg, wu, wd, s=None):
                for i, (w, n) in enumerate(((wg, D_EXP), (wu, D_EXP), (wd, D))):
                    sp.dma_start(esl[:, slot, i, :].rearrange("p (k n) -> p k n", n=n), w.rearrange("(k p) n -> p k n", p=P))\
                        .then_inc(s if s is not None else efull[slot], 16)

            def expert(l, e):
                return [a[n][l, bass.ds(e, 1)].rearrange("o r n -> (o r) n") for n in ("we_gate", "we_up", "we_down")]

            sp.dma_start(x[:, 0:LAT_TILES, :], a["x"][0].rearrange("(t p) d -> p t d", p=P)).then_inc(sem("x_loaded"), 16)
            sp.dma_start(x[:, LAT_TILES:, :], a["ctx"][0].rearrange("(t p) d -> p t d", p=P)).then_inc(sem("x_loaded"), 16)
            for l in range(DEPTH):
                for j in range(l * per_layer, (l + 1) * per_layer):
                    load_ring(j)
                nt = out_tiles[l]
                for j in range((l + 1) * per_layer - RING, (l + 1) * per_layer):
                    sp.wait_ge(*last_use(j))
                sp.wait_ge(*stage(f"mm_norm1_{l}", 1))
                load_expert(2, a["ws_gate"][l], a["ws_up"][l], a["ws_down"][l])
                for e in range(EXP_SLOTS):
                    if e == 2:
                        sp.wait_ge(*stage(f"mm_sdown_{l}", nt))
                    load_expert(e, *expert(l, e))
                with sp.Fori(0, N_EXP // EXP_SLOTS - 1) as r:
                    for s in range(EXP_SLOTS):
                        sp.wait_ge(*stage(f"mm_down_{l}", r * EXP_SLOTS + (s + 1)))
                        load_expert(s, *expert(l, r * EXP_SLOTS + (s + EXP_SLOTS)))
                sp.wait_ge(*stage(f"mm_down_{l}", N_EXP))
                sp.wait_ge(*stage(f"list_ready_{l}", 1))
                n = sp.value_load(xl[0:1, 64:65], min_val=0, max_val=max_extra(l))
                with sp.Fori(0, max_extra(l)) as j:
                    with sp.If(j < n):
                        e = sp.value_load(xl[0:1, bass.ds(j, 1)], min_val=0, max_val=N_EXP - 1)
                        sp.wait_ge(sem(f"x_step_{l}"), j * XSTEPS + (X0 - XSTEPS + 9))
                        load_expert(0, *expert(l, e), s=sem(f"x_weights_{l}"))
                        sp.wait_ge(sem(f"x_step_{l}"), j * XSTEPS + (X0 + 9))
                        sp.sem_inc(sem("sync_passed"), 1)
            sp.wait_ge(phase, phase_start(DEPTH, "ada0"))
            sp.dma_start(out[0].rearrange("(t p) d -> p t d", p=P), x[:, 0:LAT_TILES, :]).then_inc(sem("out_written"), 16)
            sp.wait_ge(sem("out_written"), 16)

        @block.gpsimd
        def _(pool):
            def rows(dst, src):
                pool.dma_start(dst, src).then_inc(param, 16)

            def dispatch(l):
                nt = out_tiles[l]
                for t in range(nt):
                    pool.wait_ge(*stage(f"hn_norm1_{l}", t + 1))
                    pool.dma_start(h_d[t * P:(t + 1) * P, :], hn[:, t % 2, :]).then_inc(sem(f"h_written{t % 2}_{l}"), 16)
                pool.wait_ge(*stage(f"norow_{l}", 1))
                pool.dma_start(tab_d.rearrange("(p n) o -> p (n o)", p=P), nor[:, :]).then_inc(sem(f"tab_cleared_{l}"), 16)
                pool.wait_ge(*stage(f"tab_cleared_{l}", 16))
                pool.wait_ge(*stage(f"dest_{l}", EXP_SLOTS))
                for t in range(nt):
                    for k in range(TOP_K):
                        c = t * TOP_K + k
                        pool.indirect_dma_start(out=tab_d, out_offset=bass.IndirectOffsetOnAxis(ap=dst_i[:, t, k:k + 1], axis=0),
                                                in_=cst[:, C_PAY + c:C_PAY + c + 1], in_offset=None).then_inc(sem(f"tab_written_{l}"), 16)
                pool.wait_ge(*stage(f"tab_written_{l}", 16 * nt * TOP_K))
                pool.dma_start(tsb[:, :], tab_d.rearrange("(e c) o -> e (c o)", c=CAP)).then_inc(sem(f"tab_read_{l}"), 16)
                for i in range(2):
                    pool.wait_ge(*stage(f"h_written{i}_{l}", 16 * nt // 2))

                def gather(e, slot):
                    pool.wait_ge(*stage(f"staged_{l}", e + 1))
                    pool.sem_inc(sem("pool_passed"), 1)
                    pool.indirect_dma_start(out=xg[slot][:, :], out_offset=None, in_=h_d,
                                            in_offset=bass.IndirectOffsetOnAxis(ap=gstg[:, slot:slot + 1], axis=0),
                                            bounds_check=nt * P - 1, oob_is_err=False).then_inc(sem(f"gath{slot}_{l}"), 16)

                def scatter(e, slot):
                    pool.wait_ge(*stage(f"ev_ya_{l}", e + 1))
                    pool.wait_ge(*stage(f"ev_yv_{l}", e + 1))
                    pool.sem_inc(sem("pool_passed"), 1)
                    pool.indirect_dma_start(out=y_d, out_offset=bass.IndirectOffsetOnAxis(ap=sstg[:, slot:slot + 1], axis=0),
                                            in_=ysb[slot][:, :], in_offset=None,
                                            bounds_check=nt * P * TOP_K - 1, oob_is_err=False).then_inc(sem(f"scat{slot}_{l}"), 16)

                def step(e, j):
                    gather(e + EXP_SLOTS, j)
                    scatter(e - 1, (j + 3) % 4)

                for e in range(EXP_SLOTS + 1):
                    gather(e, e % 4)
                for e in (1, 2, 3):
                    step(e, e)
                with pool.Fori(1, N_EXP // 4 - 1) as r:
                    for j in range(4):
                        step(r * 4 + j, j)
                for e in range(N_EXP - 4, N_EXP + 1):
                    scatter(e - 1, (e - 1) % 4)
                for i in range(EXP_SLOTS):
                    pool.wait_ge(*stage(f"scat{i}_{l}", 16 * N_EXP // EXP_SLOTS))
                pool.wait_ge(*stage(f"list_ready_{l}", 1))
                n = pool.value_load(xl[0:1, 64:65], min_val=0, max_val=max_extra(l))
                with pool.Fori(0, max_extra(l)) as j:
                    with pool.If(j < n):
                        pool.wait_ge(sem(f"x_step_{l}"), j * XSTEPS + (X0 + 1))
                        pool.sem_inc(sem("pool_passed"), 1)
                        pool.indirect_dma_start(out=xg[0][:, :], out_offset=None, in_=h_d,
                                                in_offset=bass.IndirectOffsetOnAxis(ap=gstg[:, 0:1], axis=0),
                                                bounds_check=nt * P - 1, oob_is_err=False).then_inc(sem(f"x_gath_{l}"), 16)
                        pool.wait_ge(sem(f"x_step_{l}"), j * XSTEPS + (X0 + 10))
                        pool.sem_inc(sem("pool_passed"), 1)
                        pool.indirect_dma_start(out=y_d, out_offset=bass.IndirectOffsetOnAxis(ap=sstg[:, 0:1], axis=0),
                                                in_=ysb[0][:, :], in_offset=None,
                                                bounds_check=nt * P * TOP_K - 1, oob_is_err=False).then_inc(sem(f"x_scat_{l}"), 16)
                        pool.wait_ge(sem(f"x_scat_{l}"), j * 16 + 16)
                        pool.sem_inc(sem(f"x_step_{l}"), 1)
                pool.wait_ge(*stage(f"mm_down_{l}", N_EXP))
                for u in range(nt * 4):
                    t, kp = u // 4, u % 4
                    if u >= 4:
                        pool.wait_ge(*stage(f"combined_{l}", u - 3))
                    pool.dma_start(comb[:, kp, :, :], y_d[t * P * TOP_K:(t + 1) * P * TOP_K, :]
                                   .rearrange("(p k) d -> p k d", k=TOP_K)[:, 2 * kp:2 * kp + 2, :]).then_inc(sem(f"comb{kp}_{l}"), 16)

            pool.dma_start(cst[:, :], cst_d).then_inc(cond, 16)
            pool.dma_start(crw[0:8, :], a["c"].rearrange("o (k p) -> (o k) p", p=P)).then_inc(cond, 16)
            pool.dma_start(crw[8:16, :], a["c_ctx"].rearrange("(k p) -> k p", p=P)).then_inc(cond, 16)
            for l in range(DEPTH):
                if l:
                    pool.wait_ge(phase, phase_start(l, "ada0"))
                for half in range(2):
                    if half:
                        pool.wait_ge(phase, phase_start(l, "ada1"))
                    rows(bada[:, :], a["b_ada"][l, half * 3 * D:(half + 1) * 3 * D].partition_broadcast(2))
                    rows(gnorm[:, 0, :], a[("g_mix_pre", "g_ffn_pre")[half]][l].partition_broadcast(2))
                    rows(gnorm[:, 1, :], a[("g_mix_post", "g_ffn_post")[half]][l].partition_broadcast(2))
                    if half == 0:
                        rows(dtb[:, :], a["ssm_dt_bias"][l].rearrange("d h -> (d h)").partition_broadcast(P))
                        rows(alog[:, :], a["ssm_a_log"][l].rearrange("d h -> (d h)").partition_broadcast(P))
                        rows(dsk[:, :], a["ssm_d"][l].partition_broadcast(P))
                        rows(nw[:, :], a["ssm_norm"][l].partition_broadcast(P))
                        rows(nsink[:, :], a["sink_w"][l].partition_broadcast(P))
                        rows(brt[:, :], a["b_router"][l].partition_broadcast(P))
                        rows(crow[0:36, :], a["ssm_conv_w"][l].rearrange("w (c p) -> (w c) p", p=P))
                        rows(crow[36:48, :], a["ssm_conv_b"][l].rearrange("(c p) -> c p", p=P))
                        rows(wdt[:, :, :], a["w_in"][l][:, COL_DT:COL_DT + 32].rearrange("(k p) n -> p k n", p=P))
                        pool.wait_ge(phase, phase_start(l, "inproj"))
                        for h in range(HEADS + KV):
                            pool.dma_start(gqk[:, h * HD:(h + 1) * HD],
                                           a["g_q_a" if h < HEADS else "g_k_a"][l].partition_broadcast(P)).then_inc(sem("gqk_loaded"), 16)
                    else:
                        rows(wr[:, :, :], a["w_router"][l].rearrange("(k p) n -> p k n", p=P))
                dispatch(l)

        HALF_LOADS = [3 + 6 + 3, 3 + 1]

        def params_at(l, half):
            return 16 * (l * sum(HALF_LOADS) + HALF_LOADS[0] + (HALF_LOADS[1] if half else 0))

        @block.tensor
        def _(pe):
            def mms(o, pairs, start=True, stop=True):
                for i, (lt, rh) in enumerate(pairs):
                    last = nc.tensor.matmul(o, lt, rh, start=start and i == 0, stop=stop and i == len(pairs) - 1)
                return last

            def transposes(bank, ins):
                for i, blk in enumerate(ins):
                    last = nc.tensor.transpose(ps[:, bank, i * P:(i + 1) * P], blk, ident)
                return last

            pe.wait_ge(cond, 16 * 3)
            nc.tensor.transpose(ps[:, 0, 0:16], crw[:, :], cst[0:16, C_ID:C_ID + 16]).then_inc(sem("mm_cond"), 1)
            pe.wait_ge(sem("cond_silu"), 2)
            for l in range(DEPTH):
                nt = out_tiles[l]

                def ada(half):
                    kind = f"ada{half}"
                    pe.wait_ge(phase, phase_start(l, kind)) if phase_start(l, kind) else None
                    if half == 0:
                        pe.wait_ge(param, params_at(l, 0))
                        nc.tensor.transpose(ps[:, 6, 0:48], crow[:, :], cst[0:48, C_ID:C_ID + 48]).then_inc(sem(f"mm_ccol_{l}"), 1)
                    for n in range(6):
                        w, ready = chunk(l, kind, n)
                        pe.wait_ge(*ready)
                        if n >= 2:
                            pe.wait_ge(*stage(f"ev_{kind}_{l}", n - 1))
                        mms(ps[0:2, n % 2, :], [(cT[:, k::8], w[:, k, :]) for k in range(KD)]).then_inc(sem(f"mm_{kind}_{l}"), 1)
                    pe.wait_ge(*stage(f"modrow_{kind}_{l}", 2))
                    for i in range(12):
                        v, s, n2 = i // 4, i // 2 % 2, i % 2
                        if i >= 4:
                            pe.wait_ge(*stage(f"bc_{kind}_{l}", i - 3))
                        mms(ps[:, 2 + i % 4, :], [(cst[0:2, C_SEL + s * P:C_SEL + (s + 1) * P], modrow[:, v, n2 * NCH:(n2 + 1) * NCH])])\
                            .then_inc(sem(f"mm_bc_{kind}_{l}"), 1)

                def norm(half, tiles):
                    kind = f"norm{half}"
                    pe.wait_ge(phase, phase_start(l, kind))
                    for t in range(tiles):
                        pe.wait_ge(*stage(f"hn_{kind}_{l}", t + 1))
                        for b in range(2):
                            u = 2 * t + b
                            if u >= 4:
                                pe.wait_ge(*stage(f"ev_{kind}_{l}", u - 3))
                            transposes(u % 4, [hn[:, t % 2, (4 * b + i) * P:(4 * b + i + 1) * P] for i in range(4)])\
                                .then_inc(sem(f"mm_{kind}_{l}"), 1)

                ada(0)
                norm(0, TILES)

                pe.wait_ge(phase, phase_start(l, "inproj"))

                def conv_transposes(ct):
                    pe.wait_ge(*stage(f"conv_u_{l}", ct + 1))
                    if ct >= 2:
                        pe.wait_ge(*stage(f"ev_uT_{l}", ct - 1))
                    src = cu[:, ct % 2, :] if ct < 8 else bcc[:, ct - 8, :]
                    transposes(2 + ct % 2, [src[:, t * P:(t + 1) * P] for t in range(TILES)]).then_inc(sem(f"mm_uT_{l}"), 1)

                for ct in range(CONV_T):
                    w, ready = chunk(l, "xbc", ct // 4)
                    pe.wait_ge(*ready)
                    if ct >= 2:
                        pe.wait_ge(*stage(f"conv_in_{l}", ct - 1))
                    mms(ps[:, ct % 2, :], [(w[:, k, (ct % 4) * P:(ct % 4 + 1) * P], hT[:, k, :]) for k in range(KD)])\
                        .then_inc(sem(f"mm_xbc_{l}"), 1)
                    if ct >= 2:
                        conv_transposes(ct - 2)
                for t in range(TILES):
                    last = mms(ps[:, 4, t * 32:(t + 1) * 32], [(hT[:, k, t * P:(t + 1) * P], wdt[:, k, :]) for k in range(KD)])
                last.then_inc(sem(f"mm_dt_{l}"), 1)
                u = 0
                for kind, units in (("qkv", qkv_units(l)), ("z", [(n, t) for n in range(2) for t in range(nt)])):
                    for n, t in units:
                        w, ready = chunk(l, kind, n)
                        pe.wait_ge(*ready)
                        if u >= 3:
                            pe.wait_ge(*stage(f"ev_proj_{l}", u - 2))
                        mms(ps[:, 5 + u % 3, :], [(hT[:, k, t * P:(t + 1) * P], w[:, k, :]) for k in range(KD)])\
                            .then_inc(sem(f"mm_{kind}_{l}"), 1)
                        u += 1

                pe.wait_ge(phase, phase_start(l, "attn"))
                e = 0
                for i, (t, ty) in enumerate(tr_units(l)):
                    pe.wait_ge(*stage(f"roped_{l}", i + 1))
                    for part in range(2):
                        if part == 0 and not has_q(l, t):
                            continue
                        if e >= 4:
                            pe.wait_ge(*stage(f"ev_qT_{l}", e - 3))
                        ins = [rq[:, i % 2, h * P:(h + 1) * P] for h in range(GQ)] if part == 0 else [rq[:, i % 2, 512:640]]
                        transposes(e % 4, ins).then_inc(sem(f"mm_qT_{l}"), 1)
                        e += 1
                pe.wait_ge(*stage(f"ev_qT_{l}", e))
                units = attn_units(l)

                def keys(t):
                    return (0, TILES) if t < LAT_TILES else (LAT_TILES, TILES)

                for i in range(len(units) + 2):
                    if i < len(units):
                        t, ty, g, h = units[i]
                        k0, k1 = keys(t)
                        if i >= 3:
                            pe.wait_ge(*stage(f"prob_{l}", i - 2))
                        o = ps[:, i % 3, 0:(k1 - k0) * P]
                        part = slice(g * HD, (g + 1) * HD)
                        masked = ty == 1 and t < LAT_TILES
                        m = nc.tensor.matmul(o, qT[part, ty, h, t * P:(t + 1) * P], kT[part, ty, k0 * P:k1 * P], start=True, stop=not masked)
                        if masked:
                            neg = cst[:, C_NA:C_NA + P] if t == 0 else cst[:, C_NB:C_NB + P]
                            m = nc.tensor.matmul(ps[:, i % 3, (1 - t) * P:(2 - t) * P], ident, neg, start=False, stop=True)
                        m.then_inc(sem(f"mm_score_{l}"), 1)
                    if 1 <= i <= len(units):
                        j = i - 1
                        t = units[j][0]
                        k0, k1 = keys(t)
                        pe.wait_ge(*stage(f"prob_{l}", j + 1))
                        if j >= 2:
                            pe.wait_ge(*stage(f"ev_pT_{l}", j - 1))
                        transposes(3 + j % 2, [pr[:, j % 2, c * P:(c + 1) * P] for c in range(k1 - k0)]).then_inc(sem(f"mm_pT_{l}"), 1)
                    if i >= 2:
                        j = i - 2
                        t, ty, g, h = units[j]
                        k0, k1 = keys(t)
                        pe.wait_ge(*stage(f"ev_pT_{l}", j + 1))
                        grp, hh = j // HEADS, j % HEADS
                        if hh == 0 and grp >= 2:
                            pe.wait_ge(*stage(f"ev_o_{l}", grp - 1))
                        v0 = ty * 768 + 640 + g * HD
                        mms(ps[:, 5 + grp % 2, hh * HD:(hh + 1) * HD],
                            [(pT[:, j % 2, c * P:(c + 1) * P], qk[:, k0 + c, v0:v0 + HD]) for c in range(k1 - k0)])\
                            .then_inc(sem(f"mm_pv_{l}"), 1)
                for t in range(nt):
                    pe.wait_ge(*stage(f"ev_o_{l}", 2 * (t + 1)))
                    for ty in range(2):
                        u = 2 * t + ty
                        if u >= 2:
                            pe.wait_ge(*stage(f"ev_oT_{l}", u - 1))
                        if u == 0:
                            pe.wait_ge(*stage(f"ev_pT_{l}", len(units)))
                        transposes(3 + u % 2, [qk[:, t, ty * 768 + c * P:ty * 768 + (c + 1) * P] for c in range(4)])\
                            .then_inc(sem(f"mm_oT_{l}"), 1)

                pe.wait_ge(phase, phase_start(l, "ssd"))
                pe.wait_ge(*stage(f"a_ready_{l}", 1))
                for d in range(2):
                    mms(ps[:, 7, d * 64:(d + 1) * 64], [(tri[d], dts[:, 1, d])])
                mms(ps[:, 7, 128:256], [(ones, dts[:, 1])]).then_inc(sem(f"mm_cum_{l}"), 1)
                ny = ns = 0
                for s, d, t in scan_steps(l):
                    if s > 0 and t < nt:
                        pe.wait_ge(*stage(f"state_{l}", 2 * (s - 1) + d + 1))
                        if ny >= 2:
                            pe.wait_ge(*stage(f"ev_yoff_{l}", ny - 1))
                        for g in range(SG):
                            m = mms(ps[:, 2 * (ny % 2) + g, :], [(bcc[:, 2 + g, t * P:(t + 1) * P], st[:, d, g * NCH:(g + 1) * NCH])])
                        m.then_inc(sem(f"mm_yoff_{l}"), 1)
                        ny += 1
                    if s < 3:
                        pe.wait_ge(*stage(f"xw_{l}", ns + 1))
                        for g in range(SG):
                            m = mms(ps[:, 4 + g, :], [(btok[:, t, g * SN:(g + 1) * SN], tmp[:, g * NCH:(g + 1) * NCH])])
                        m.then_inc(sem(f"mm_state_{l}"), 1)
                        ns += 1
                pe.wait_ge(*stage(f"scan_done_{l}", 1))
                q = 0
                for u in range(nt * SG + 1):
                    for d in range(2):
                        if u < nt * SG:
                            t, g = u // SG, u % SG
                            if d == 0:
                                if u >= 1:
                                    pe.wait_ge(*stage(f"cbm_{l}", 2 * u))
                                mms(ps[:, 0, 0:P], [(bcc[:, g, t * P:(t + 1) * P], bcc[:, 2 + g, t * P:(t + 1) * P])]).then_inc(sem(f"mm_cb_{l}"), 1)
                            if q >= 2:
                                pe.wait_ge(*stage(f"diff_{l}", q - 1))
                            for h in range(8):
                                last = mms(ps[:, 1 + 2 * (q % 2) + h // 4, (h % 4) * P:(h % 4 + 1) * P],
                                           [(dts[:, 1, d, t, g * 8 + h:g * 8 + h + 1].to_broadcast([P, P]), tri[d])])
                            last.then_inc(sem(f"mm_r_{l}"), 1)
                            q += 1
                    if u >= 1:
                        pu = u - 1
                        t, g = pu // SG, pu % SG
                        pe.wait_ge(*stage(f"m_ready_{l}", 2 * u))
                        if pu >= 2:
                            pe.wait_ge(*stage(f"ev_y_{l}", pu - 1))
                        for h in range(8):
                            for d in range(2):
                                hh = g * 8 + h
                                last = nc.tensor.matmul(ps[:, 5 + pu % 2, h * HD:(h + 1) * HD], mt[:, (2 * pu + d) % 3, h, :],
                                                        xs[:, t, hh * HD:(hh + 1) * HD], start=d == 0, stop=d == 1)
                        last.then_inc(sem(f"mm_y_{l}"), 1)

                def row_transposes(name, tiles, src):
                    for t in range(tiles):
                        pe.wait_ge(*stage(f"{name}_rows_{l}", t + 1))
                        for b in range(2):
                            u = 2 * t + b
                            if u >= 4:
                                pe.wait_ge(*stage(f"ev_{name}_{l}", u - 3))
                            transposes(4 + u % 4, [src[:, t, (4 * b + i) * P:(4 * b + i + 1) * P] for i in range(4)])\
                                .then_inc(sem(f"mm_{name}_{l}"), 1)

                pe.wait_ge(phase, phase_start(l, "gn"))
                row_transposes("gn", nt, y)

                pe.wait_ge(phase, phase_start(l, "merge"))
                u = 0
                for bn in range(6):
                    b, n = bn // 2, bn % 2
                    wg, g_ready = chunk(l, "gate", bn)
                    wb, b_ready = chunk(l, "br", bn)
                    pe.wait_ge(*g_ready)
                    pe.wait_ge(*b_ready)
                    src = [(oT, 0, 4), (oT, 4, 4), (ysT, 0, 8)][b]
                    for t in range(nt):
                        if u >= 2:
                            pe.wait_ge(*stage(f"gated_{l}", u - 1))
                        mms(ps[:, u % 2, :], [(hT[:, k, t * P:(t + 1) * P], wg[:, k, :]) for k in range(KD)]).then_inc(sem(f"mm_gate_{l}"), 1)
                        mms(ps[:, 2 + u % 2, :], [(src[0][:, src[1] + k, t * P:(t + 1) * P], wb[:, k, :]) for k in range(src[2])])\
                            .then_inc(sem(f"mm_br_{l}"), 1)
                        u += 1
                row_transposes("mg", nt, acc)

                pe.wait_ge(phase, phase_start(l, "out"))
                for u, (n, t) in enumerate([(n, t) for n in range(2) for t in range(nt)]):
                    w, ready = chunk(l, "out", n)
                    pe.wait_ge(*ready)
                    if u >= 2:
                        pe.wait_ge(*stage(f"ev_out_{l}", u - 1))
                    mms(ps[:, u % 2, :], [(mT[:, k, t * P:(t + 1) * P], w[:, k, :]) for k in range(KD)]).then_inc(sem(f"mm_out_{l}"), 1)

                ada(1)
                norm(1, nt)

                pe.wait_ge(phase, phase_start(l, "router"))
                pe.wait_ge(param, params_at(l, 1))
                for t in range(nt):
                    last = mms(ps[:, 0, t * N_EXP:(t + 1) * N_EXP], [(hT[:, k, t * P:(t + 1) * P], wr[:, k, :]) for k in range(KD)])
                last.then_inc(sem(f"mm_router_{l}"), 1)

                pe.wait_ge(*stage(f"masks_{l}", 1))
                for t in range(nt):
                    mms(ps[:, 1, t * N_EXP:(t + 1) * N_EXP], [(UT, rtr[:, 8, t, :])] + [(ones, rtr[:, 8, i, :]) for i in range(t)])
                mms(ps[0:N_EXP, 2, 0:1], [(rtr[:, 8, t, :], cst[:, C_ONE:C_ONE + 1]) for t in range(nt)]).then_inc(sem(f"mm_rank_{l}"), 1)

                pe.wait_ge(phase, phase_start(l, "moe"))
                pe.wait_ge(*stage(f"weights2_{l}", 48))
                for t in range(nt):
                    b = t % 2
                    wgu = esl[:, 2, 0:2, :].rearrange("p a (k n) -> p k a n", n=D_EXP)
                    if t >= 2:
                        pe.wait_ge(*stage(f"shid_{l}", t - 1))
                    mms(ps[:, b, :].rearrange("p (a n) -> p a n", a=2), [(hT[:, k, t * P:(t + 1) * P], wgu[:, k]) for k in range(KD)])\
                        .then_inc(sem(f"mm_sgu_{l}"), 1)
                    pe.wait_ge(*stage(f"shid_{l}", t + 1))
                    transposes(2 + b, [hsg[:, b, c * P:(c + 1) * P] for c in range(2)]).then_inc(sem(f"mm_shT_{l}"), 1)
                    pe.wait_ge(*stage(f"ev_shT_{l}", t + 1))
                    if t >= 2:
                        pe.wait_ge(*stage(f"ev_sy_{l}", t - 1))
                    for n in range(2):
                        m = mms(ps[:, 4 + 2 * b + n, :], [(hgT[:, b, c, :], esl[:, 2, 2, c * D + n * NCH:c * D + (n + 1) * NCH]) for c in range(2)])
                    m.then_inc(sem(f"mm_sdown_{l}"), 1)

                pe.wait_ge(*stage(f"tab_read_{l}", 16))
                for b in range(BLOCKS):
                    m = nc.tensor.transpose(ps[:, 0, b * N_EXP:(b + 1) * N_EXP], tsb[:, b * P:(b + 1) * P], cst[0:N_EXP, C_ID:C_ID + N_EXP])
                m.then_inc(sem(f"mm_tab_{l}"), 1)
                pe.wait_ge(*stage(f"flags_{l}", 1))
                e64 = slice(0, N_EXP)
                mms(ps[e64, 1, 0:3], [(cst[e64, C_UT:C_UT + N_EXP], stat[e64, 0, 0:3])])
                mms(ps[e64, 1, 3:6], [(cst[e64, C_ONE:C_ONE + 1].to_broadcast([N_EXP, N_EXP]), stat[e64, 0, 0:3])]).then_inc(sem(f"mm_pos_{l}"), 1)
                pe.wait_ge(*stage(f"places_{l}", 1))
                xoh = stat[e64, 4:6, :].rearrange("p a n -> p (a n)")[:, 0:96].rearrange("p (b n) -> p b n", n=32)
                mms(ps[0:1, 2, 0:32], [(cst[e64, C_EID:C_EID + 1], xoh[:, b, :]) for b in range(BLOCKS - 1)])
                mms(ps[0:1, 2, 32:64], [(cst[e64, C_COL + b:C_COL + b + 1], xoh[:, b, :]) for b in range(BLOCKS - 1)]).then_inc(sem(f"mm_list_{l}"), 1)

                def x_transposes(slot):
                    for b in range(2):
                        m = transposes(b, [xg[slot][:, (4 * b + c) * P:(4 * b + c + 1) * P] for c in range(4)])
                    return m

                def gate_up(par, slot):
                    wgu = esl[:, slot, 0:2, :].rearrange("p a (k n) -> p k a n", n=D_EXP)
                    return mms(ps[:, 2, :].rearrange("p (a n) -> p a n", a=2), [(xgT[:, par, k, :], wgu[:, k]) for k in range(KD)])

                def down(par, slot):
                    for n in range(2):
                        m = mms(ps[:, 4 + n, :], [(hgT[:, par, c, :], esl[:, slot, 2, c * D + n * NCH:c * D + (n + 1) * NCH]) for c in range(2)])
                    return m

                def do_xT(e, j, rounds, first=False):
                    pe.wait_ge(*stage(f"gath{j % 4}_{l}", rounds * 16))
                    if not first:
                        pe.wait_ge(*stage(f"ev_xa_{l}", e))
                        pe.wait_ge(*stage(f"ev_xv_{l}", e))
                    x_transposes(j % 4).then_inc(sem(f"mm_xT_{l}"), 1)

                def do_gu(e, j, loads, first=False):
                    pe.wait_ge(*stage(f"ev_xa_{l}", e + 1))
                    pe.wait_ge(*stage(f"ev_xv_{l}", e + 1))
                    pe.wait_ge(*stage(f"weights{j}_{l}", loads * 48))
                    if not first:
                        pe.wait_ge(*stage(f"hidden_{l}", e))
                    gate_up(j % 2, j).then_inc(sem(f"mm_gu_{l}"), 1)

                def do_down(e, j, first=False):
                    pe.wait_ge(*stage(f"hidden_{l}", e + 1))
                    if not first:
                        pe.wait_ge(*stage(f"ev_hT_{l}", e))
                    transposes(3, [hsg[:, j % 2, c * P:(c + 1) * P] for c in range(2)]).then_inc(sem(f"mm_hT_{l}"), 1)
                    pe.wait_ge(*stage(f"ev_hT_{l}", e + 1))
                    if not first:
                        pe.wait_ge(*stage(f"ev_ya_{l}", e))
                        pe.wait_ge(*stage(f"ev_yv_{l}", e))
                    down(j % 2, j).then_inc(sem(f"mm_down_{l}"), 1)

                def step(e, r, j):
                    do_gu(e, j, r + (2 if j == 2 else 1), first=isinstance(e, int) and e == 0)
                    if not (isinstance(e, int) and e == N_EXP - 1):
                        do_xT(e + 1, j + 1, r + ((j + 1) // 4 + 1))
                    if not (isinstance(e, int) and e == 0):
                        do_down(e - 1, (j + 3) % 4, first=isinstance(e, int) and e == 1)

                do_xT(0, 0, 1, first=True)
                for e in range(4):
                    step(e, 0, e)
                with pe.Fori(1, N_EXP // 4 - 1) as r:
                    for j in range(4):
                        step(r * 4 + j, r, j)
                for e in range(N_EXP - 4, N_EXP):
                    step(e, N_EXP // 4 - 1, e % 4)
                do_down(N_EXP - 1, 3)

                n = pe.value_load(xl[0:1, 64:65], min_val=0, max_val=max_extra(l))
                with pe.Fori(0, max_extra(l)) as i:
                    with pe.If(i < n):
                        xstep = sem(f"x_step_{l}")
                        pe.wait_ge(sem(f"x_gath_{l}"), i * 16 + 16)
                        pe.wait_ge(xstep, i * XSTEPS + (X0 + 1))
                        x_transposes(0).then_inc(xstep, 1)
                        pe.wait_ge(xstep, i * XSTEPS + (X0 + 3))
                        pe.wait_ge(sem(f"x_weights_{l}"), i * 48 + 48)
                        gate_up(0, 0).then_inc(xstep, 1)
                        pe.wait_ge(xstep, i * XSTEPS + (X0 + 6))
                        transposes(3, [hsg[:, 0, c * P:(c + 1) * P] for c in range(2)]).then_inc(xstep, 1)
                        pe.wait_ge(xstep, i * XSTEPS + (X0 + 8))
                        down(0, 0).then_inc(xstep, 1)

        @block.scalar
        def _(act):
            do = Steps(act, sem("act_order"))
            nc_a = nc.scalar
            act.wait_ge(sem("mm_cond"), 1)
            act.wait_ge(sem("x_loaded"), 32)
            do.run(nc_a.activation(cT[:, :], ps[:, 0, 0:16], ACT.Silu))
            nc_a.activation(cT[:, :], cT[:, :], ACT.Copy).then_inc(sem("cond_silu"), 1)
            act.sem_inc(sem("cond_silu"), 1)
            for l in range(DEPTH):
                nt = out_tiles[l]

                def end():
                    act.wait_ge(do.own, do.n.get(do.own.name, 0))
                    act.sem_inc(phase, 1)

                def ada(half):
                    kind = f"ada{half}"
                    act.wait_ge(phase, phase_start(l, kind)) if phase_start(l, kind) else None
                    if half == 0:
                        act.wait_ge(*stage(f"mm_ccol_{l}", 1))
                        do.run(nc_a.activation(ccol[:, :], ps[:, 6, 0:48], ACT.Copy))
                    for i in range(12):
                        v, s, n2 = i // 4, i // 2 % 2, i % 2
                        act.wait_ge(*stage(f"mm_bc_{kind}_{l}", i + 1))
                        do.run(nc_a.activation(bc[:, v, s, n2 * NCH:(n2 + 1) * NCH], ps[:, 2 + i % 4, :], ACT.Copy), sem(f"bc_{kind}_{l}"))
                    act.sem_inc(phase, 1)

                def rstd(src, n, waits, ready):
                    act.wait_ge(*waits)
                    do.run(nc_a.activation(stat[:, 2, 0:n], stat[:, 1, 0:n], ACT.Sqrt), ready)

                def norm(half, tiles):
                    kind = f"norm{half}"
                    act.wait_ge(phase, phase_start(l, kind))
                    for t in range(tiles):
                        do.run(nc_a.activation(junk[:, :], x[:, t, :], ACT.Square, accum_out=stat[:, 0, t:t + 1]), sem(f"sq_{kind}_{l}"))
                    rstd(None, tiles, stage(f"inv_{kind}_{l}", 1), sem(f"rstd_{kind}_{l}"))
                    for u in range(2 * tiles):
                        t, b = u // 2, u % 2
                        act.wait_ge(*stage(f"mm_{kind}_{l}", u + 1))
                        do.run(nc_a.activation(hT[:, 4 * b:4 * b + 4, t * P:(t + 1) * P],
                                               ps[:, u % 4, :].rearrange("p (k n) -> p k n", n=P), ACT.Copy), sem(f"ev_{kind}_{l}"))
                    act.sem_inc(phase, 1)

                ada(0)
                norm(0, TILES)

                act.wait_ge(phase, phase_start(l, "inproj"))
                act.wait_ge(*stage(f"xp_zero_{l}", 2))
                for ct in range(CONV_T + 1):
                    if ct < CONV_T:
                        act.wait_ge(*stage(f"mm_xbc_{l}", ct + 1))
                        if ct >= 2:
                            act.wait_ge(*stage(f"conv_{l}", ct - 1))
                        do.run(nc_a.activation(xp[ct % 2][:, :, 1:SEG + 1], ps[:, ct % 2, :].rearrange("p (s n) -> p s n", s=2), ACT.Copy),
                               sem(f"conv_in_{l}"))
                    if ct >= 1:
                        c = ct - 1
                        act.wait_ge(*stage(f"conv_{l}", c + 1))
                        if c >= 2 and c < 8:
                            act.wait_ge(*stage(f"mm_uT_{l}", c - 1))
                        dst = cu[:, c % 2, :] if c < 8 else bcc[:, c - 8, :]
                        do.run(nc_a.activation(dst, cacc[:, c % 2, :], ACT.Silu), sem(f"conv_u_{l}"))
                u = 0
                for kind, units in (("qkv", qkv_units(l)), ("z", [(n, t) for n in range(2) for t in range(nt)])):
                    for i, (n, t) in enumerate(units):
                        act.wait_ge(*stage(f"mm_{kind}_{l}", i + 1))
                        dst = (qk if kind == "qkv" else zs)[:, t, n * NCH:(n + 1) * NCH]
                        do.run(nc_a.activation(dst, ps[:, 5 + u % 3, :], ACT.Copy if kind == "qkv" else ACT.Silu), sem(f"ev_proj_{l}"))
                        u += 1
                act.sem_inc(phase, 1)

                act.wait_ge(phase, phase_start(l, "attn"))
                rstd(None, TILES * 10, stage(f"inv_qk_{l}", 1), sem(f"rstd_qk_{l}"))
                e = 0
                for t, ty in tr_units(l):
                    for part in range(2):
                        if part == 0 and not has_q(l, t):
                            continue
                        act.wait_ge(*stage(f"mm_qT_{l}", e + 1))
                        if part == 0:
                            ins = nc_a.activation(qT[:, ty, :, t * P:(t + 1) * P], ps[:, e % 4, :].rearrange("p (h n) -> p h n", n=P), ACT.Copy)
                        else:
                            ins = nc_a.activation(kT[:, ty, t * P:(t + 1) * P], ps[:, e % 4, 0:P], ACT.Copy)
                        do.run(ins, sem(f"ev_qT_{l}"))
                        e += 1
                units = attn_units(l)
                for i in range(len(units) + 1):
                    if i < len(units):
                        t = units[i][0]
                        n = (TILES if t < LAT_TILES else CTX_TILES) * P
                        act.wait_ge(*stage(f"negmax_{l}", i + 1))
                        if i >= 2:
                            act.wait_ge(*stage(f"mm_pT_{l}", i - 1))
                        col = i % 16
                        if i >= 16 and i % 8 == 0:
                            act.wait_ge(*stage(f"ev_o_{l}", i // 8 - 1))
                        do.run(nc_a.activation(pr[:, i % 2, 0:n], ps[:, i % 3, 0:n], ACT.Exp, bias=stat[:, 3, col:col + 1], scale=SCALE,
                                               accum_out=stat[:, 4, col:col + 1]), sem(f"prob_{l}"))
                        if i % 8 == 7 and units[i][1] == 1:
                            g8 = slice(col - 7, col + 1)
                            act.wait_ge(*stage(f"sinkarg_{l}", i // 16 + 1))
                            do.run(nc_a.activation(stat[:, 5, g8], stat[:, 5, g8], ACT.Exp), sem(f"sinkexp_{l}"))
                    if i >= 1:
                        j = i - 1
                        t = units[j][0]
                        n = (TILES if t < LAT_TILES else CTX_TILES) * P
                        act.wait_ge(*stage(f"mm_pT_{l}", j + 1))
                        if j >= 2:
                            act.wait_ge(*stage(f"mm_pv_{l}", j - 1))
                        do.run(nc_a.activation(pT[:, j % 2, 0:n], ps[:, 3 + j % 2, 0:n], ACT.Copy), sem(f"ev_pT_{l}"))
                for u in range(2 * nt):
                    t, ty = u // 2, u % 2
                    act.wait_ge(*stage(f"mm_oT_{l}", u + 1))
                    do.run(nc_a.activation(oT[:, 4 * ty:4 * ty + 4, t * P:(t + 1) * P], ps[:, 3 + u % 2, :].rearrange("p (k n) -> p k n", n=P), ACT.Copy),
                           sem(f"ev_oT_{l}"))
                act.sem_inc(phase, 1)

                act.wait_ge(phase, phase_start(l, "ssd"))
                do.run(nc_a.activation(alog[:, :], alog[:, :], ACT.Exp), sem(f"expA_{l}"))
                act.wait_ge(*stage(f"nabs_{l}", 1))
                do.run(nc_a.activation(dts[:, 7], dts[:, 7], ACT.Exp), sem(f"softexp_{l}"))
                act.wait_ge(*stage(f"onep_{l}", 1))
                do.run(nc_a.activation(dts[:, 3], dts[:, 8], ACT.Ln), sem(f"softln_{l}"))
                act.wait_ge(*stage(f"cum_{l}", 1))
                do.mark(nc_a.activation(dts[:, 4], dts[:, 2], ACT.Exp))
                do.mark(nc_a.activation(dts[:, 5], dts[:, 5], ACT.Exp))
                do.mark(nc_a.activation(dts[:, 6], dts[:, 3], ACT.Exp), sem(f"decays_{l}"))
                for q in range(2 * SG * nt):
                    act.wait_ge(*stage(f"diff_{l}", q + 1))
                    m3 = mt[:, q % 3]
                    do.run(nc_a.activation(m3, m3, ACT.Exp), sem(f"expd_{l}"))
                act.sem_inc(phase, 1)

                act.wait_ge(phase, phase_start(l, "gn"))
                for t in range(nt):
                    act.wait_ge(*stage(f"yz_{l}", t + 1))
                    for g in range(SG):
                        do.run(nc_a.activation(junk[:, 0:NCH], y[:, t, g * NCH:(g + 1) * NCH], ACT.Square,
                                               accum_out=stat[:, 0, 2 * t + g:2 * t + g + 1]), sem(f"sq_gn_{l}"))
                rstd(None, 2 * nt, stage(f"inv_gn_{l}", 1), sem(f"rstd_gn_{l}"))

                def evac_rows(name, dst):
                    for u in range(2 * nt):
                        t, b = u // 2, u % 2
                        act.wait_ge(*stage(f"mm_{name}_{l}", u + 1))
                        do.run(nc_a.activation(dst[:, 4 * b:4 * b + 4, t * P:(t + 1) * P],
                                               ps[:, 4 + u % 4, :].rearrange("p (k n) -> p k n", n=P), ACT.Copy), sem(f"ev_{name}_{l}"))

                evac_rows("gn", ysT)
                act.sem_inc(phase, 1)

                act.wait_ge(phase, phase_start(l, "merge"))
                for u in range(6 * nt):
                    act.wait_ge(*stage(f"mm_gate_{l}", u + 1))
                    if u >= 2:
                        act.wait_ge(*stage(f"gated_{l}", u - 1))
                    do.run(nc_a.activation(gs[:, u % 2, :], ps[:, u % 2, :], ACT.Sigmoid), sem(f"gate_{l}"))
                evac_rows("mg", mT)
                act.sem_inc(phase, 1)

                act.wait_ge(phase, phase_start(l, "out"))
                for u, (n, t) in enumerate([(n, t) for n in range(2) for t in range(nt)]):
                    act.wait_ge(*stage(f"mm_out_{l}", u + 1))
                    do.run(nc_a.activation(ml[:, t, n * NCH:(n + 1) * NCH], ps[:, u % 2, :], ACT.Copy), sem(f"ev_out_{l}"))

                def post(name, src):
                    for t in range(nt):
                        do.run(nc_a.activation(junk[:, :], src[:, t, :], ACT.Square, accum_out=stat[:, 0, t:t + 1]), sem(f"sq_{name}_{l}"))
                    rstd(None, nt, stage(f"inv_{name}_{l}", 1), sem(f"rstd_{name}_{l}"))
                    act.sem_inc(phase, 1)

                post("out", ml)
                ada(1)
                norm(1, nt)

                act.wait_ge(phase, phase_start(l, "router"))
                act.wait_ge(*stage(f"mm_router_{l}", 1))
                do.run(nc_a.activation(rtr[:, 0, 0:nt, :], ps[:, 0, 0:nt * N_EXP].rearrange("p (t n) -> p t n", n=N_EXP), ACT.Sigmoid), sem(f"scores_{l}"))
                act.sem_inc(phase, 1)

                act.wait_ge(phase, phase_start(l, "moe"))
                for t in range(nt):
                    b = t % 2
                    act.wait_ge(*stage(f"mm_sgu_{l}", t + 1))
                    do.run(nc_a.activation(hsg[:, b, :], ps[:, b, 0:D_EXP], ACT.Silu), sem(f"ssilu_{l}"))
                    act.wait_ge(*stage(f"mm_shT_{l}", t + 1))
                    do.run(nc_a.activation(hgT[:, b, :, :], ps[:, 2 + b, 0:2 * P].rearrange("p (c n) -> p c n", n=P), ACT.Copy), sem(f"ev_shT_{l}"))

                def ev_x(e, par):
                    act.wait_ge(*stage(f"mm_xT_{l}", e + 1))
                    nc_a.activation(xgT[:, par, 0:4, :], ps[:, 0, :].rearrange("p (k n) -> p k n", n=P), ACT.Copy).then_inc(sem(f"ev_xa_{l}"), 1)

                def hidden_out(e, j, scat):
                    act.wait_ge(*stage(f"mm_hT_{l}", e + 1))
                    nc_a.activation(hgT[:, j % 2, :, :], ps[:, 3, 0:2 * P].rearrange("p (c n) -> p c n", n=P), ACT.Copy).then_inc(sem(f"ev_hT_{l}"), 1)
                    act.wait_ge(*stage(f"mm_down_{l}", e + 1))
                    if scat is not None:
                        act.wait_ge(*stage(f"scat{j}_{l}", scat))
                    nc_a.activation(ysb[j][:, 0:NCH], ps[:, 4, :], ACT.Copy).then_inc(sem(f"ev_ya_{l}"), 1)

                def step(e, r, j):
                    act.wait_ge(*stage(f"mm_gu_{l}", e + 1))
                    nc_a.activation(hsg[:, j % 2, :], ps[:, 2, 0:D_EXP], ACT.Silu).then_inc(sem(f"silu_{l}"), 1)
                    static = isinstance(e, int)
                    if not (static and e == N_EXP - 1):
                        ev_x(e + 1, (j + 1) % 2)
                    if not (static and e == 0):
                        hidden_out(e - 1, (j + 3) % 4, None if static and e < 5 else r * 16 + 16 * ((j - 5) // 4 + 1))

                ev_x(0, 0)
                for e in range(5):
                    step(e, 0, e)
                with act.Fori(1, N_EXP // 4 - 2) as r:
                    for j in range(1, 5):
                        step(r * 4 + j, r, j)
                for e in range(N_EXP - 7, N_EXP):
                    step(e, e // 4, e % 4)
                hidden_out(N_EXP - 1, 3, 16 * ((N_EXP - 5) // 4 + 1))

                act.wait_ge(*stage(f"list_ready_{l}", 1))
                n = act.value_load(xl[0:1, 64:65], min_val=0, max_val=max_extra(l))
                with act.Fori(0, max_extra(l)) as i:
                    with act.If(i < n):
                        xstep = sem(f"x_step_{l}")
                        act.wait_ge(xstep, i * XSTEPS + (X0 + 2))
                        nc_a.activation(xgT[:, 0, :, :], ps[:, 0:2, :].rearrange("p a (k n) -> p (a k) n", n=P), ACT.Copy).then_inc(xstep, 1)
                        act.wait_ge(xstep, i * XSTEPS + (X0 + 4))
                        nc_a.activation(hsg[:, 0, :], ps[:, 2, 0:D_EXP], ACT.Silu).then_inc(xstep, 1)
                        act.wait_ge(xstep, i * XSTEPS + (X0 + 7))
                        nc_a.activation(hgT[:, 0, :, :], ps[:, 3, 0:2 * P].rearrange("p (c n) -> p c n", n=P), ACT.Copy).then_inc(xstep, 1)
                        act.wait_ge(xstep, i * XSTEPS + (X0 + 9))
                        nc_a.activation(ysb[0][:, :], ps[:, 4:6, :].rearrange("p a n -> p (a n)"), ACT.Copy).then_inc(xstep, 1)
                act.wait_ge(*stage(f"ev_ya_{l}", N_EXP))
                act.sem_inc(phase, 1)

                act.wait_ge(phase, phase_start(l, "post"))
                post("post", acc)

        @block.vector
        def _(dve):
            do = Steps(dve, sem("dve_order"))
            v = nc.vector
            dve.wait_ge(sem("x_loaded"), 32)
            for l in range(DEPTH):
                nt = out_tiles[l]

                def end():
                    dve.sem_inc(phase, 1)

                def ada(half):
                    kind = f"ada{half}"
                    dve.wait_ge(phase, phase_start(l, kind)) if phase_start(l, kind) else None
                    dve.wait_ge(param, params_at(l, half))
                    if half == 0:
                        do.run(v.tensor_scalar(nsink[:, :], nsink[:, :], -1.0, None, ALU.mult))
                    for n in range(6):
                        dve.wait_ge(*stage(f"mm_{kind}_{l}", n + 1))
                        o = modrow[:, n // 2, (n % 2) * NCH:(n % 2 + 1) * NCH]
                        do.run(v.tensor_tensor(o, ps[0:2, n % 2, :], bada[:, n * NCH:(n + 1) * NCH], ALU.add), sem(f"ev_{kind}_{l}"))
                    do.run(v.scalar_tensor_tensor(modrow[:, 1, :], modrow[:, 1, :], 1.0, gnorm[:, 0, :], ALU.add, ALU.mult), sem(f"modrow_{kind}_{l}"))
                    do.run(v.tensor_tensor(modrow[:, 2, :], modrow[:, 2, :], gnorm[:, 1, :], ALU.mult), sem(f"modrow_{kind}_{l}"))
                    end()

                def inverse_ms(n, width, ready):
                    do.run(v.tensor_scalar(stat[:, 0, 0:n], stat[:, 0, 0:n], 1.0 / width, EPS, ALU.mult, ALU.add))
                    do.run(v.reciprocal(stat[:, 1, 0:n], stat[:, 0, 0:n]), ready)

                def norm(half, tiles):
                    kind = f"norm{half}"
                    dve.wait_ge(phase, phase_start(l, kind))
                    dve.wait_ge(*stage(f"sq_{kind}_{l}", tiles))
                    inverse_ms(tiles, D, sem(f"inv_{kind}_{l}"))
                    dve.wait_ge(*stage(f"rstd_{kind}_{l}", 1))
                    for t in range(tiles):
                        s = 0 if t < LAT_TILES else 1
                        if t >= 2:
                            dve.wait_ge(*stage(f"mm_{kind}_{l}", 2 * (t - 1)))
                            if half:
                                dve.wait_ge(*stage(f"h_written{t % 2}_{l}", 16 * (t // 2)))
                        do.run(v.scalar_tensor_tensor(hn[:, t % 2, :], x[:, t, :], stat[:, 2, t:t + 1], bc[:, 1, s, :], ALU.mult, ALU.mult))
                        do.run(v.tensor_tensor(hn[:, t % 2, :], hn[:, t % 2, :], bc[:, 0, s, :], ALU.add), sem(f"hn_{kind}_{l}"))
                    end()

                ada(0)
                norm(0, TILES)

                dve.wait_ge(phase, phase_start(l, "inproj"))
                for i in range(2):
                    do.run(v.memset(xp[i][:, :, :], 0.0), sem(f"xp_zero_{l}"))

                def evac_uT(ct):
                    dve.wait_ge(*stage(f"mm_uT_{l}", ct + 1))
                    dst = xs[:, :, ct * P:(ct + 1) * P] if ct < 8 else btok[:, :, (ct - 8) * P:(ct - 7) * P]
                    do.run(v.tensor_copy(dst, ps[:, 2 + ct % 2, :].rearrange("p (t n) -> p t n", n=P)), sem(f"ev_uT_{l}"))

                for ct in range(CONV_T):
                    dve.wait_ge(*stage(f"conv_in_{l}", ct + 1))
                    if ct >= 2:
                        dve.wait_ge(*stage(f"conv_u_{l}", ct - 1))
                    src = xp[ct % 2]
                    o = cacc[:, ct % 2, :].rearrange("p (s n) -> p s n", s=2)
                    wcol = lambda w: ccol[:, w * CONV_T + ct:w * CONV_T + ct + 1]
                    do.run(v.tensor_scalar(o, src[:, :, 1:SEG + 1], wcol(1), wcol(3), ALU.mult, ALU.add))
                    do.run(v.scalar_tensor_tensor(o, src[:, :, 0:SEG], wcol(0), o, ALU.mult, ALU.add))
                    do.run(v.scalar_tensor_tensor(o, src[:, :, 2:SEG + 2], wcol(2), o, ALU.mult, ALU.add), sem(f"conv_{l}"))
                    if ct >= 2:
                        evac_uT(ct - 2)
                dve.wait_ge(*stage(f"mm_dt_{l}", 1))
                for d in range(2):
                    do.run(v.tensor_tensor(dts[:, 0, d], ps[:, 4, 0:TILES * 32].rearrange("p (t d h) -> p d t h", d=2, h=SH)[:, d],
                                           dtb[:, d * SH:(d + 1) * SH].unsqueeze(1).to_broadcast([P, TILES, SH]), ALU.add))
                end()

                dve.wait_ge(phase, phase_start(l, "attn"))
                for t in range(TILES):
                    h0 = 0 if has_q(l, t) else HEADS
                    w = (10 - h0) * HD
                    src = qk[:, t, h0 * HD:640]
                    do.run(v.tensor_tensor(rt[:, 0:w], src, src, ALU.mult))
                    do.run(v.tensor_reduce(stat[:, 0, t * 10 + h0:(t + 1) * 10], rt[:, 0:w].rearrange("p (h d) -> p h d", d=HD), AX.X, ALU.add))
                    if h0:
                        do.run(v.memset(stat[:, 0, t * 10:t * 10 + h0], 1.0))
                inverse_ms(TILES * 10, HD, sem(f"inv_qk_{l}"))
                dve.wait_ge(*stage(f"rstd_qk_{l}", 1))
                dve.wait_ge(sem("gqk_loaded"), 16 * (HEADS + KV) * (l + 1))
                for t, ty in tr_units(l):
                    h0 = 0 if has_q(l, t) else HEADS
                    nh = 10 - h0
                    cur = qk[:, t, ty * 768 + h0 * HD:ty * 768 + 640]
                    heads = cur.rearrange("p (h d) -> p h d", d=HD)
                    if ty == 0:
                        r = stat[:, 2, t * 10 + h0:(t + 1) * 10].unsqueeze(2).to_broadcast([P, nh, HD])
                        do.run(v.tensor_tensor(heads, heads, r, ALU.mult))
                        do.run(v.tensor_tensor(cur, cur, gqk[:, h0 * HD:640], ALU.mult))
                    if t < LAT_TILES:
                        cosb = cst[:, C_COS + t * HD:C_COS + (t + 1) * HD].unsqueeze(1).to_broadcast([P, nh, HD])
                        sv = cst[:, C_SIN + t * HD:C_SIN + (t + 1) * HD].rearrange("p (x f j) -> p x f j", x=2, f=2)
                        hv = cur.rearrange("p (h x f j) -> p h x f j", x=2, f=2, j=16)
                        mv = rt[:, :].rearrange("p (h x f j) -> p h x f j", x=2, f=2, j=16)
                        for f in range(2):
                            for ax in range(2):
                                do.mark(v.tensor_tensor(mv[:, :, ax, f, :], hv[:, :, ax, 1 - f, :],
                                                        sv[:, ax, f, :].unsqueeze(1).to_broadcast([P, nh, 16]), ALU.mult))
                        dve.wait_ge(do.own, do.n[do.own.name])
                        do.run(v.tensor_tensor(heads, heads, cosb, ALU.mult))
                    u = tr_units(l).index((t, ty))
                    if u >= 2:
                        dve.wait_ge(*stage(f"mm_qT_{l}", sum(1 + has_q(l, tt) for tt, _ in tr_units(l)[:u - 1])))
                    if has_q(l, t):
                        qd = rq[:, u % 2, 0:512].rearrange("p (h g d) -> p g h d", g=KV, d=HD)
                        q4 = lambda z: z.rearrange("p (g h d) -> p g h d", g=KV, d=HD)
                        qs = q4(cur[:, 0:512])
                        do.mark(v.tensor_tensor(qd, qs, q4(rt[:, 0:512]), ALU.add) if t < LAT_TILES else v.tensor_copy(qd, qs))
                    ks, kd = cur[:, nh * HD - P:nh * HD], rq[:, u % 2, 512:640]
                    do.run(v.tensor_tensor(kd, ks, rt[:, 512:640], ALU.add) if t < LAT_TILES else v.tensor_copy(kd, ks), sem(f"roped_{l}"))

                units = attn_units(l)

                def finish_group(grp):
                    t, ty = grp // 2, grp % 2
                    c0 = (grp % 2) * 8
                    dve.wait_ge(*stage(f"mm_pv_{l}", 8 * (grp + 1)))
                    den = stat[:, 4, c0:c0 + 8]
                    if ty == 1:
                        dve.wait_ge(*stage(f"sinkexp_{l}", t + 1))
                        do.run(v.tensor_tensor(den, den, stat[:, 5, c0:c0 + 8], ALU.add))
                    do.run(v.reciprocal(stat[:, 6, 0:8], den))
                    o = qk[:, t, ty * 768:ty * 768 + 512].rearrange("p (h d) -> p h d", d=HD)
                    do.run(v.tensor_tensor(o, ps[:, 5 + grp % 2, :].rearrange("p (h d) -> p h d", d=HD),
                                           stat[:, 6, 0:8].unsqueeze(2).to_broadcast([P, HEADS, HD]), ALU.mult), sem(f"ev_o_{l}"))

                for i, (t, ty, g, h) in enumerate(units):
                    n = (TILES if t < LAT_TILES else CTX_TILES) * P
                    col = i % 16
                    dve.wait_ge(*stage(f"mm_score_{l}", i + 1))
                    do.run(v.tensor_reduce(stat[:, 7, col:col + 1], ps[:, i % 3, 0:n], AX.X, ALU.max, negate=True))
                    if ty == 0:
                        ins = v.tensor_scalar(stat[:, 3, col:col + 1], stat[:, 7, col:col + 1], SCALE, None, ALU.mult)
                    else:
                        ins = v.tensor_scalar(stat[:, 3, col:col + 1], stat[:, 7, col:col + 1], SCALE, nsink[:, i % 8:i % 8 + 1], ALU.mult, ALU.min)
                    do.run(ins, sem(f"negmax_{l}"))
                    if i % 8 == 7 and ty == 1:
                        do.run(v.tensor_tensor(stat[:, 5, 8:16], stat[:, 3, 8:16], nsink[:, :], ALU.subtract), sem(f"sinkarg_{l}"))
                    if i >= 3 and (i - 3) % 8 == 7:
                        finish_group((i - 3) // 8)
                finish_group(len(units) // 8 - 1)
                end()

                dve.wait_ge(phase, phase_start(l, "ssd"))
                dt, aa, cum, tot, ein, eend, edec = (dts[:, i] for i in range(7))
                flat = lambda z: z.rearrange("p d t h -> p (d t h)")
                do.run(v.scalar_tensor_tensor(flat(dts[:, 7]), flat(dt), -1.0, flat(dt), ALU.mult, ALU.min), sem(f"nabs_{l}"))
                dve.wait_ge(*stage(f"softexp_{l}", 1))
                do.run(v.tensor_scalar(flat(dts[:, 8]), flat(dts[:, 7]), 1.0, None, ALU.add), sem(f"onep_{l}"))
                do.run(v.scalar_tensor_tensor(flat(dts[:, 4]), flat(dts[:, 8]), 1.0, flat(dts[:, 7]), ALU.subtract, ALU.subtract))
                do.run(v.reciprocal(flat(dts[:, 5]), flat(dts[:, 8])))
                do.run(v.scalar_tensor_tensor(flat(dts[:, 4]), flat(dts[:, 4]), -1.0, flat(dts[:, 5]), ALU.mult, ALU.mult))
                do.run(v.scalar_tensor_tensor(flat(dt), flat(dt), 0.0, flat(dts[:, 4]), ALU.max, ALU.add))
                dve.wait_ge(*stage(f"softln_{l}", 1))
                do.run(v.tensor_tensor(flat(dt), flat(dt), flat(tot), ALU.add))
                dve.wait_ge(*stage(f"expA_{l}", 1))
                for d in range(2):
                    do.run(v.tensor_tensor(aa[:, d], dt[:, d], alog[:, d * SH:(d + 1) * SH].unsqueeze(1).to_broadcast([P, TILES, SH]), ALU.mult))
                do.run(v.tensor_scalar(flat(aa), flat(aa), -1.0, None, ALU.mult), sem(f"a_ready_{l}"))
                dve.wait_ge(*stage(f"mm_cum_{l}", 1))
                do.run(v.tensor_copy(dts[:, 2:4].rearrange("p a d t h -> p (a d t h)"), ps[:, 7, 0:256]))
                do.run(v.tensor_tensor(flat(eend), flat(tot), flat(cum), ALU.subtract), sem(f"cum_{l}"))
                dve.wait_ge(*stage(f"decays_{l}", 1))
                do.run(v.tensor_tensor(flat(eend), flat(eend), flat(dt), ALU.mult))
                perhead = lambda z: z.rearrange("p (h d) -> p h d", d=HD)
                hb = lambda z: z.unsqueeze(2).to_broadcast([P, SH, HD])
                for t in range(nt):
                    do.run(v.tensor_tensor(perhead(y[:, t, :]), perhead(xs[:, t, :]), hb(dsk[:, :]), ALU.mult))
                ny = ns = 0
                for s, d, t in scan_steps(l):
                    if s > 0 and t < nt:
                        dve.wait_ge(*stage(f"mm_yoff_{l}", ny + 1))
                        bank = 2 * (ny % 2)
                        yo = mt[:, 0].rearrange("p a n -> p (a n)")
                        do.run(v.tensor_tensor(perhead(yo), ps[:, bank:bank + 2, :].rearrange("p a (h d) -> p (a h) d", d=HD), hb(ein[:, d, t, :]), ALU.mult),
                               sem(f"ev_yoff_{l}"))
                        do.run(v.tensor_tensor(y[:, t, :], y[:, t, :], yo, ALU.add))
                        ny += 1
                    if s < 3:
                        if ns:
                            dve.wait_ge(*stage(f"mm_state_{l}", ns))
                        do.run(v.tensor_tensor(perhead(tmp[:, :]), perhead(xs[:, t, :]), hb(eend[:, d, t, :]), ALU.mult), sem(f"xw_{l}"))
                        dve.wait_ge(*stage(f"mm_state_{l}", ns + 1))
                        add = ps[:, 4:6, :].rearrange("p a n -> p (a n)")
                        if s == 0:
                            do.run(v.tensor_copy(st[:, d, :], add), sem(f"state_{l}"))
                        else:
                            if ny and t < nt:
                                dve.wait_ge(*stage(f"mm_yoff_{l}", ny))
                            do.run(v.tensor_tensor(perhead(st[:, d, :]), perhead(st[:, d, :]), hb(edec[:, d, t, :]), ALU.mult))
                            do.run(v.tensor_tensor(st[:, d, :], st[:, d, :], add, ALU.add), sem(f"state_{l}"))
                        ns += 1
                do.run(v.memset(stat[:, 6, 0:1], 0.0), sem(f"scan_done_{l}"))

                def decayed(q):
                    u, d = q // 2, q % 2
                    t, g = u // SG, u % SG
                    dve.wait_ge(*stage(f"expd_{l}", q + 1))
                    for h in range(8):
                        ins = v.scalar_tensor_tensor(mt[:, q % 3, h, :], mt[:, q % 3, h, :], dt[:, d, t, g * 8 + h:g * 8 + h + 1], cbm[:, d, :], ALU.mult, ALU.mult)
                        do.mark(ins, sem(f"m_ready_{l}")) if h == 7 else None

                def add_y(u):
                    t, g = u // SG, u % SG
                    dve.wait_ge(*stage(f"mm_y_{l}", u + 1))
                    yy = y[:, t, g * NCH:(g + 1) * NCH]
                    do.run(v.tensor_tensor(yy, yy, ps[:, 5 + u % 2, :], ALU.add), sem(f"ev_y_{l}"))

                NQ = 2 * SG * nt
                for q in range(NQ + 1):
                    if q < NQ:
                        u, d = q // 2, q % 2
                        t, g = u // SG, u % SG
                        dve.wait_ge(*stage(f"mm_r_{l}", q + 1))
                        if q >= 3:
                            dve.wait_ge(*stage(f"mm_y_{l}", (q - 3) // 2 + 1))
                        for h in range(8):
                            ins = v.tensor_scalar(mt[:, q % 3, h, :], ps[:, 1 + 2 * (q % 2) + h // 4, (h % 4) * P:(h % 4 + 1) * P],
                                                  cum[:, d, t, g * 8 + h:g * 8 + h + 1], 0.0, ALU.subtract, ALU.min)
                        do.mark(ins, sem(f"diff_{l}"))
                    if q >= 1:
                        if (q - 1) % 2 == 0:
                            pu = (q - 1) // 2
                            dve.wait_ge(*stage(f"mm_cb_{l}", pu + 1))
                            for dd in range(2):
                                do.run(v.tensor_tensor(cbm[:, dd, :], ps[:, 0, 0:P], tri[dd], ALU.mult), sem(f"cbm_{l}"))
                        decayed(q - 1)
                        if (q - 1) % 2 == 1:
                            add_y((q - 1) // 2)
                end()

                dve.wait_ge(phase, phase_start(l, "gn"))
                for t in range(nt):
                    do.run(v.tensor_tensor(y[:, t, :], y[:, t, :], zs[:, t, :], ALU.mult), sem(f"yz_{l}"))
                dve.wait_ge(*stage(f"sq_gn_{l}", SG * nt))
                inverse_ms(SG * nt, NCH, sem(f"inv_gn_{l}"))
                dve.wait_ge(*stage(f"rstd_gn_{l}", 1))
                for t in range(nt):
                    for g in range(SG):
                        yy = y[:, t, g * NCH:(g + 1) * NCH]
                        ins = v.scalar_tensor_tensor(yy, yy, stat[:, 2, 2 * t + g:2 * t + g + 1], nw[:, g * NCH:(g + 1) * NCH], ALU.mult, ALU.mult)
                    do.run(ins, sem(f"gn_rows_{l}"))
                end()

                dve.wait_ge(phase, phase_start(l, "merge"))
                for u in range(6 * nt):
                    bn, t = u // nt, u % nt
                    b, n = bn // 2, bn % 2
                    dve.wait_ge(*stage(f"gate_{l}", u + 1))
                    dve.wait_ge(*stage(f"mm_br_{l}", u + 1))
                    dst = acc[:, t, n * NCH:(n + 1) * NCH]
                    if b == 0:
                        do.run(v.tensor_tensor(dst, ps[:, 2 + u % 2, :], gs[:, u % 2, :], ALU.mult), sem(f"gated_{l}"))
                    else:
                        do.run(v.tensor_tensor(tmp[:, 0:NCH], ps[:, 2 + u % 2, :], gs[:, u % 2, :], ALU.mult), sem(f"gated_{l}"))
                        do.run(v.tensor_tensor(dst, dst, tmp[:, 0:NCH], ALU.add), sem(f"mg_rows_{l}") if bn == 5 else None)
                end()

                def post(name, src):
                    dve.wait_ge(phase, phase_start(l, name))
                    dve.wait_ge(*stage(f"sq_{name}_{l}", nt))
                    inverse_ms(nt, D, sem(f"inv_{name}_{l}"))
                    dve.wait_ge(*stage(f"rstd_{name}_{l}", 1))
                    for t in range(nt):
                        s = 0 if t < LAT_TILES else 1
                        do.run(v.scalar_tensor_tensor(tmp[:, :], src[:, t, :], stat[:, 2, t:t + 1], bc[:, 2, s, :], ALU.mult, ALU.mult))
                        do.run(v.tensor_tensor(x[:, t, :], x[:, t, :], tmp[:, :], ALU.add))
                    end()

                post("out", ml)
                ada(1)
                norm(1, nt)

                dve.wait_ge(phase, phase_start(l, "router"))
                do.run(v.memset(nor[:, :], NOROW), sem(f"norow_{l}"))
                dve.wait_ge(*stage(f"scores_{l}", 1))
                for t in range(nt):
                    R = lambda i: rtr[:, i, t, :]
                    do.run(v.tensor_tensor(R(1), R(0), brt[:, :], ALU.add))
                    for g in range(8):
                        do.mark(v.max(R(2)[:, g * 8:(g + 1) * 8], R(1)[:, g * 8:(g + 1) * 8]))
                    dve.wait_ge(do.own, do.n[do.own.name])
                    top2 = R(2).rearrange("p (g e) -> p g e", e=8)
                    gsum = R(3)[:, 0:8]
                    do.run(v.tensor_tensor(gsum.unsqueeze(2), top2[:, :, 0:1], top2[:, :, 1:2], ALU.add))
                    mine = gsum.unsqueeze(2).to_broadcast([P, 8, 8])
                    other = gsum.unsqueeze(1).to_broadcast([P, 8, 8])
                    g88 = lambda i: R(i).rearrange("p (g e) -> p g e", e=8)
                    do.run(v.tensor_tensor(g88(4), other, mine, ALU.is_equal))
                    do.run(v.tensor_tensor(R(4), R(4), cst[:, C_TRI8:C_TRI8 + 64], ALU.mult))
                    do.run(v.tensor_tensor(g88(5), other, mine, ALU.is_gt))
                    do.run(v.tensor_tensor(R(5), R(5), R(4), ALU.add))
                    do.run(v.tensor_reduce(R(3)[:, 8:16], g88(5), AX.X, ALU.add))
                    do.run(v.tensor_scalar(R(3)[:, 16:24], R(3)[:, 8:16], 3.5, None, ALU.is_lt))
                    gm = R(3)[:, 16:24].unsqueeze(2).to_broadcast([P, 8, 8])
                    do.run(v.tensor_tensor(g88(6), g88(1), gm, ALU.mult))
                    do.run(v.tensor_scalar(R(3)[:, 24:32], R(3)[:, 16:24], 1.0, -NEG, ALU.subtract, ALU.mult))
                    do.run(v.tensor_tensor(g88(6), g88(6), R(3)[:, 24:32].unsqueeze(2).to_broadcast([P, 8, 8]), ALU.add))
                    do.run(v.max(R(7)[:, 0:8], R(6)))
                    do.run(v.max_index(eiu[:, t, :], R(7)[:, 0:8], R(6)))
                    do.run(v.tensor_copy(eif[:, t, :], eiu[:, t, :]))
                    do.run(v.match_replace(R(8), R(7)[:, 0:8], R(6), 3 * NEG))
                    do.run(v.tensor_tensor(R(8), R(8), R(6), ALU.not_equal))
                    do.run(v.tensor_tensor(R(9), R(8), R(0), ALU.mult))
                    do.run(v.tensor_reduce(R(7)[:, 8:9], R(9), AX.X, ALU.add))
                    do.run(v.reciprocal(R(7)[:, 9:10], R(7)[:, 8:9]))
                    do.run(v.tensor_scalar(R(10), R(9), R(7)[:, 9:10], ROUTED_SCALE, ALU.mult, ALU.mult))
                do.run(v.memset(stat[:, 6, 0:1], 0.0), sem(f"masks_{l}"))
                dve.wait_ge(*stage(f"mm_rank_{l}", 1))
                for t in range(nt):
                    over_e = lambda z: z.unsqueeze(1).to_broadcast([P, TOP_K, N_EXP])
                    do.run(v.tensor_tensor(oneh[:, :, :], over_e(cst[:, C_IOTA:C_IOTA + N_EXP]),
                                           eif[:, t, :].unsqueeze(2).to_broadcast([P, TOP_K, N_EXP]), ALU.is_equal))
                    do.run(v.tensor_tensor(onet[:, :, :], oneh[:, :, :], over_e(ps[:, 1, t * N_EXP:(t + 1) * N_EXP]), ALU.mult))
                    do.run(v.tensor_reduce(rnk[:, t, :], onet[:, :, :], AX.X, ALU.add))
                    do.run(v.tensor_tensor(onet[:, :, :], oneh[:, :, :], over_e(rtr[:, 10, t, :]), ALU.mult))
                    do.run(v.tensor_reduce(wk[:, t, :], onet[:, :, :], AX.X, ALU.add))
                    do.run(v.scalar_tensor_tensor(rnk[:, t, :], eif[:, t, :], float(CAP), rnk[:, t, :], ALU.mult, ALU.add))
                    do.run(v.tensor_scalar(dst_i[:, t, :], rnk[:, t, :], -1.0, None, ALU.add))
                e64 = slice(0, N_EXP)
                do.run(v.tensor_copy(stat[e64, 1, 0:1], ps[e64, 2, 0:1]))
                do.run(v.tensor_tensor(stat[e64, 0, 0:3], stat[e64, 1, 0:1].to_broadcast([N_EXP, 3]), cst[e64, C_THR:C_THR + 3], ALU.is_gt))
                for i in range(2):
                    dve.wait_ge(*stage(f"h_written{i}_{l}", 16 * nt // 2))
                for i in range(EXP_SLOTS):
                    do.run(v.memset(xg[i][:, :], 0.0), sem(f"dest_{l}"))
                end()

                dve.wait_ge(phase, phase_start(l, "moe"))
                for t in range(nt):
                    b = t % 2
                    dve.wait_ge(*stage(f"ssilu_{l}", t + 1))
                    do.run(v.tensor_tensor(hsg[:, b, :], hsg[:, b, :], ps[:, b, D_EXP:2 * D_EXP], ALU.mult), sem(f"shid_{l}"))
                    dve.wait_ge(*stage(f"mm_sdown_{l}", t + 1))
                    do.run(v.tensor_copy(acc[:, t, :], ps[:, 4 + 2 * b:6 + 2 * b, :].rearrange("p a n -> p (a n)")), sem(f"ev_sy_{l}"))

                dve.wait_ge(*stage(f"mm_tab_{l}", 1))
                do.run(v.tensor_copy(si[:, :], ps[:, 0, 0:BLOCKS * N_EXP]))
                do.run(v.tensor_single_scalar(gi[:, :], si[:, :], 3, ALU.arith_shift_right), sem(f"flags_{l}"))

                def stage_gather(e, slot):
                    v.tensor_copy(gstg[:, slot:slot + 1], gi[:, bass.ds(e, 1)]).then_inc(sem(f"staged_{l}"), 1)

                for e in range(EXP_SLOTS):
                    stage_gather(e, e)
                dve.wait_ge(*stage(f"mm_pos_{l}", 1))
                do.run(v.tensor_copy(stat[e64, 1, 0:6], ps[e64, 1, 0:6]))
                do.run(v.tensor_tensor(stat[e64, 1, 1:3], stat[e64, 1, 1:3], stat[e64, 1, 3:4].to_broadcast([N_EXP, 2]), ALU.add))
                do.run(v.tensor_tensor(stat[e64, 1, 2:3], stat[e64, 1, 2:3], stat[e64, 1, 4:5], ALU.add))
                do.run(v.tensor_tensor(stat[e64, 1, 0:3], stat[e64, 1, 0:3], stat[e64, 0, 0:3], ALU.mult))
                xoh = stat[e64, 4:6, :].rearrange("p a n -> p (a n)")
                for b in range(BLOCKS - 1):
                    do.run(v.tensor_scalar(xoh[:, b * 32:(b + 1) * 32], cst[e64, C_IOTA + 1:C_IOTA + 33], stat[e64, 1, b:b + 1], None, ALU.is_equal))
                do.run(v.tensor_reduce(stat[e64, 2, 0:1], stat[e64, 1, 3:6], AX.X, ALU.add), sem(f"places_{l}"))
                dve.wait_ge(*stage(f"mm_list_{l}", 1))
                do.run(v.tensor_copy(xl[0:1, 0:64], ps[0:1, 2, 0:64]))
                dve.sem_inc(sem(f"x_step_{l}"), X0)
                do.run(v.tensor_copy(xl[0:1, 64:65], stat[0:1, 2, 0:1]), sem(f"list_ready_{l}"))

                def ev_x(e, par):
                    dve.wait_ge(*stage(f"mm_xT_{l}", e + 1))
                    v.tensor_copy(xgT[:, par, 4:8, :], ps[:, 1, :].rearrange("p (k n) -> p k n", n=P)).then_inc(sem(f"ev_xv_{l}"), 1)

                def ev_y(e, j, scat):
                    dve.wait_ge(*stage(f"mm_down_{l}", e + 1))
                    if scat is not None:
                        dve.wait_ge(*stage(f"scat{j}_{l}", scat))
                    v.tensor_copy(sstg[:, j:j + 1], si[:, bass.ds(e, 1)])
                    v.tensor_copy(ysb[j][:, NCH:], ps[:, 5, :]).then_inc(sem(f"ev_yv_{l}"), 1)

                def step(e, r, j):
                    dve.wait_ge(*stage(f"silu_{l}", e + 1))
                    v.tensor_tensor(hsg[:, j % 2, :], hsg[:, j % 2, :], ps[:, 2, D_EXP:2 * D_EXP], ALU.mult).then_inc(sem(f"hidden_{l}"), 1)
                    static = isinstance(e, int)
                    if not (static and e == N_EXP - 1):
                        ev_x(e + 1, (j + 1) % 2)
                    if not (static and e == 0):
                        ev_y(e - 1, (j + 3) % 4, None if static and e < 5 else r * 16 + 16 * ((j - 5) // 4 + 1))
                    if not (static and e >= N_EXP - 4):
                        stage_gather(e + EXP_SLOTS, j % 4)

                ev_x(0, 0)
                for e in range(5):
                    step(e, 0, e)
                with dve.Fori(1, N_EXP // 4 - 2) as r:
                    for j in range(1, 5):
                        step(r * 4 + j, r, j)
                for e in range(N_EXP - 7, N_EXP):
                    step(e, e // 4, e % 4)
                ev_y(N_EXP - 1, 3, 16 * ((N_EXP - 5) // 4 + 1))

                for i in range(EXP_SLOTS):
                    dve.wait_ge(*stage(f"scat{i}_{l}", 16 * N_EXP // EXP_SLOTS))
                n = dve.value_load(xl[0:1, 64:65], min_val=0, max_val=max_extra(l))
                with dve.Fori(0, max_extra(l)) as i:
                    with dve.If(i < n):
                        xstep = sem(f"x_step_{l}")
                        col = dve.value_load(xl[0:1, bass.ds(i + 32, 1)], min_val=0, max_val=BLOCKS * N_EXP - 1)
                        dve.wait_ge(xstep, i * XSTEPS + 2)
                        v.tensor_copy(gstg[:, 0:1], gi[:, bass.ds(col, 1)])
                        v.tensor_copy(sstg[:, 0:1], si[:, bass.ds(col, 1)]).then_inc(xstep, 1)
                        dve.wait_ge(xstep, i * XSTEPS + (X0 + 5))
                        v.tensor_tensor(hsg[:, 0, :], hsg[:, 0, :], ps[:, 2, D_EXP:2 * D_EXP], ALU.mult).then_inc(xstep, 1)

                for u in range(nt * 4):
                    t, kp = u // 4, u % 4
                    dve.wait_ge(*stage(f"comb{kp}_{l}", 16 * (t + 1)))
                    for i in range(2):
                        ins = v.scalar_tensor_tensor(acc[:, t, :], comb[:, kp, i, :], wk[:, t, 2 * kp + i:2 * kp + i + 1], acc[:, t, :], ALU.mult, ALU.add)
                        do.run(ins, sem(f"combined_{l}") if i == 1 else None)
                end()
                post("post", acc)


SHARED = {"squares_summed": (("sq_gn", (2 * TILES, 2 * LAT_TILES)), ("sq_out", (TILES, LAT_TILES)), ("sq_post", (TILES, LAT_TILES))),
          "rstd_found": tuple((f"rstd_{n}", (1, 1)) for n in ("qk", "gn", "out", "post")),
          "inv_found": tuple((f"inv_{n}", (1, 1)) for n in ("qk", "gn", "out", "post"))}

BEFORE = {'x_loaded': 32,
 'h_written0': 32,
 'h_written1': 32,
 'tab_cleared': 16,
 'tab_written': 512,
 'tab_read': 16,
 'comb0': 64,
 'comb1': 64,
 'comb2': 64,
 'comb3': 64,
 'mm_ccol': 1,
 'mm_ada': 12,
 'mm_bc_ada': 24,
 'mm_norm': 16,
 'mm_xbc': 12,
 'mm_uT': 10,
 'mm_dt': 1,
 'mm_qkv': 12,
 'mm_z': 8,
 'mm_qT': 16,
 'mm_score': 64,
 'mm_pT': 64,
 'mm_pv': 64,
 'mm_oT': 8,
 'mm_cum': 1,
 'mm_state': 6,
 'mm_yoff': 6,
 'mm_cb': 8,
 'mm_r': 16,
 'mm_y': 8,
 'mm_gn': 8,
 'mm_gate': 24,
 'mm_br': 24,
 'mm_mg': 8,
 'mm_out': 8,
 'mm_router': 1,
 'mm_rank': 1,
 'mm_sgu': 4,
 'mm_shT': 4,
 'mm_sdown': 4,
 'mm_tab': 1,
 'mm_pos': 1,
 'mm_list': 1,
 'bc_ada': 24,
 'sq_norm': 8,
 'rstd_norm': 2,
 'ev_norm': 16,
 'conv_in': 12,
 'conv_u': 12,
 'ev_proj': 20,
 'rstd_found': 4,
 'ev_qT': 16,
 'prob': 64,
 'ev_pT': 64,
 'sinkexp': 4,
 'ev_oT': 8,
 'expA': 1,
 'softexp': 1,
 'softln': 1,
 'decays': 1,
 'expd': 16,
 'squares_summed': 16,
 'ev_gn': 8,
 'gate': 24,
 'ev_mg': 8,
 'ev_out': 8,
 'scores': 1,
 'ssilu': 4,
 'ev_shT': 4,
 'ev_ada': 12,
 'modrow_ada': 4,
 'inv_norm': 2,
 'hn_norm': 8,
 'xp_zero': 2,
 'conv': 12,
 'ev_uT': 10,
 'inv_found': 4,
 'roped': 8,
 'negmax': 64,
 'ev_o': 8,
 'sinkarg': 4,
 'nabs': 1,
 'onep': 1,
 'a_ready': 1,
 'cum': 1,
 'xw': 6,
 'state': 6,
 'ev_yoff': 6,
 'scan_done': 1,
 'diff': 16,
 'cbm': 16,
 'm_ready': 16,
 'ev_y': 8,
 'yz': 4,
 'gn_rows': 4,
 'gated': 24,
 'mg_rows': 4,
 'norow': 1,
 'masks': 1,
 'dest': 4,
 'shid': 4,
 'ev_sy': 4,
 'flags': 1,
 'places': 1,
 'list_ready': 1,
 'combined': 16}
EACH_EXPERT = ("mm_xT", "mm_gu", "mm_hT", "mm_down", "ev_xa", "ev_xv", "ev_hT", "ev_ya", "ev_yv", "silu", "hidden", "staged")
BEFORE.update({n: N_EXP for n in EACH_EXPERT})
BEFORE.update({f"{n}{i}": 16 * N_EXP // EXP_SLOTS for n in ("gath", "scat") for i in range(EXP_SLOTS)})
BEFORE.update({f"weights{i}": 48 * (N_EXP // EXP_SLOTS + (i == 2)) for i in range(EXP_SLOTS)})

_NAMES = ['x', 'c', 'ctx', 'c_ctx', 'w_ada', 'b_ada', 'g_mix_pre', 'g_mix_post', 'g_ffn_pre', 'g_ffn_post', 'w_in', 'g_q_a', 'g_k_a',
          'sink_w', 'ssm_conv_w', 'ssm_conv_b', 'ssm_dt_bias', 'ssm_a_log', 'ssm_d', 'ssm_norm', 'w_br_a', 'w_br_w', 'w_br_s', 'w_out',
          'w_router', 'b_router', 'we_gate', 'we_up', 'we_down', 'ws_gate', 'ws_up', 'ws_down']


def kernel(**inputs):
    import concourse.bacc as bacc
    from concourse.bass_utils import run_bass_kernel_spmd

    nc = bacc.Bacc("TRN2", target_bir_lowering=False, num_devices=1)
    arrays, aps = {}, {}
    for name in _NAMES:
        v = np.ascontiguousarray(inputs[name])
        arrays[f"in_{name}"] = v
        aps[name] = nc.dram_tensor(f"in_{name}", v.shape, mybir.dt.from_np(v.dtype), kind="ExternalInput").ap()
    arrays["in_constants"] = constants()
    cst_d = nc.dram_tensor("in_constants", (P, C_END), F32, kind="ExternalInput").ap()
    out = nc.dram_tensor("out", (1, SEG, D), F32, kind="ExternalOutput").ap()
    build(nc, aps, cst_d, out)
    r = run_bass_kernel_spmd(nc, [arrays], core_ids=[0])
    return r.results[0]["out"]
```

```python
import numpy as np
from contextlib import ExitStack
import concourse.bass as bass
from concourse import mybir

F32 = mybir.dt.float32
ALU = mybir.AluOpType
ACT = mybir.ActivationFunctionType
AX = mybir.AxisListType

P = 128
D = 1024
KD = D // P
DEPTH = 2
LAT_TILES, CTX_TILES = 2, 2
TILES = LAT_TILES + CTX_TILES
TOK = TILES * P
SEG = LAT_TILES * P
HD = 64
HEADS, KV = 8, 2
GQ = HEADS // KV
SH, SP_, SG, SN = 16, 64, 2, 128
SI = SH * SP_
CONV_T = 12
N_EXP, D_EXP = 64, 256
EPS = 1e-6
NEG = -1.0e30
SCALE = HD ** -0.5
ROUTED_SCALE = 2.5
TOP_K = 8
I32, U32 = mybir.dt.int32, mybir.dt.uint32
BLOCKS = TOK // P
CAP = TOK
NOROW = float(1 << 20)
XG = 4
XSTEPS = 11
X0 = 3
NCH = 512
COL_XBC, COL_DT, COL_QKV, COL_Z, COL_GATE = 2560, 4096, 0, 1536, 4128
RING = 3
EXP_SLOTS = 4

LOOP_SEMS = ("x_step", "x_gath", "x_scat", "x_weights")

C_ID, C_UT, C_LT, C_NA, C_NB, C_COS, C_SIN, C_TRI8, C_IOTA, C_PAY, C_THR, C_EID, C_COL, C_ONE, C_MOD, C_END = (
    0, 128, 256, 384, 512, 640, 768, 896, 960, 1024, 1056, 1059, 1060, 1063, 1064, 1065)


def constants():
    c = np.zeros((P, C_END), np.float32)
    i = np.arange(P)
    c[:, C_ID:C_ID + P] = np.eye(P)
    c[:, C_UT:C_UT + P] = i[:, None] <= i[None, :]
    c[:, C_LT:C_LT + P] = i[:, None] >= i[None, :]
    c[:, C_NA:C_NA + P] = np.where(i[None, :] > i[:, None], NEG, 0)
    c[:, C_NB:C_NB + P] = np.where(i[None, :] < i[:, None], NEG, 0)
    c[:, C_ONE] = 1
    c[16:32, C_MOD] = 1
    c[:, C_IOTA:C_IOTA + 64] = np.arange(64)
    for t in range(TILES):
        for k in range(TOP_K):
            c[:, C_PAY + t * TOP_K + k] = (t * P + i) * TOP_K + k
    for b in range(BLOCKS - 1):
        c[:, C_THR + b] = (b + 1) * P
        c[:, C_COL + b] = (b + 1) * N_EXP + i
    c[:, C_EID] = i
    half = HD // 2
    inv = np.float32(10000.0) ** (-np.arange(0, half, 2, dtype=np.float32) / np.float32(half))
    for t in range(LAT_TILES):
        tok = t * P + i
        ang = np.stack([(tok // 64).astype(np.float32)[:, None] * inv, (tok % 64).astype(np.float32)[:, None] * inv], 1)
        co, si = np.cos(ang), np.sin(ang)
        c[:, C_COS + t * HD:C_COS + (t + 1) * HD] = np.stack([co, co], 2).reshape(P, HD)
        c[:, C_SIN + t * HD:C_SIN + (t + 1) * HD] = np.stack([-si, si], 2).reshape(P, HD)
    g = np.arange(8)
    c[:, C_TRI8:C_TRI8 + 64] = (g[None, :] < g[:, None]).reshape(1, 64)
    return c


def ring_jobs():
    jobs, ends = [], [0]
    for l in range(DEPTH):
        if l == 0:
            jobs += [(l, "ada0", n) for n in range(6)]
        jobs += [(l, "xbc", n) for n in range(3)]
        jobs += [(l, "qkv", n) for n in range(3)]
        jobs += [(l, "z", n) for n in range(2)]
        jobs += [(l, "ada1", n) for n in range(6)]
        if l + 1 < DEPTH:
            jobs += [(l + 1, "ada0", n) for n in range(6)]
        for b in range(3):
            for n in range(2):
                jobs += [(l, "gate", b * 2 + n), (l, "br", b * 2 + n)]
        jobs += [(l, "out", n) for n in range(2)]
        ends.append(len(jobs))
    return jobs, ends


def build(nc, a, cst_d, out):
    jobs, ring_ends = ring_jobs()
    job_at = {j: i for i, j in enumerate(jobs)}
    out_tiles = [TILES, LAT_TILES]
    before = BEFORE
    ctx = ExitStack()
    with ctx:
        top = [nc.sbuf_base + 31 & ~31]

        def at(name, shape, offset, dt=F32):
            return nc.alloc_sbuf_tensor_at(name, shape, dt, offset=offset)

        def region(nbytes):
            o = top[0]
            top[0] += nbytes + 31 & ~31
            return o

        sems = {}

        def instance(name):
            stem, l = name[:-2], name[-2:]
            if l not in ("_0", "_1") or stem in LOOP_SEMS:
                return name, 0
            for shared, members in SHARED.items():
                names = [m for m, _ in members]
                if stem in names:
                    here = sum(n[int(l[1])] for _, n in members[:names.index(stem)])
                    return shared, here + (sum(n[0] for _, n in members) if l == "_1" else 0)
            if stem[:-1].endswith("norm"):
                both = before[stem[:-1]]
                return stem[:-1], (both if l == "_1" else 0) + (both // 2 if stem[-1] == "1" else 0)
            return stem, before[stem] if l == "_1" else 0

        def sem(name):
            name = instance(name)[0]
            if name not in sems:
                sems[name] = ctx.enter_context(nc.semaphore(name))
            return sems[name]

        def stage(name, value):
            return sem(name), value + instance(name)[1]

        x = at("x", [P, TILES, D], region(TILES * D * 4))
        r_ring = region(RING * KD * NCH * 4)
        ring = at("ring", [P, RING, KD, NCH], r_ring)
        r_qT = region(10 * TOK * 4)
        bcc = at("bcc", [P, 4, TOK], region(4 * TOK * 4))
        btok = at("btok", [P, TILES, 2 * SN], region(TILES * 2 * SN * 4))
        hT = at("hT", [P, KD, TOK], region(KD * TOK * 4))
        esl = at("esl", [P, EXP_SLOTS, 3, 2048], r_ring)
        comb = at("comb", [P, 4, 2, D], r_ring + RING * KD * NCH * 4)
        assert top[0] - r_ring >= EXP_SLOTS * 3 * 2048 * 4
        r_bc = region(6 * D * 4)
        bc = at("bc", [P, 3, 2, D], r_bc)
        zs = at("zs", [P, TILES, D], r_bc)
        mT = at("mT", [P, KD, TOK], r_bc)
        cst = at("cst", [P, C_END], region(C_END * 4))
        r_qk = region(TILES * 1536 * 4)
        qk = at("qk", [P, TILES, 1536], r_qk)
        y = at("y", [P, TILES, D], r_qk)
        st = at("st", [P, 2, SI], r_qk + TILES * D * 4)
        acc = at("acc", [P, TILES, D], r_qk)
        qT = at("qT", [P, 2, GQ, TOK], r_qT)
        kT = at("kT", [P, 2, TOK], r_qT + 2 * GQ * TOK * 4)
        oT = at("oT", [P, KD, TOK], r_qT)
        XPB = (2 * (SEG + 2) * 4 + 31) & ~31
        xp = [at(f"xp{i}", [P, 2, SEG + 2], r_qT + i * XPB) for i in range(2)]
        cacc = at("cacc", [P, 2, TOK], r_qT + 2 * XPB)
        cu = at("cu", [P, 2, TOK], r_qT + 2 * XPB + 2 * TOK * 4)
        r_mod = r_qT + KD * TOK * 4
        mstg = at("mstg", [2, NCH], r_mod)
        mrow = at("mrow", [48, P], r_mod + 2048)
        mbias = at("mbias", [48, P], r_mod + 2560)
        mgain = at("mgain", [48, P], r_mod + 3072)
        r_xs = region(TILES * SI * 4)
        xs = at("xs", [P, TILES, SI], r_xs)
        ysT = at("ysT", [P, KD, TOK], r_xs)
        ml = at("ml", [P, TILES, D], r_xs)
        r_t = region(3 * D * 4)
        hn = at("hn", [P, 2, D], r_t)
        pr = at("pr", [P, 2, NCH], r_t)
        pT = at("pT", [P, 2, NCH], r_t + 2 * NCH * 4)
        rt = at("rt", [P, 640], r_t)
        rq = at("rq", [P, 2, 640], r_t + 640 * 4)
        xw = at("xw", [P, 2, D], r_t + D * 4)
        mt = at("mt", [P, 3, 8, P], r_t)
        tmp = at("tmp", [P, D], r_t + 2 * D * 4)
        gs = at("gs", [P, 2, NCH], r_t)
        junk = at("junk", [P, D], r_t + 2 * D * 4)
        shs = at("shs", [P, TILES, D_EXP], r_bc)
        hsg = at("hsg", [P, 2, D_EXP], r_t)
        hgT = at("hgT", [P, 2, 2, P], r_t + 2 * D_EXP * 4)
        r_nw = region(SI * 4)
        nw = at("nw", [P, SI], r_nw)
        xg = [at(f"xg{i}", [P, D], o) for i, o in enumerate((r_t + D * 4, r_t + 2 * D * 4, r_xs + 2 * D * 4, r_nw))]
        ysb = [at(f"ysb{i}", [P, D], o) for i, o in enumerate((r_bc + 2 * D * 4, r_bc + 3 * D * 4, r_xs, r_xs + D * 4))]
        xgT = at("xgT", [P, 2, KD, P], r_bc)
        r_rt = r_qk + TILES * D * 4
        oneh = at("oneh", [P, TOP_K, N_EXP], r_rt)
        onet = at("onet", [P, TOP_K, N_EXP], r_rt + 2048)
        tsb = at("tsb", [N_EXP, CAP], r_rt + 4096)
        nor = at("nor", [P, N_EXP * CAP // P], r_rt + 6144)
        eiu = at("eiu", [P, TILES, TOP_K], r_rt + 7168, U32)
        eif = at("eif", [P, TILES, TOP_K], r_rt + 7296)
        rnk = at("rnk", [P, TILES, TOP_K], r_rt + 7424)
        wk = at("wk", [P, TILES, TOP_K], r_rt + 7552)
        dst_i = at("dst_i", [P, TILES, TOP_K], r_rt + 7680, I32)
        xl = at("xl", [1, 72], r_rt + 7808, I32)
        gqk = at("gqk", [P, 640], r_t + 3 * 640 * 4)
        nsink = at("nsink", [P, HEADS], region(HEADS * 4))
        dtb = at("dtb", [P, 32], region(128))
        alog = at("alog", [P, 32], region(128))
        dsk = at("dsk", [P, SH], region(64))
        brt = at("brt", [P, N_EXP], region(256))
        crow = at("crow", [4 * CONV_T, P], region(512))
        ccol = at("ccol", [P, 4 * CONV_T], region(4 * CONV_T * 4))
        wdt = at("wdt", [P, KD, 32], region(KD * 32 * 4))
        r_small = region(9 * P * 4)
        dts = at("dts", [P, 9, 2, TILES, SH], r_small)
        wr = at("wr", [P, KD, N_EXP], r_xs)
        rtr = at("rtr", [P, 12, TILES, N_EXP], r_xs + KD * N_EXP * 4)
        gi = at("gi", [P, BLOCKS * N_EXP], r_xs + 14336, I32)
        si = at("si", [P, BLOCKS * N_EXP], r_xs + 15360, I32)
        gstg = at("gstg", [P, EXP_SLOTS], region(32), I32)
        sstg = at("sstg", [P, EXP_SLOTS], region(32), I32)
        stat = at("stat", [P, 8, 64], region(8 * 64 * 4))
        cT = at("cT", [P, 16], region(64))
        crw = at("crw", [16, P], region(512))
        cbm = at("cbm", [P, 2, P], region(2 * P * 4))

        ps = ctx.enter_context(nc.psum_tensor("ps", [P, 8, NCH], F32))

        h_d = nc.dram_tensor("h_rows", (TOK, D), F32, kind="Internal").ap()
        modp_d = nc.dram_tensor("modulation_products", (2 * DEPTH, 3, 2, D), F32, kind="Internal").ap()
        mod_d = nc.dram_tensor("modulation", (2 * DEPTH, 6 * D), F32, kind="Internal").ap()
        tab_d = nc.dram_tensor("slot_table", (N_EXP * CAP, 1), F32, kind="Internal").ap()
        y_d = nc.dram_tensor("routed_rows", (TOK * TOP_K, D), F32, kind="Internal").ap()

        ident = cst[:, C_ID:C_ID + P]
        UT, LT = cst[:, C_UT:C_UT + P], cst[:, C_LT:C_LT + P]
        tri = [UT, LT]
        ones = cst[:, C_ONE:C_ONE + 1].to_broadcast([P, P])
        cond = sem("cond_loaded")
        param = sem("params_loaded")
        phase = sem("phase_done")
        full = [sem(f"ring_full{i}") for i in range(RING)]
        expert_full = [sem(f"weights{i}_0") for i in range(EXP_SLOTS)]

        def max_extra(l):
            return out_tiles[l] * P * TOP_K // (P + 1)

        def extra_groups(l):
            return -(-max_extra(l) // XG)

        def qkv_units(l):
            return [(n, t) for t in range(TILES) for n in range(3) if n > 0 or t < out_tiles[l]]

        def qkv_until(l, t):
            return sum(1 for _, tt in qkv_units(l) if tt <= t)

        def attn_units(l):
            return [(t, ty, g, h) for t in range(out_tiles[l]) for ty in range(2) for g in range(KV) for h in range(GQ)]

        def scan_order(d):
            ctx_t, lat_t = [2, 3], [0, 1]
            return ctx_t + lat_t if d == 0 else ctx_t[::-1] + lat_t[::-1]

        def scan_steps(l):
            return [(s, d, scan_order(d)[s]) for s in range(4) for d in range(2)]

        def tr_units(l):
            return [(t, ty) for t in range(TILES) for ty in range(2)]

        def has_q(l, t):
            return t < out_tiles[l]

        def sets_before(l):
            return min(2 * l + 1, 2 * DEPTH) if l else 0

        def sets_with(m):
            return sets_before((m + 1) // 2) if m else 1

        def last_use(j):
            l, kind, n = jobs[j]
            if kind in ("ada0", "ada1"):
                return sem("mm_ada"), 6 * (2 * l + int(kind[3])) + n + 1
            if kind == "xbc":
                return stage(f"mm_xbc_{l}", 4 * (n + 1))
            if kind == "qkv":
                u = qkv_units(l)
                return stage(f"mm_qkv_{l}", max(i for i, (m, _) in enumerate(u) if m == n) + 1)
            if kind == "z":
                return stage(f"mm_z_{l}", (n + 1) * out_tiles[l])
            if kind == "gate":
                return stage(f"mm_gate_{l}", (n + 1) * out_tiles[l])
            if kind == "br":
                return stage(f"mm_br_{l}", (n + 1) * out_tiles[l])
            return stage(f"mm_out_{l}", 2 * out_tiles[l] - 1 + n)

        def ring_source(j):
            l, kind, n = jobs[j]
            rows = lambda w, c: w[:, c:c + NCH].rearrange("(k p) n -> p k n", p=P)
            if kind in ("ada0", "ada1"):
                return rows(a["w_ada"][l], (3 * D if kind == "ada1" else 0) + n * NCH)
            if kind in ("xbc", "qkv", "z", "gate"):
                base = {"xbc": COL_XBC, "qkv": COL_QKV, "z": COL_Z, "gate": COL_GATE}[kind]
                return rows(a["w_in"][l], base + n * NCH)
            if kind == "br":
                return rows(a[("w_br_a", "w_br_w", "w_br_s")[n // 2]][l], (n % 2) * NCH)
            return rows(a["w_out"][l], n * NCH)

        def chunk(l, kind, n):
            j = job_at[(l, kind, n)]
            return ring[:, j % RING], (full[j % RING], 16 * (j // RING + 1))

        PHASES = [(l, n) for l in range(DEPTH) for n in ("ada0", "norm0", "inproj", "attn", "ssd", "gn", "merge", "out", "norm1", "router", "moe", "post")
                  if l == 0 or n != "ada0"]

        def phase_start(l, name):
            return 2 * (PHASES.index((l, name)) if l < DEPTH else len(PHASES))

        def after_layer(l):
            return phase_start(l + 1, "norm0") if l + 1 < DEPTH else 2 * len(PHASES)

        class Steps:

            def __init__(self, eng, own):
                self.eng, self.own, self.n = eng, own, {}

            def mark(self, ins, s=None):
                s = s if s is not None else self.own
                self.n[s.name] = self.n.get(s.name, 0) + 1
                ins.then_inc(s, 1)

            def run(self, ins, s=None):
                s = s if s is not None else self.own
                self.mark(ins, s)
                self.eng.wait_ge(s, self.n[s.name])

        block = ctx.enter_context(nc.Block())

        @block.sync
        def _(sp):
            def load_ring(j):
                if j >= RING:
                    sp.wait_ge(*last_use(j - RING))
                src = ring_source(j)
                sp.dma_start(ring[:, j % RING, 0:src.shape[1], :], src).then_inc(full[j % RING], 16)

            def load_expert(slot, wg, wu, wd, s=None):
                for i, (w, n) in enumerate(((wg, D_EXP), (wu, D_EXP), (wd, D))):
                    sp.dma_start(esl[:, slot, i, :].rearrange("p (k n) -> p k n", n=n), w.rearrange("(k p) n -> p k n", p=P))\
                        .then_inc(s if s is not None else expert_full[slot], 16)

            def expert(l, e):
                return [a[n][l, bass.ds(e, 1)].rearrange("o r n -> (o r) n") for n in ("we_gate", "we_up", "we_down")]

            sp.dma_start(cst[:, :], cst_d).then_inc(cond, 16)
            sp.dma_start(crw[0:8, :], a["c"].rearrange("o (k p) -> (o k) p", p=P)).then_inc(cond, 16)
            sp.dma_start(crw[8:16, :], a["c_ctx"].rearrange("(k p) -> k p", p=P)).then_inc(cond, 16)
            sp.dma_start(x[:, 0:LAT_TILES, :], a["x"][0].rearrange("(t p) d -> p t d", p=P)).then_inc(sem("x_loaded"), 16)
            sp.dma_start(x[:, LAT_TILES:, :], a["ctx"][0].rearrange("(t p) d -> p t d", p=P)).then_inc(sem("x_loaded"), 16)
            for l in range(DEPTH):
                if l:
                    sp.wait_ge(*stage(f"combined_{l - 1}", 4 * out_tiles[l - 1] - 3))
                for j in range(ring_ends[l], ring_ends[l + 1]):
                    if jobs[j] == (0, "xbc", 1):
                        sp.wait_ge(sem("mod_loaded"), 16)
                    load_ring(j)
                nt = out_tiles[l]
                sp.wait_ge(*stage(f"mm_br_{l}", 6 * nt))
                sp.wait_ge(sem("mod_written"), 16 * sets_before(l + 1))
                load_expert(2, a["ws_gate"][l], a["ws_up"][l], a["ws_down"][l])
                for j in range(ring_ends[l + 1] - RING, ring_ends[l + 1]):
                    sp.wait_ge(*last_use(j))
                for e in range(EXP_SLOTS):
                    if e == 2:
                        sp.wait_ge(*stage(f"mm_sdown_{l}", nt))
                    load_expert(e, *expert(l, e))
                with sp.Fori(0, N_EXP // EXP_SLOTS - 1) as r:
                    for s in range(EXP_SLOTS):
                        sp.wait_ge(*stage(f"mm_down_{l}", r * EXP_SLOTS + (s + 1)))
                        load_expert(s, *expert(l, r * EXP_SLOTS + (s + EXP_SLOTS)))
                sp.wait_ge(*stage(f"mm_down_{l}", N_EXP))
                sp.wait_ge(*stage(f"list_ready_{l}", 1))
                n = sp.value_load(xl[0:1, 64:65], min_val=0, max_val=max_extra(l))
                with sp.Fori(0, extra_groups(l)) as o:
                    with sp.If(o * XG < n):
                        with sp.Fori(0, XG) as k:
                            j = o * XG + k
                            with sp.If(j < n):
                                e = sp.value_load(xl[0:1, bass.ds(j, 1)], min_val=0, max_val=N_EXP - 1)
                                sp.wait_ge(sem(f"x_step_{l}"), j * XSTEPS + (X0 - XSTEPS + 9))
                                load_expert(0, *expert(l, e), s=sem(f"x_weights_{l}"))
                                sp.wait_ge(sem(f"x_step_{l}"), j * XSTEPS + (X0 + 9))
                                sp.sem_inc(sem("sync_passed"), 1)
            sp.wait_ge(phase, 2 * len(PHASES))
            sp.dma_start(out[0].rearrange("(t p) d -> p t d", p=P), x[:, 0:LAT_TILES, :]).then_inc(sem("out_written"), 16)
            sp.wait_ge(sem("out_written"), 16)

        @block.gpsimd
        def _(pool):
            def rows(dst, src):
                pool.dma_start(dst, src).then_inc(param, 16)

            def dispatch(l):
                nt = out_tiles[l]
                for t in range(nt):
                    pool.wait_ge(*stage(f"hn_norm1_{l}", t + 1))
                    pool.dma_start(h_d[t * P:(t + 1) * P, :], hn[:, t % 2, :]).then_inc(sem(f"h_written{t % 2}_{l}"), 16)
                pool.wait_ge(*stage(f"norow_{l}", 1))
                pool.dma_start(tab_d.rearrange("(p n) o -> p (n o)", p=P), nor[:, :]).then_inc(sem(f"tab_cleared_{l}"), 16)
                pool.wait_ge(*stage(f"tab_cleared_{l}", 16))
                for t in range(nt):
                    pool.wait_ge(*stage(f"dest_{l}", t + 1))
                    for k in range(TOP_K):
                        c = t * TOP_K + k
                        pool.indirect_dma_start(out=tab_d, out_offset=bass.IndirectOffsetOnAxis(ap=dst_i[:, t, k:k + 1], axis=0),
                                                in_=cst[:, C_PAY + c:C_PAY + c + 1], in_offset=None).then_inc(sem(f"tab_written_{l}"), 16)
                pool.wait_ge(*stage(f"tab_written_{l}", 16 * nt * TOP_K))
                pool.dma_start(tsb[:, :], tab_d.rearrange("(e c) o -> e (c o)", c=CAP)).then_inc(sem(f"tab_read_{l}"), 16)
                for i in range(2):
                    pool.wait_ge(*stage(f"h_written{i}_{l}", 16 * nt // 2))

                def gather(e, slot):
                    pool.wait_ge(*stage(f"staged_{l}", e + 1))
                    pool.sem_inc(sem("pool_passed"), 1)
                    pool.indirect_dma_start(out=xg[slot][:, :], out_offset=None, in_=h_d,
                                            in_offset=bass.IndirectOffsetOnAxis(ap=gstg[:, slot:slot + 1], axis=0),
                                            bounds_check=nt * P - 1, oob_is_err=False).then_inc(sem(f"gath{slot}_{l}"), 16)

                def scatter(e, slot):
                    pool.wait_ge(*stage(f"ev_ya_{l}", e + 1))
                    pool.wait_ge(*stage(f"ev_yv_{l}", e + 1))
                    pool.sem_inc(sem("pool_passed"), 1)
                    pool.indirect_dma_start(out=y_d, out_offset=bass.IndirectOffsetOnAxis(ap=sstg[:, slot:slot + 1], axis=0),
                                            in_=ysb[slot][:, :], in_offset=None,
                                            bounds_check=nt * P * TOP_K - 1, oob_is_err=False).then_inc(sem(f"scat{slot}_{l}"), 16)

                def step(e, j):
                    gather(e + EXP_SLOTS, j)
                    scatter(e - 1, (j + 3) % 4)

                for e in range(EXP_SLOTS + 1):
                    gather(e, e % 4)
                for e in (1, 2, 3):
                    step(e, e)
                with pool.Fori(1, N_EXP // 4 - 1) as r:
                    for j in range(4):
                        step(r * 4 + j, j)
                for e in range(N_EXP - 4, N_EXP + 1):
                    scatter(e - 1, (e - 1) % 4)
                if l + 1 < DEPTH:
                    layer_params(l + 1)
                for i in range(EXP_SLOTS):
                    pool.wait_ge(*stage(f"scat{i}_{l}", 16 * N_EXP // EXP_SLOTS))
                pool.wait_ge(*stage(f"list_ready_{l}", 1))
                n = pool.value_load(xl[0:1, 64:65], min_val=0, max_val=max_extra(l))
                with pool.Fori(0, extra_groups(l)) as o:
                    with pool.If(o * XG < n):
                        with pool.Fori(0, XG) as k:
                            j = o * XG + k
                            with pool.If(j < n):
                                pool.wait_ge(sem(f"x_step_{l}"), j * XSTEPS + (X0 + 1))
                                pool.sem_inc(sem("pool_passed"), 1)
                                pool.indirect_dma_start(out=xg[0][:, :], out_offset=None, in_=h_d,
                                                        in_offset=bass.IndirectOffsetOnAxis(ap=gstg[:, 0:1], axis=0),
                                                        bounds_check=nt * P - 1, oob_is_err=False).then_inc(sem(f"x_gath_{l}"), 16)
                                pool.wait_ge(sem(f"x_step_{l}"), j * XSTEPS + (X0 + 10))
                                pool.sem_inc(sem("pool_passed"), 1)
                                pool.indirect_dma_start(out=y_d, out_offset=bass.IndirectOffsetOnAxis(ap=sstg[:, 0:1], axis=0),
                                                        in_=ysb[0][:, :], in_offset=None,
                                                        bounds_check=nt * P * TOP_K - 1, oob_is_err=False).then_inc(sem(f"x_scat_{l}"), 16)
                                pool.wait_ge(sem(f"x_scat_{l}"), j * 16 + 16)
                                pool.sem_inc(sem(f"x_step_{l}"), 1)
                pool.wait_ge(*stage(f"mm_down_{l}", N_EXP))
                for u in range(nt * 4):
                    t, kp = u // 4, u % 4
                    if u >= 4:
                        pool.wait_ge(*stage(f"combined_{l}", u - 3))
                    pool.dma_start(comb[:, kp, :, :], y_d[t * P * TOP_K:(t + 1) * P * TOP_K, :]
                                   .rearrange("(p k) d -> p k d", k=TOP_K)[:, 2 * kp:2 * kp + 2, :]).then_inc(sem(f"comb{kp}_{l}"), 16)
                if l + 1 < DEPTH:
                    mod_load(2 * l + 2, 0)
                    norm_weight(l + 1)

            def mod_params(m):
                l, half = m // 2, m % 2
                if m:
                    pool.wait_ge(sem("mod_written"), 16 * m)
                pool.wait_ge(sem("mod_cleared"), m + 1)
                for s in range(2):
                    for v_ in range(3):
                        r = v_ * 16 + s * 8
                        pool.dma_start(mbias[r:r + 8, :], a["b_ada"][l, (half * 3 + v_) * D:(half * 3 + v_ + 1) * D].rearrange("(r p) -> r p", p=P))\
                            .then_inc(sem("mod_params"), 16)
                    for i, n in enumerate((("g_mix_pre", "g_mix_post"), ("g_ffn_pre", "g_ffn_post"))[half]):
                        r = 16 * (i + 1) + s * 8
                        pool.dma_start(mgain[r:r + 8, :], a[n][l].rearrange("(r p) -> r p", p=P)).then_inc(sem("mod_params"), 16)

            def mod_store(m):
                for n in range(6):
                    pool.wait_ge(sem("ev_mod"), 6 * m + n + 1)
                    pool.dma_start(modp_d[m, n // 2, :, n % 2 * NCH:(n % 2 + 1) * NCH], mstg[:, :]).then_inc(sem("products_stored"), 16)
                pool.wait_ge(sem("products_stored"), 96 * (m + 1))
                pool.dma_start(mrow[:, :], modp_d[m].rearrange("v s (k p) -> (v s k) p", p=P)).then_inc(sem("mod_params"), 16)
                pool.wait_ge(sem("mod_done"), m + 1)
                pool.dma_start(mod_d[m].rearrange("(r p) -> r p", p=P), mrow[:, :]).then_inc(sem("mod_written"), 16)

            def mod_load(m, part):
                if part == 0:
                    pool.wait_ge(sem("mod_written"), 16 * sets_with(m))
                lo, hi = (0, 4 * D) if part == 0 else (4 * D, 6 * D)
                pool.dma_start(bc[:, :, :, :].rearrange("p v s n -> p (v s n)")[:, lo:hi], mod_d[m, lo:hi].partition_broadcast(P))\
                    .then_inc(sem(("mod_loaded", "gate_loaded")[part]), 16)

            def layer_params(l):
                rows(crow[0:36, :], a["ssm_conv_w"][l].rearrange("w (c p) -> (w c) p", p=P))
                rows(crow[36:48, :], a["ssm_conv_b"][l].rearrange("(c p) -> c p", p=P))
                rows(dtb[:, :], a["ssm_dt_bias"][l].rearrange("d h -> (d h)").partition_broadcast(P))
                rows(alog[:, :], a["ssm_a_log"][l].rearrange("d h -> (d h)").partition_broadcast(P))
                rows(dsk[:, :], a["ssm_d"][l].partition_broadcast(P))
                rows(nsink[:, :], a["sink_w"][l].partition_broadcast(P))
                rows(brt[:, :], a["b_router"][l].partition_broadcast(P))
                rows(wdt[:, :, :], a["w_in"][l][:, COL_DT:COL_DT + 32].rearrange("(k p) n -> p k n", p=P))

            def norm_weight(l):
                rows(nw[:, :], a["ssm_norm"][l].partition_broadcast(P))

            layer_params(0)
            norm_weight(0)
            mod_params(0)
            mod_store(0)
            mod_load(0, 0)
            mod_load(0, 1)
            for l in range(DEPTH):
                if l:
                    pool.wait_ge(phase, after_layer(l - 1))
                    mod_load(2 * l, 1)
                pool.wait_ge(phase, phase_start(l, "inproj"))
                for h in range(HEADS + KV):
                    pool.dma_start(gqk[:, h * HD:(h + 1) * HD],
                                   a["g_q_a" if h < HEADS else "g_k_a"][l].partition_broadcast(P)).then_inc(sem("gqk_loaded"), 16)
                pool.wait_ge(phase, phase_start(l, "ssd"))
                sets = range(2 * l + 1, sets_before(l + 1))
                for m in sets:
                    mod_params(m)
                    mod_store(m)
                pool.wait_ge(*stage(f"mm_out_{l}", 2 * out_tiles[l]))
                mod_load(2 * l + 1, 0)
                pool.wait_ge(phase, phase_start(l, "norm1"))
                rows(wr[:, :, :], a["w_router"][l].rearrange("(k p) n -> p k n", p=P))
                mod_load(2 * l + 1, 1)
                dispatch(l)

        def params_at(l, half):
            return 16 * (10 * l + 9 + half)

        @block.tensor
        def _(pe):
            def mms(o, pairs, start=True, stop=True):
                for i, (lt, rh) in enumerate(pairs):
                    last = nc.tensor.matmul(o, lt, rh, start=start and i == 0, stop=stop and i == len(pairs) - 1)
                return last

            def transposes(bank, ins):
                for i, blk in enumerate(ins):
                    last = nc.tensor.transpose(ps[:, bank, i * P:(i + 1) * P], blk, ident)
                return last

            pe.wait_ge(cond, 16 * 3)
            nc.tensor.transpose(ps[:, 0, 0:16], crw[:, :], cst[0:16, C_ID:C_ID + 16]).then_inc(sem("mm_cond"), 1)
            pe.wait_ge(sem("cond_silu"), 2)
            for l in range(DEPTH):
                nt = out_tiles[l]

                def mod_chunk(m, n):
                    w, ready = chunk(m // 2, f"ada{m % 2}", n)
                    pe.wait_ge(*ready)
                    bank = 7 - n % 2 if m == 0 else 7
                    done = 6 * m + n - (1 if m == 0 else 0)
                    if done > 0:
                        pe.wait_ge(sem("ev_mod"), done)
                    mms(ps[0:2, bank, :], [(cT[:, k::8], w[:, k, :]) for k in range(KD)]).then_inc(sem("mm_ada"), 1)

                def norm(half, tiles):
                    kind = f"norm{half}"
                    pe.wait_ge(phase, phase_start(l, kind))
                    if half == 0:
                        pe.wait_ge(param, params_at(l, 0))
                        nc.tensor.transpose(ps[:, 6, 0:48], crow[:, :], cst[0:48, C_ID:C_ID + 48]).then_inc(sem(f"mm_ccol_{l}"), 1)
                    for t in range(tiles):
                        pe.wait_ge(*stage(f"hn_{kind}_{l}", t + 1))
                        for b in range(2):
                            u = 2 * t + b
                            if u >= 4:
                                pe.wait_ge(*stage(f"ev_{kind}_{l}", u - 3))
                            transposes(u % 4, [hn[:, t % 2, (4 * b + i) * P:(4 * b + i + 1) * P] for i in range(4)])\
                                .then_inc(sem(f"mm_{kind}_{l}"), 1)

                if l == 0:
                    for n in range(6):
                        mod_chunk(0, n)
                norm(0, TILES)

                pe.wait_ge(phase, phase_start(l, "inproj"))

                def conv_transposes(ct):
                    pe.wait_ge(*stage(f"conv_u_{l}", ct + 1))
                    if ct >= 2:
                        pe.wait_ge(*stage(f"ev_uT_{l}", ct - 1))
                    src = cu[:, ct % 2, :] if ct < 8 else bcc[:, ct - 8, :]
                    transposes(2 + ct % 2, [src[:, t * P:(t + 1) * P] for t in range(TILES)]).then_inc(sem(f"mm_uT_{l}"), 1)

                for ct in range(CONV_T):
                    w, ready = chunk(l, "xbc", ct // 4)
                    pe.wait_ge(*ready)
                    if ct >= 2:
                        pe.wait_ge(*stage(f"conv_in_{l}", ct - 1))
                    mms(ps[:, ct % 2, :], [(w[:, k, (ct % 4) * P:(ct % 4 + 1) * P], hT[:, k, :]) for k in range(KD)])\
                        .then_inc(sem(f"mm_xbc_{l}"), 1)
                    if ct >= 2:
                        conv_transposes(ct - 2)
                for t in range(TILES):
                    last = mms(ps[:, 4, t * 32:(t + 1) * 32], [(hT[:, k, t * P:(t + 1) * P], wdt[:, k, :]) for k in range(KD)])
                last.then_inc(sem(f"mm_dt_{l}"), 1)
                u = 0
                e = 0

                def q_transposes(t):
                    nonlocal e
                    for ty in range(2):
                        i = tr_units(l).index((t, ty))
                        pe.wait_ge(*stage(f"roped_{l}", i + 1))
                        for part in range(2):
                            if part == 0 and not has_q(l, t):
                                continue
                            if e == 0:
                                pe.wait_ge(*stage(f"conv_in_{l}", CONV_T))
                                pe.wait_ge(*stage(f"ev_uT_{l}", CONV_T - 2))
                            if e >= 4:
                                pe.wait_ge(*stage(f"ev_qT_{l}", e - 3))
                            ins = [rq[:, i % 2, h * P:(h + 1) * P] for h in range(GQ)] if part == 0 else [rq[:, i % 2, 512:640]]
                            transposes(e % 4, ins).then_inc(sem(f"mm_qT_{l}"), 1)
                            e += 1

                for u, (n, t) in enumerate(qkv_units(l)):
                    w, ready = chunk(l, "qkv", n)
                    pe.wait_ge(*ready)
                    if u >= 3:
                        pe.wait_ge(*stage(f"ev_proj_{l}", u - 2))
                    mms(ps[:, 5 + u % 3, :], [(hT[:, k, t * P:(t + 1) * P], w[:, k, :]) for k in range(KD)])\
                        .then_inc(sem(f"mm_qkv_{l}"), 1)
                    if n == 2 and t == 0:
                        pe.wait_ge(*stage(f"a_ready_{l}", 1))
                        for d in range(2):
                            mms(ps[:, 4, d * 64:(d + 1) * 64], [(tri[d], dts[:, 1, d])])
                        mms(ps[:, 4, 128:256], [(ones, dts[:, 1])]).then_inc(sem(f"mm_cum_{l}"), 1)
                    if n == 2 and t >= 1:
                        q_transposes(t - 1)
                q_transposes(TILES - 1)

                def z_product(i):
                    q, k = i // KD, i % KD
                    n, t = q // nt, q % nt
                    w, ready = chunk(l, "z", n)
                    if k == 0:
                        pe.wait_ge(*ready)
                        if q:
                            pe.wait_ge(*stage(f"ev_z_{l}", q))
                    m = nc.tensor.matmul(ps[:, 7, :], hT[:, k, t * P:(t + 1) * P], w[:, k, :], start=k == 0, stop=k == KD - 1)
                    if k == KD - 1:
                        m.then_inc(sem(f"mm_z_{l}"), 1)

                pe.wait_ge(phase, phase_start(l, "attn"))
                units = attn_units(l)

                def keys(t):
                    return (0, TILES) if t < LAT_TILES else (LAT_TILES, TILES)

                for i in range(len(units) + 2):
                    if i < len(units):
                        t, ty, g, h = units[i]
                        k0, k1 = keys(t)
                        if i >= 3:
                            pe.wait_ge(*stage(f"prob_{l}", i - 2))
                        o = ps[:, i % 3, 0:(k1 - k0) * P]
                        part = slice(g * HD, (g + 1) * HD)
                        masked = ty == 1 and t < LAT_TILES
                        m = nc.tensor.matmul(o, qT[part, ty, h, t * P:(t + 1) * P], kT[part, ty, k0 * P:k1 * P], start=True, stop=not masked)
                        if masked:
                            neg = cst[:, C_NA:C_NA + P] if t == 0 else cst[:, C_NB:C_NB + P]
                            m = nc.tensor.matmul(ps[:, i % 3, (1 - t) * P:(2 - t) * P], ident, neg, start=False, stop=True)
                        m.then_inc(sem(f"mm_score_{l}"), 1)
                    if 1 <= i <= len(units):
                        j = i - 1
                        t = units[j][0]
                        k0, k1 = keys(t)
                        pe.wait_ge(*stage(f"prob_{l}", j + 1))
                        if j >= 2:
                            pe.wait_ge(*stage(f"ev_pT_{l}", j - 1))
                        transposes(3 + j % 2, [pr[:, j % 2, c * P:(c + 1) * P] for c in range(k1 - k0)]).then_inc(sem(f"mm_pT_{l}"), 1)
                    if i >= 2:
                        j = i - 2
                        t, ty, g, h = units[j]
                        k0, k1 = keys(t)
                        pe.wait_ge(*stage(f"ev_pT_{l}", j + 1))
                        grp, hh = j // HEADS, j % HEADS
                        if hh == 0 and grp >= 2:
                            pe.wait_ge(*stage(f"ev_o_{l}", grp - 1))
                        v0 = ty * 768 + 640 + g * HD
                        mms(ps[:, 5 + grp % 2, hh * HD:(hh + 1) * HD],
                            [(pT[:, j % 2, c * P:(c + 1) * P], qk[:, k0 + c, v0:v0 + HD]) for c in range(k1 - k0)])\
                            .then_inc(sem(f"mm_pv_{l}"), 1)
                    if i < 2 * nt * KD:
                        z_product(i)
                for t in range(nt):
                    pe.wait_ge(*stage(f"ev_o_{l}", 2 * (t + 1)))
                    for ty in range(2):
                        u = 2 * t + ty
                        if u >= 2:
                            pe.wait_ge(*stage(f"ev_oT_{l}", u - 1))
                        if u == 0:
                            pe.wait_ge(*stage(f"ev_pT_{l}", len(units)))
                        transposes(3 + u % 2, [qk[:, t, ty * 768 + c * P:ty * 768 + (c + 1) * P] for c in range(4)])\
                            .then_inc(sem(f"mm_oT_{l}"), 1)

                pe.wait_ge(phase, phase_start(l, "ssd"))
                ny = ns = 0
                sets = range(2 * l + 1, sets_before(l + 1))
                mod_jobs = [(m, n) for m in sets for n in range(6)]
                for i, (s, d, t) in enumerate(scan_steps(l)):
                    if i >= 2 and mod_jobs:
                        mod_chunk(*mod_jobs.pop(0))
                    if s < 3:
                        pe.wait_ge(*stage(f"xw_{l}", ns + 1))
                        if ns >= 2:
                            pe.wait_ge(*stage(f"state_{l}", ns - 1))
                        for g in range(SG):
                            m = mms(ps[:, 2 + 2 * (ns % 2) + g, :], [(btok[:, t, g * SN:(g + 1) * SN], xw[:, ns % 2, g * NCH:(g + 1) * NCH])])
                        m.then_inc(sem(f"mm_state_{l}"), 1)
                        ns += 1
                    if s > 0 and t < nt:
                        pe.wait_ge(*stage(f"state_{l}", 2 * (s - 1) + d + 1))
                        if ny:
                            pe.wait_ge(*stage(f"ev_yoff_{l}", ny))
                        for g in range(SG):
                            m = mms(ps[:, g, :], [(bcc[:, 2 + g, t * P:(t + 1) * P], st[:, d, g * NCH:(g + 1) * NCH])])
                        m.then_inc(sem(f"mm_yoff_{l}"), 1)
                        ny += 1
                pe.wait_ge(*stage(f"scan_done_{l}", 1))
                q = 0
                for u in range(nt * SG + 1):
                    if u >= 2 and mod_jobs:
                        mod_chunk(*mod_jobs.pop(0))
                    for d in range(2):
                        if u < nt * SG:
                            t, g = u // SG, u % SG
                            if d == 0:
                                if u >= 1:
                                    pe.wait_ge(*stage(f"cbm_{l}", 2 * u))
                                mms(ps[:, 0, 0:P], [(bcc[:, g, t * P:(t + 1) * P], bcc[:, 2 + g, t * P:(t + 1) * P])]).then_inc(sem(f"mm_cb_{l}"), 1)
                            if q >= 2:
                                pe.wait_ge(*stage(f"diff_{l}", q - 1))
                            for h in range(8):
                                last = mms(ps[:, 1 + 2 * (q % 2) + h // 4, (h % 4) * P:(h % 4 + 1) * P],
                                           [(dts[:, 1, d, t, g * 8 + h:g * 8 + h + 1].to_broadcast([P, P]), tri[d])])
                            last.then_inc(sem(f"mm_r_{l}"), 1)
                            q += 1
                    if u >= 1:
                        pu = u - 1
                        t, g = pu // SG, pu % SG
                        pe.wait_ge(*stage(f"m_ready_{l}", 2 * u))
                        if pu >= 2:
                            pe.wait_ge(*stage(f"ev_y_{l}", pu - 1))
                        for h in range(8):
                            for d in range(2):
                                hh = g * 8 + h
                                last = nc.tensor.matmul(ps[:, 5 + pu % 2, h * HD:(h + 1) * HD], mt[:, (2 * pu + d) % 3, h, :],
                                                        xs[:, t, hh * HD:(hh + 1) * HD], start=d == 0, stop=d == 1)
                        last.then_inc(sem(f"mm_y_{l}"), 1)

                def row_transposes(name, tiles, src):
                    for t in range(tiles):
                        pe.wait_ge(*stage(f"{name}_rows_{l}", t + 1))
                        for b in range(2):
                            u = 2 * t + b
                            if u >= 4:
                                pe.wait_ge(*stage(f"ev_{name}_{l}", u - 3))
                            transposes(4 + u % 4, [src[:, t, (4 * b + i) * P:(4 * b + i + 1) * P] for i in range(4)])\
                                .then_inc(sem(f"mm_{name}_{l}"), 1)

                assert not mod_jobs
                pe.wait_ge(phase, phase_start(l, "gn"))
                row_transposes("gn", nt, y)

                pe.wait_ge(phase, phase_start(l, "merge"))
                u = 0
                for bn in range(6):
                    b, n = bn // 2, bn % 2
                    wg, g_ready = chunk(l, "gate", bn)
                    wb, b_ready = chunk(l, "br", bn)
                    pe.wait_ge(*g_ready)
                    pe.wait_ge(*b_ready)
                    src = [(oT, 0, 4), (oT, 4, 4), (ysT, 0, 8)][b]
                    for t in range(nt):
                        if u >= 2:
                            pe.wait_ge(*stage(f"gated_{l}", u - 1))
                        mms(ps[:, u % 2, :], [(hT[:, k, t * P:(t + 1) * P], wg[:, k, :]) for k in range(KD)]).then_inc(sem(f"mm_gate_{l}"), 1)
                        mms(ps[:, 2 + u % 2, :], [(src[0][:, src[1] + k, t * P:(t + 1) * P], wb[:, k, :]) for k in range(src[2])])\
                            .then_inc(sem(f"mm_br_{l}"), 1)
                        u += 1
                row_transposes("mg", nt, acc)

                pe.wait_ge(phase, phase_start(l, "out"))
                for u, (n, t) in enumerate([(n, t) for t in range(nt) for n in range(2)]):
                    w, ready = chunk(l, "out", n)
                    pe.wait_ge(*ready)
                    if u >= 2:
                        pe.wait_ge(*stage(f"ev_out_{l}", u - 1))
                    mms(ps[:, u % 2, :], [(mT[:, k, t * P:(t + 1) * P], w[:, k, :]) for k in range(KD)]).then_inc(sem(f"mm_out_{l}"), 1)

                norm(1, nt)

                pe.wait_ge(phase, phase_start(l, "router"))
                pe.wait_ge(param, params_at(l, 1))
                for t in range(nt):
                    last = mms(ps[:, 0, t * N_EXP:(t + 1) * N_EXP], [(hT[:, k, t * P:(t + 1) * P], wr[:, k, :]) for k in range(KD)])
                last.then_inc(sem(f"mm_router_{l}"), 1)

                pe.wait_ge(*stage(f"weights2_{l}", 48))
                wgu = esl[:, 2, 0:2, :].rearrange("p a (k n) -> p k a n", n=D_EXP)
                for t in range(nt):
                    mms(ps[:, 4 + t, :].rearrange("p (a n) -> p a n", a=2), [(hT[:, k, t * P:(t + 1) * P], wgu[:, k]) for k in range(KD)])\
                        .then_inc(sem(f"mm_sgu_{l}"), 1)

                pe.wait_ge(*stage(f"masks_{l}", 1))
                for t in range(nt):
                    mms(ps[:, 1, t * N_EXP:(t + 1) * N_EXP], [(UT, rtr[:, 8, t, :])] + [(ones, rtr[:, 8, i, :]) for i in range(t)])
                mms(ps[0:N_EXP, 0, 0:1], [(rtr[:, 8, t, :], cst[:, C_ONE:C_ONE + 1]) for t in range(nt)]).then_inc(sem(f"mm_rank_{l}"), 1)

                pe.wait_ge(*stage(f"shid_{l}", nt))
                for t in range(nt):
                    b = t % 2
                    if t:
                        pe.wait_ge(*stage(f"ev_shT_{l}", t))
                    transposes(2, [shs[:, t, c * P:(c + 1) * P] for c in range(2)]).then_inc(sem(f"mm_shT_{l}"), 1)
                    pe.wait_ge(*stage(f"ev_shT_{l}", t + 1))
                    if t >= 2:
                        pe.wait_ge(*stage(f"ev_sy_{l}", t - 1))
                    for n in range(2):
                        m = mms(ps[:, 4 + 2 * b + n, :], [(hgT[:, b, c, :], esl[:, 2, 2, c * D + n * NCH:c * D + (n + 1) * NCH]) for c in range(2)])
                    m.then_inc(sem(f"mm_sdown_{l}"), 1)

                pe.wait_ge(phase, phase_start(l, "moe"))

                pe.wait_ge(*stage(f"tab_read_{l}", 16))
                for b in range(BLOCKS):
                    m = nc.tensor.transpose(ps[:, 0, b * N_EXP:(b + 1) * N_EXP], tsb[:, b * P:(b + 1) * P], cst[0:N_EXP, C_ID:C_ID + N_EXP])
                m.then_inc(sem(f"mm_tab_{l}"), 1)
                pe.wait_ge(*stage(f"flags_{l}", 1))
                e64 = slice(0, N_EXP)
                mms(ps[e64, 1, 0:3], [(cst[e64, C_UT:C_UT + N_EXP], stat[e64, 0, 0:3])])
                mms(ps[e64, 1, 3:6], [(cst[e64, C_ONE:C_ONE + 1].to_broadcast([N_EXP, N_EXP]), stat[e64, 0, 0:3])]).then_inc(sem(f"mm_pos_{l}"), 1)
                pe.wait_ge(*stage(f"places_{l}", 1))
                xoh = stat[e64, 4:6, :].rearrange("p a n -> p (a n)")[:, 0:96].rearrange("p (b n) -> p b n", n=32)
                mms(ps[0:1, 2, 0:32], [(cst[e64, C_EID:C_EID + 1], xoh[:, b, :]) for b in range(BLOCKS - 1)])
                mms(ps[0:1, 2, 32:64], [(cst[e64, C_COL + b:C_COL + b + 1], xoh[:, b, :]) for b in range(BLOCKS - 1)]).then_inc(sem(f"mm_list_{l}"), 1)

                def x_transposes(slot):
                    for b in range(2):
                        m = transposes(b, [xg[slot][:, (4 * b + c) * P:(4 * b + c + 1) * P] for c in range(4)])
                    return m

                def gate_up(par, slot):
                    wgu = esl[:, slot, 0:2, :].rearrange("p a (k n) -> p k a n", n=D_EXP)
                    return mms(ps[:, 2, :].rearrange("p (a n) -> p a n", a=2), [(xgT[:, par, k, :], wgu[:, k]) for k in range(KD)])

                def down(par, slot):
                    for n in range(2):
                        m = mms(ps[:, 4 + n, :], [(hgT[:, par, c, :], esl[:, slot, 2, c * D + n * NCH:c * D + (n + 1) * NCH]) for c in range(2)])
                    return m

                def do_xT(e, j, rounds, first=False):
                    pe.wait_ge(*stage(f"gath{j % 4}_{l}", rounds * 16))
                    if not first:
                        pe.wait_ge(*stage(f"ev_xa_{l}", e))
                        pe.wait_ge(*stage(f"ev_xv_{l}", e))
                    x_transposes(j % 4).then_inc(sem(f"mm_xT_{l}"), 1)

                def do_gu(e, j, loads, first=False):
                    pe.wait_ge(*stage(f"ev_xa_{l}", e + 1))
                    pe.wait_ge(*stage(f"ev_xv_{l}", e + 1))
                    pe.wait_ge(*stage(f"weights{j}_{l}", loads * 48))
                    if not first:
                        pe.wait_ge(*stage(f"hidden_{l}", e))
                    gate_up(j % 2, j).then_inc(sem(f"mm_gu_{l}"), 1)

                def do_hT(e, j, first=False):
                    pe.wait_ge(*stage(f"hidden_{l}", e + 1))
                    if not first:
                        pe.wait_ge(*stage(f"ev_hT_{l}", e))
                    transposes(3, [hsg[:, j % 2, c * P:(c + 1) * P] for c in range(2)]).then_inc(sem(f"mm_hT_{l}"), 1)

                def do_down(e, j, first=False):
                    pe.wait_ge(*stage(f"ev_hT_{l}", e + 1))
                    if not first:
                        pe.wait_ge(*stage(f"ev_ya_{l}", e))
                        pe.wait_ge(*stage(f"ev_yv_{l}", e))
                    down(j % 2, j).then_inc(sem(f"mm_down_{l}"), 1)

                def step(e, r, j):
                    do_gu(e, j, r + (2 if j == 2 else 1), first=isinstance(e, int) and e == 0)
                    if not (isinstance(e, int) and e == 0):
                        do_hT(e - 1, (j + 3) % 4, first=isinstance(e, int) and e == 1)
                    if not (isinstance(e, int) and e == N_EXP - 1):
                        do_xT(e + 1, j + 1, r + ((j + 1) // 4 + 1))
                    if not (isinstance(e, int) and e == 0):
                        do_down(e - 1, (j + 3) % 4, first=isinstance(e, int) and e == 1)

                do_xT(0, 0, 1, first=True)
                for e in range(4):
                    step(e, 0, e)
                with pe.Fori(1, N_EXP // 4 - 1) as r:
                    for j in range(4):
                        step(r * 4 + j, r, j)
                for e in range(N_EXP - 4, N_EXP):
                    step(e, N_EXP // 4 - 1, e % 4)
                do_hT(N_EXP - 1, 3)
                do_down(N_EXP - 1, 3)

                n = pe.value_load(xl[0:1, 64:65], min_val=0, max_val=max_extra(l))
                with pe.Fori(0, extra_groups(l)) as o:
                    with pe.If(o * XG < n):
                        with pe.Fori(0, XG) as k:
                            i = o * XG + k
                            with pe.If(i < n):
                                xstep = sem(f"x_step_{l}")
                                pe.wait_ge(sem(f"x_gath_{l}"), i * 16 + 16)
                                pe.wait_ge(xstep, i * XSTEPS + (X0 + 1))
                                x_transposes(0).then_inc(xstep, 1)
                                pe.wait_ge(xstep, i * XSTEPS + (X0 + 3))
                                pe.wait_ge(sem(f"x_weights_{l}"), i * 48 + 48)
                                gate_up(0, 0).then_inc(xstep, 1)
                                pe.wait_ge(xstep, i * XSTEPS + (X0 + 6))
                                transposes(3, [hsg[:, 0, c * P:(c + 1) * P] for c in range(2)]).then_inc(xstep, 1)
                                pe.wait_ge(xstep, i * XSTEPS + (X0 + 8))
                                down(0, 0).then_inc(xstep, 1)

        @block.scalar
        def _(act):
            do = Steps(act, sem("act_order"))
            nc_a = nc.scalar
            act.wait_ge(sem("mm_cond"), 1)
            act.wait_ge(sem("x_loaded"), 32)
            do.run(nc_a.activation(cT[:, :], ps[:, 0, 0:16], ACT.Silu))
            nc_a.activation(cT[:, :], cT[:, :], ACT.Copy).then_inc(sem("cond_silu"), 1)
            act.sem_inc(sem("cond_silu"), 1)
            for l in range(DEPTH):
                nt = out_tiles[l]

                def end():
                    act.wait_ge(do.own, do.n.get(do.own.name, 0))
                    act.sem_inc(phase, 1)

                def mod_evac(m, n):
                    act.wait_ge(sem("mm_ada"), 6 * m + n + 1)
                    if 6 * m + n:
                        act.wait_ge(sem("products_stored"), 16 * (6 * m + n))
                    do.run(nc_a.activation(mstg[:, :], ps[0:2, 7 - n % 2 if m == 0 else 7, :], ACT.Copy), sem("ev_mod"))

                def rstd(src, n, waits, ready):
                    act.wait_ge(*waits)
                    do.run(nc_a.activation(stat[:, 2, 0:n], stat[:, 1, 0:n], ACT.Sqrt), ready)

                def norm_squares(half, tiles):
                    for t in range(tiles):
                        if half:
                            act.wait_ge(*stage(f"xup_out_{l}", t + 1))
                        elif l:
                            act.wait_ge(*stage(f"xup_post_{l - 1}", t + 1))
                        do.run(nc_a.activation(hn[:, 0, :], x[:, t, :], ACT.Square, accum_out=stat[:, 0, t:t + 1]), sem(f"sq_norm{half}_{l}"))

                def norm(half, tiles):
                    kind = f"norm{half}"
                    if (l, half) != (0, 0):
                        norm_squares(half, tiles)
                    act.wait_ge(phase, phase_start(l, kind))
                    if half == 0:
                        act.wait_ge(*stage(f"mm_ccol_{l}", 1))
                        do.run(nc_a.activation(ccol[:, :], ps[:, 6, 0:48], ACT.Copy))
                    rstd(None, tiles, stage(f"inv_{kind}_{l}", 1), sem(f"rstd_{kind}_{l}"))
                    for u in range(2 * tiles):
                        t, b = u // 2, u % 2
                        act.wait_ge(*stage(f"mm_{kind}_{l}", u + 1))
                        do.run(nc_a.activation(hT[:, 4 * b:4 * b + 4, t * P:(t + 1) * P],
                                               ps[:, u % 4, :].rearrange("p (k n) -> p k n", n=P), ACT.Copy), sem(f"ev_{kind}_{l}"))
                    act.sem_inc(phase, 1)

                if l == 0:
                    norm_squares(0, TILES)
                    for n in range(6):
                        mod_evac(0, n)
                    act.sem_inc(phase, 1)
                norm(0, TILES)

                act.wait_ge(phase, phase_start(l, "inproj"))
                act.wait_ge(*stage(f"xp_zero_{l}", 2))
                for ct in range(CONV_T + 1):
                    if ct < CONV_T:
                        act.wait_ge(*stage(f"mm_xbc_{l}", ct + 1))
                        if ct >= 2:
                            act.wait_ge(*stage(f"conv_{l}", ct - 1))
                        do.run(nc_a.activation(xp[ct % 2][:, :, 1:SEG + 1], ps[:, ct % 2, :].rearrange("p (s n) -> p s n", s=2), ACT.Copy),
                               sem(f"conv_in_{l}"))
                    if ct >= 1:
                        c = ct - 1
                        act.wait_ge(*stage(f"conv_{l}", c + 1))
                        if c >= 2 and c < 8:
                            act.wait_ge(*stage(f"mm_uT_{l}", c - 1))
                        dst = cu[:, c % 2, :] if c < 8 else bcc[:, c - 8, :]
                        do.run(nc_a.activation(dst, cacc[:, c % 2, :], ACT.Silu), sem(f"conv_u_{l}"))
                e = 0

                def evac_qT(t):
                    nonlocal e
                    for ty in range(2):
                        for part in range(2):
                            if part == 0 and not has_q(l, t):
                                continue
                            act.wait_ge(*stage(f"mm_qT_{l}", e + 1))
                            if part == 0:
                                ins = nc_a.activation(qT[:, ty, :, t * P:(t + 1) * P], ps[:, e % 4, :].rearrange("p (h n) -> p h n", n=P), ACT.Copy)
                            else:
                                ins = nc_a.activation(kT[:, ty, t * P:(t + 1) * P], ps[:, e % 4, 0:P], ACT.Copy)
                            do.run(ins, sem(f"ev_qT_{l}"))
                            e += 1

                do.run(nc_a.activation(alog[:, :], alog[:, :], ACT.Exp), sem(f"expA_{l}"))
                act.wait_ge(*stage(f"nabs_{l}", 1))
                do.run(nc_a.activation(dts[:, 7], dts[:, 7], ACT.Exp), sem(f"softexp_{l}"))
                act.wait_ge(*stage(f"onep_{l}", 1))
                do.run(nc_a.activation(dts[:, 3], dts[:, 8], ACT.Ln), sem(f"softln_{l}"))
                for u, (n, t) in enumerate(qkv_units(l)):
                    act.wait_ge(*stage(f"mm_qkv_{l}", u + 1))
                    do.run(nc_a.activation(qk[:, t, n * NCH:(n + 1) * NCH], ps[:, 5 + u % 3, :], ACT.Copy), sem(f"ev_proj_{l}"))
                    if n == 2:
                        if t == 0:
                            act.wait_ge(*stage(f"cum_{l}", 1))
                            do.mark(nc_a.activation(dts[:, 4], dts[:, 2], ACT.Exp))
                            do.mark(nc_a.activation(dts[:, 5], dts[:, 5], ACT.Exp))
                            do.mark(nc_a.activation(dts[:, 6], dts[:, 3], ACT.Exp), sem(f"decays_{l}"))
                        act.wait_ge(*stage(f"inv_qk_{l}", t + 1))
                        do.run(nc_a.activation(stat[:, 2, t * 10:(t + 1) * 10], stat[:, 1, t * 10:(t + 1) * 10], ACT.Sqrt), sem(f"rstd_qk_{l}"))
                        if t >= 1:
                            evac_qT(t - 1)
                evac_qT(TILES - 1)
                act.sem_inc(phase, 1)

                act.wait_ge(phase, phase_start(l, "attn"))
                units = attn_units(l)
                for i in range(len(units) + 1):
                    if i and i % KD == 0 and i <= 2 * nt * KD:
                        q = i // KD - 1
                        act.wait_ge(*stage(f"mm_z_{l}", q + 1))
                        do.run(nc_a.activation(zs[:, q % nt, q // nt * NCH:(q // nt + 1) * NCH], ps[:, 7, :], ACT.Copy), sem(f"ev_z_{l}"))
                    if i < len(units):
                        t = units[i][0]
                        n = (TILES if t < LAT_TILES else CTX_TILES) * P
                        act.wait_ge(*stage(f"negmax_{l}", i + 1))
                        if i >= 2:
                            act.wait_ge(*stage(f"mm_pT_{l}", i - 1))
                        col = i % 16
                        if i >= 16 and i % 8 == 0:
                            act.wait_ge(*stage(f"ev_o_{l}", i // 8 - 1))
                        do.run(nc_a.activation(pr[:, i % 2, 0:n], ps[:, i % 3, 0:n], ACT.Exp, bias=stat[:, 3, col:col + 1], scale=SCALE,
                                               accum_out=stat[:, 4, col:col + 1]), sem(f"prob_{l}"))
                        if i % 8 == 7 and units[i][1] == 1:
                            g8 = slice(col - 7, col + 1)
                            act.wait_ge(*stage(f"sinkarg_{l}", i // 16 + 1))
                            do.run(nc_a.activation(stat[:, 5, g8], stat[:, 5, g8], ACT.Exp), sem(f"sinkexp_{l}"))
                    if i >= 1:
                        j = i - 1
                        t = units[j][0]
                        n = (TILES if t < LAT_TILES else CTX_TILES) * P
                        act.wait_ge(*stage(f"mm_pT_{l}", j + 1))
                        if j >= 2:
                            act.wait_ge(*stage(f"mm_pv_{l}", j - 1))
                        do.run(nc_a.activation(pT[:, j % 2, 0:n], ps[:, 3 + j % 2, 0:n], ACT.Copy), sem(f"ev_pT_{l}"))
                for u in range(2 * nt):
                    t, ty = u // 2, u % 2
                    act.wait_ge(*stage(f"mm_oT_{l}", u + 1))
                    do.run(nc_a.activation(oT[:, 4 * ty:4 * ty + 4, t * P:(t + 1) * P], ps[:, 3 + u % 2, :].rearrange("p (k n) -> p k n", n=P), ACT.Copy),
                           sem(f"ev_oT_{l}"))
                act.sem_inc(phase, 1)

                act.wait_ge(phase, phase_start(l, "ssd"))
                for t in range(nt):
                    do.run(nc_a.activation(zs[:, t, :], zs[:, t, :], ACT.Silu), sem(f"silu_z_{l}"))
                sets = range(2 * l + 1, sets_before(l + 1))
                mod_jobs = [(m, n) for m in sets for n in range(6)]
                for _ in range(6):
                    mod_evac(*mod_jobs.pop(0))
                for q in range(2 * SG * nt):
                    if q % 2 == 0 and q >= 4 and mod_jobs:
                        mod_evac(*mod_jobs.pop(0))
                    act.wait_ge(*stage(f"diff_{l}", q + 1))
                    m3 = mt[:, q % 3]
                    do.run(nc_a.activation(m3, m3, ACT.Exp), sem(f"expd_{l}"))
                act.sem_inc(phase, 1)

                act.wait_ge(phase, phase_start(l, "gn"))
                for t in range(nt):
                    act.wait_ge(*stage(f"yz_{l}", t + 1))
                    for g in range(SG):
                        do.run(nc_a.activation(junk[:, 0:NCH], y[:, t, g * NCH:(g + 1) * NCH], ACT.Square,
                                               accum_out=stat[:, 0, 2 * t + g:2 * t + g + 1]), sem(f"sq_gn_{l}"))
                rstd(None, 2 * nt, stage(f"inv_gn_{l}", 1), sem(f"rstd_gn_{l}"))

                def evac_rows(name, dst):
                    for u in range(2 * nt):
                        t, b = u // 2, u % 2
                        act.wait_ge(*stage(f"mm_{name}_{l}", u + 1))
                        do.run(nc_a.activation(dst[:, 4 * b:4 * b + 4, t * P:(t + 1) * P],
                                               ps[:, 4 + u % 4, :].rearrange("p (k n) -> p k n", n=P), ACT.Copy), sem(f"ev_{name}_{l}"))

                evac_rows("gn", ysT)
                act.sem_inc(phase, 1)

                act.wait_ge(phase, phase_start(l, "merge"))
                for u in range(6 * nt):
                    act.wait_ge(*stage(f"mm_gate_{l}", u + 1))
                    if u >= 2:
                        act.wait_ge(*stage(f"gated_{l}", u - 1))
                    do.run(nc_a.activation(gs[:, u % 2, :], ps[:, u % 2, :], ACT.Sigmoid), sem(f"gate_{l}"))
                evac_rows("mg", mT)
                act.sem_inc(phase, 1)

                act.wait_ge(phase, phase_start(l, "out"))
                for u, (n, t) in enumerate([(n, t) for t in range(nt) for n in range(2)]):
                    act.wait_ge(*stage(f"mm_out_{l}", u + 1))
                    do.run(nc_a.activation(ml[:, t, n * NCH:(n + 1) * NCH], ps[:, u % 2, :], ACT.Copy), sem(f"ev_out_{l}"))
                    if n == 1:
                        do.run(nc_a.activation(junk[:, :], ml[:, t, :], ACT.Square, accum_out=stat[:, 0, t:t + 1]), sem(f"sq_out_{l}"))

                def post(name, src):
                    for t in range(nt if name == "post" else 0):
                        act.wait_ge(*stage(f"combined_{l}", 4 * (t + 1)))
                        do.run(nc_a.activation(junk[:, :], src[:, t, :], ACT.Square, accum_out=stat[:, 0, t:t + 1]), sem(f"sq_{name}_{l}"))
                    rstd(None, nt, stage(f"inv_{name}_{l}", 1), sem(f"rstd_{name}_{l}"))
                    act.sem_inc(phase, 1)

                post("out", ml)
                norm(1, nt)

                act.wait_ge(phase, phase_start(l, "router"))
                act.wait_ge(*stage(f"mm_router_{l}", 1))
                do.run(nc_a.activation(rtr[:, 0, 0:nt, :], ps[:, 0, 0:nt * N_EXP].rearrange("p (t n) -> p t n", n=N_EXP), ACT.Sigmoid), sem(f"scores_{l}"))
                for t in range(nt):
                    act.wait_ge(*stage(f"mm_sgu_{l}", t + 1))
                    do.run(nc_a.activation(shs[:, t, :], ps[:, 4 + t, 0:D_EXP], ACT.Silu), sem(f"ssilu_{l}"))
                for t in range(nt):
                    b = t % 2
                    act.wait_ge(*stage(f"mm_shT_{l}", t + 1))
                    if t == 0:
                        for i in range(2):
                            act.wait_ge(*stage(f"h_written{i}_{l}", 16 * nt // 2))
                    do.run(nc_a.activation(hgT[:, b, :, :], ps[:, 2, 0:2 * P].rearrange("p (c n) -> p c n", n=P), ACT.Copy), sem(f"ev_shT_{l}"))
                    act.wait_ge(*stage(f"mm_sdown_{l}", t + 1))
                    do.run(nc_a.activation(acc[:, t, :], ps[:, 4 + 2 * b:6 + 2 * b, :].rearrange("p a n -> p (a n)"), ACT.Copy), sem(f"ev_sy_{l}"))
                act.sem_inc(phase, 1)

                act.wait_ge(phase, phase_start(l, "moe"))

                def ev_x(e, par):
                    act.wait_ge(*stage(f"mm_xT_{l}", e + 1))
                    nc_a.activation(xgT[:, par, 0:4, :], ps[:, 0, :].rearrange("p (k n) -> p k n", n=P), ACT.Copy).then_inc(sem(f"ev_xa_{l}"), 1)

                def ev_hidden(e, j):
                    act.wait_ge(*stage(f"mm_hT_{l}", e + 1))
                    nc_a.activation(hgT[:, j % 2, :, :], ps[:, 3, 0:2 * P].rearrange("p (c n) -> p c n", n=P), ACT.Copy).then_inc(sem(f"ev_hT_{l}"), 1)

                def rows_out(e, j, scat):
                    act.wait_ge(*stage(f"mm_down_{l}", e + 1))
                    if scat is not None:
                        act.wait_ge(*stage(f"scat{j}_{l}", scat))
                    nc_a.activation(ysb[j][:, 0:NCH], ps[:, 4, :], ACT.Copy).then_inc(sem(f"ev_ya_{l}"), 1)

                def step(e, r, j):
                    act.wait_ge(*stage(f"mm_gu_{l}", e + 1))
                    nc_a.activation(hsg[:, j % 2, :], ps[:, 2, 0:D_EXP], ACT.Silu).then_inc(sem(f"silu_{l}"), 1)
                    static = isinstance(e, int)
                    if not (static and e == 0):
                        ev_hidden(e - 1, (j + 3) % 4)
                    if not (static and e == N_EXP - 1):
                        ev_x(e + 1, (j + 1) % 2)
                    if not (static and e == 0):
                        rows_out(e - 1, (j + 3) % 4, None if static and e < 5 else r * 16 + 16 * ((j - 5) // 4 + 1))

                ev_x(0, 0)
                for e in range(5):
                    step(e, 0, e)
                with act.Fori(1, N_EXP // 4 - 2) as r:
                    for j in range(1, 5):
                        step(r * 4 + j, r, j)
                for e in range(N_EXP - 7, N_EXP):
                    step(e, e // 4, e % 4)
                ev_hidden(N_EXP - 1, 3)
                rows_out(N_EXP - 1, 3, 16 * ((N_EXP - 5) // 4 + 1))

                act.wait_ge(*stage(f"list_ready_{l}", 1))
                n = act.value_load(xl[0:1, 64:65], min_val=0, max_val=max_extra(l))
                with act.Fori(0, extra_groups(l)) as o:
                    with act.If(o * XG < n):
                        with act.Fori(0, XG) as k:
                            i = o * XG + k
                            with act.If(i < n):
                                xstep = sem(f"x_step_{l}")
                                act.wait_ge(xstep, i * XSTEPS + (X0 + 2))
                                nc_a.activation(xgT[:, 0, :, :], ps[:, 0:2, :].rearrange("p a (k n) -> p (a k) n", n=P), ACT.Copy).then_inc(xstep, 1)
                                act.wait_ge(xstep, i * XSTEPS + (X0 + 4))
                                nc_a.activation(hsg[:, 0, :], ps[:, 2, 0:D_EXP], ACT.Silu).then_inc(xstep, 1)
                                act.wait_ge(xstep, i * XSTEPS + (X0 + 7))
                                nc_a.activation(hgT[:, 0, :, :], ps[:, 3, 0:2 * P].rearrange("p (c n) -> p c n", n=P), ACT.Copy).then_inc(xstep, 1)
                                act.wait_ge(xstep, i * XSTEPS + (X0 + 9))
                                nc_a.activation(ysb[0][:, :], ps[:, 4:6, :].rearrange("p a n -> p (a n)"), ACT.Copy).then_inc(xstep, 1)
                act.wait_ge(*stage(f"ev_ya_{l}", N_EXP))
                act.sem_inc(phase, 1)

                post("post", acc)

        @block.vector
        def _(dve):
            do = Steps(dve, sem("dve_order"))
            v = nc.vector
            dve.wait_ge(sem("x_loaded"), 32)
            for l in range(DEPTH):
                nt = out_tiles[l]

                def end():
                    dve.sem_inc(phase, 1)

                def modulation(m):
                    dve.wait_ge(sem("mod_params"), 16 * 11 * (m + 1))
                    do.run(v.scalar_tensor_tensor(mrow[:, :], mrow[:, :], cst[0:48, C_MOD:C_MOD + 1], mbias[:, :], ALU.add, ALU.add))
                    do.run(v.tensor_tensor(mrow[:, :], mrow[:, :], mgain[:, :], ALU.mult), sem("mod_done"))

                def clear_gains():
                    do.run(v.memset(mgain[:, :], 1.0), sem("mod_cleared"))

                def inverse_ms(n, width, ready):
                    do.run(v.tensor_scalar(stat[:, 0, 0:n], stat[:, 0, 0:n], 1.0 / width, EPS, ALU.mult, ALU.add))
                    do.run(v.reciprocal(stat[:, 1, 0:n], stat[:, 0, 0:n]), ready)

                def norm(half, tiles):
                    kind = f"norm{half}"
                    dve.wait_ge(phase, phase_start(l, kind))
                    if half == 0:
                        dve.wait_ge(param, params_at(l, 0))
                        do.run(v.tensor_scalar(nsink[:, :], nsink[:, :], -1.0, None, ALU.mult))
                    dve.wait_ge(*stage(f"sq_{kind}_{l}", tiles))
                    inverse_ms(tiles, D, sem(f"inv_{kind}_{l}"))
                    dve.wait_ge(*stage(f"rstd_{kind}_{l}", 1))
                    dve.wait_ge(sem("mod_loaded"), 16 * (2 * l + half + 1))
                    for t in range(tiles):
                        s = 0 if t < LAT_TILES else 1
                        if t >= 2:
                            dve.wait_ge(*stage(f"mm_{kind}_{l}", 2 * (t - 1)))
                            if half:
                                dve.wait_ge(*stage(f"h_written{t % 2}_{l}", 16 * (t // 2)))
                        do.run(v.scalar_tensor_tensor(hn[:, t % 2, :], x[:, t, :], stat[:, 2, t:t + 1], bc[:, 1, s, :], ALU.mult, ALU.mult))
                        do.run(v.tensor_tensor(hn[:, t % 2, :], hn[:, t % 2, :], bc[:, 0, s, :], ALU.add), sem(f"hn_{kind}_{l}"))
                    end()

                if l == 0:
                    clear_gains()
                    dve.wait_ge(cond, 48)
                    modulation(0)
                    end()
                norm(0, TILES)

                dve.wait_ge(phase, phase_start(l, "inproj"))
                for i in range(2):
                    do.run(v.memset(xp[i][:, :, :], 0.0), sem(f"xp_zero_{l}"))

                def evac_uT(ct):
                    dve.wait_ge(*stage(f"mm_uT_{l}", ct + 1))
                    dst = xs[:, :, ct * P:(ct + 1) * P] if ct < 8 else btok[:, :, (ct - 8) * P:(ct - 7) * P]
                    do.run(v.tensor_copy(dst, ps[:, 2 + ct % 2, :].rearrange("p (t n) -> p t n", n=P)), sem(f"ev_uT_{l}"))

                for ct in range(CONV_T):
                    dve.wait_ge(*stage(f"conv_in_{l}", ct + 1))
                    if ct >= 2:
                        dve.wait_ge(*stage(f"conv_u_{l}", ct - 1))
                    src = xp[ct % 2]
                    o = cacc[:, ct % 2, :].rearrange("p (s n) -> p s n", s=2)
                    wcol = lambda w: ccol[:, w * CONV_T + ct:w * CONV_T + ct + 1]
                    do.run(v.tensor_scalar(o, src[:, :, 1:SEG + 1], wcol(1), wcol(3), ALU.mult, ALU.add))
                    do.run(v.scalar_tensor_tensor(o, src[:, :, 0:SEG], wcol(0), o, ALU.mult, ALU.add))
                    do.run(v.scalar_tensor_tensor(o, src[:, :, 2:SEG + 2], wcol(2), o, ALU.mult, ALU.add), sem(f"conv_{l}"))
                    if ct >= 2:
                        evac_uT(ct - 2)
                dve.wait_ge(*stage(f"mm_dt_{l}", 1))
                for d in range(2):
                    do.run(v.tensor_tensor(dts[:, 0, d], ps[:, 4, 0:TILES * 32].rearrange("p (t d h) -> p d t h", d=2, h=SH)[:, d],
                                           dtb[:, d * SH:(d + 1) * SH].unsqueeze(1).to_broadcast([P, TILES, SH]), ALU.add))

                dt, aa, cum, tot, ein, eend, edec = (dts[:, i] for i in range(7))
                flat = lambda z: z.rearrange("p d t h -> p (d t h)")
                do.run(v.scalar_tensor_tensor(flat(dts[:, 7]), flat(dt), -1.0, flat(dt), ALU.mult, ALU.min), sem(f"nabs_{l}"))
                dve.wait_ge(*stage(f"softexp_{l}", 1))
                do.run(v.tensor_scalar(flat(dts[:, 8]), flat(dts[:, 7]), 1.0, None, ALU.add), sem(f"onep_{l}"))
                do.run(v.scalar_tensor_tensor(flat(dts[:, 4]), flat(dts[:, 8]), 1.0, flat(dts[:, 7]), ALU.subtract, ALU.subtract))
                do.run(v.reciprocal(flat(dts[:, 5]), flat(dts[:, 8])))
                do.run(v.scalar_tensor_tensor(flat(dts[:, 4]), flat(dts[:, 4]), -1.0, flat(dts[:, 5]), ALU.mult, ALU.mult))
                do.run(v.scalar_tensor_tensor(flat(dt), flat(dt), 0.0, flat(dts[:, 4]), ALU.max, ALU.add))
                dve.wait_ge(*stage(f"softln_{l}", 1))
                do.run(v.tensor_tensor(flat(dt), flat(dt), flat(tot), ALU.add))
                dve.wait_ge(*stage(f"expA_{l}", 1))
                for d in range(2):
                    do.run(v.tensor_tensor(aa[:, d], dt[:, d], alog[:, d * SH:(d + 1) * SH].unsqueeze(1).to_broadcast([P, TILES, SH]), ALU.mult))
                do.run(v.tensor_scalar(flat(aa), flat(aa), -1.0, None, ALU.mult), sem(f"a_ready_{l}"))
                dve.wait_ge(*stage(f"mm_cum_{l}", 1))
                do.run(v.tensor_copy(dts[:, 2:4].rearrange("p a d t h -> p (a d t h)"), ps[:, 4, 0:256]))
                do.run(v.tensor_tensor(flat(eend), flat(tot), flat(cum), ALU.subtract), sem(f"cum_{l}"))
                dve.wait_ge(*stage(f"decays_{l}", 1))
                do.run(v.tensor_tensor(flat(eend), flat(eend), flat(dt), ALU.mult))

                def rope(t, ty):
                    h0 = 0 if has_q(l, t) else HEADS
                    nh = 10 - h0
                    cur = qk[:, t, ty * 768 + h0 * HD:ty * 768 + 640]
                    heads = cur.rearrange("p (h d) -> p h d", d=HD)
                    if ty == 0:
                        r = stat[:, 2, t * 10 + h0:(t + 1) * 10].unsqueeze(2).to_broadcast([P, nh, HD])
                        do.run(v.tensor_tensor(heads, heads, r, ALU.mult))
                        do.run(v.tensor_tensor(cur, cur, gqk[:, h0 * HD:640], ALU.mult))
                    if t < LAT_TILES:
                        cosb = cst[:, C_COS + t * HD:C_COS + (t + 1) * HD].unsqueeze(1).to_broadcast([P, nh, HD])
                        sv = cst[:, C_SIN + t * HD:C_SIN + (t + 1) * HD].rearrange("p (x f j) -> p x f j", x=2, f=2)
                        hv = cur.rearrange("p (h x f j) -> p h x f j", x=2, f=2, j=16)
                        mv = rt[:, :].rearrange("p (h x f j) -> p h x f j", x=2, f=2, j=16)
                        for f in range(2):
                            for ax in range(2):
                                do.mark(v.tensor_tensor(mv[:, :, ax, f, :], hv[:, :, ax, 1 - f, :],
                                                        sv[:, ax, f, :].unsqueeze(1).to_broadcast([P, nh, 16]), ALU.mult))
                        dve.wait_ge(do.own, do.n[do.own.name])
                        do.run(v.tensor_tensor(heads, heads, cosb, ALU.mult))
                    u = tr_units(l).index((t, ty))
                    if u >= 2:
                        dve.wait_ge(*stage(f"mm_qT_{l}", sum(1 + has_q(l, tt) for tt, _ in tr_units(l)[:u - 1])))
                    if has_q(l, t):
                        qd = rq[:, u % 2, 0:512].rearrange("p (h g d) -> p g h d", g=KV, d=HD)
                        q4 = lambda z: z.rearrange("p (g h d) -> p g h d", g=KV, d=HD)
                        qs = q4(cur[:, 0:512])
                        do.mark(v.tensor_tensor(qd, qs, q4(rt[:, 0:512]), ALU.add) if t < LAT_TILES else v.tensor_copy(qd, qs))
                    ks, kd = cur[:, nh * HD - P:nh * HD], rq[:, u % 2, 512:640]
                    do.run(v.tensor_tensor(kd, ks, rt[:, 512:640], ALU.add) if t < LAT_TILES else v.tensor_copy(kd, ks), sem(f"roped_{l}"))

                for t in range(TILES):
                    dve.wait_ge(*stage(f"ev_proj_{l}", qkv_until(l, t)))
                    h0 = 0 if has_q(l, t) else HEADS
                    w = (10 - h0) * HD
                    src = qk[:, t, h0 * HD:640]
                    do.run(v.tensor_tensor(rt[:, 0:w], src, src, ALU.mult))
                    do.run(v.tensor_reduce(stat[:, 0, t * 10 + h0:(t + 1) * 10], rt[:, 0:w].rearrange("p (h d) -> p h d", d=HD), AX.X, ALU.add))
                    if h0:
                        do.run(v.memset(stat[:, 0, t * 10:t * 10 + h0], 1.0))
                    tile = slice(t * 10, (t + 1) * 10)
                    do.run(v.tensor_scalar(stat[:, 0, tile], stat[:, 0, tile], 1.0 / HD, EPS, ALU.mult, ALU.add))
                    do.run(v.reciprocal(stat[:, 1, tile], stat[:, 0, tile]), sem(f"inv_qk_{l}"))
                    dve.wait_ge(*stage(f"rstd_qk_{l}", t + 1))
                    if t == 0:
                        dve.wait_ge(sem("gqk_loaded"), 16 * (HEADS + KV) * (l + 1))
                    rope(t, 0)
                    rope(t, 1)
                end()

                dve.wait_ge(phase, phase_start(l, "attn"))
                units = attn_units(l)

                def finish_group(grp):
                    t, ty = grp // 2, grp % 2
                    c0 = (grp % 2) * 8
                    dve.wait_ge(*stage(f"mm_pv_{l}", 8 * (grp + 1)))
                    den = stat[:, 4, c0:c0 + 8]
                    if ty == 1:
                        dve.wait_ge(*stage(f"sinkexp_{l}", t + 1))
                        do.run(v.tensor_tensor(den, den, stat[:, 5, c0:c0 + 8], ALU.add))
                    do.run(v.reciprocal(stat[:, 6, 0:8], den))
                    o = qk[:, t, ty * 768:ty * 768 + 512].rearrange("p (h d) -> p h d", d=HD)
                    do.run(v.tensor_tensor(o, ps[:, 5 + grp % 2, :].rearrange("p (h d) -> p h d", d=HD),
                                           stat[:, 6, 0:8].unsqueeze(2).to_broadcast([P, HEADS, HD]), ALU.mult), sem(f"ev_o_{l}"))

                for i, (t, ty, g, h) in enumerate(units):
                    n = (TILES if t < LAT_TILES else CTX_TILES) * P
                    col = i % 16
                    dve.wait_ge(*stage(f"mm_score_{l}", i + 1))
                    do.run(v.tensor_reduce(stat[:, 7, col:col + 1], ps[:, i % 3, 0:n], AX.X, ALU.max, negate=True))
                    if ty == 0:
                        ins = v.tensor_scalar(stat[:, 3, col:col + 1], stat[:, 7, col:col + 1], SCALE, None, ALU.mult)
                    else:
                        ins = v.tensor_scalar(stat[:, 3, col:col + 1], stat[:, 7, col:col + 1], SCALE, nsink[:, i % 8:i % 8 + 1], ALU.mult, ALU.min)
                    do.run(ins, sem(f"negmax_{l}"))
                    if i % 8 == 7 and ty == 1:
                        do.run(v.tensor_tensor(stat[:, 5, 8:16], stat[:, 3, 8:16], nsink[:, :], ALU.subtract), sem(f"sinkarg_{l}"))
                    if i >= 3 and (i - 3) % 8 == 7:
                        finish_group((i - 3) // 8)
                finish_group(len(units) // 8 - 1)
                end()

                dve.wait_ge(phase, phase_start(l, "ssd"))
                clear_gains()
                perhead = lambda z: z.rearrange("p (h d) -> p h d", d=HD)
                hb = lambda z: z.unsqueeze(2).to_broadcast([P, SH, HD])
                for t in range(nt):
                    do.run(v.tensor_tensor(perhead(y[:, t, :]), perhead(xs[:, t, :]), hb(dsk[:, :]), ALU.mult))
                states = [(d, t) for s, d, t in scan_steps(l) if s < 3]

                def source_rows(i):
                    d, t = states[i]
                    if i >= 2:
                        dve.wait_ge(*stage(f"mm_state_{l}", i - 1))
                    do.mark(v.tensor_tensor(perhead(xw[:, i % 2, :]), perhead(xs[:, t, :]), hb(eend[:, d, t, :]), ALU.mult), sem(f"xw_{l}"))

                source_rows(0)
                ny = ns = 0
                for s, d, t in scan_steps(l):
                    if ns + 1 < len(states):
                        source_rows(ns + 1)
                    if s > 0 and t < nt:
                        dve.wait_ge(*stage(f"mm_yoff_{l}", ny + 1))
                        yo = mt[:, 0].rearrange("p a n -> p (a n)")
                        do.run(v.tensor_tensor(perhead(yo), ps[:, 0:2, :].rearrange("p a (h d) -> p (a h) d", d=HD), hb(ein[:, d, t, :]), ALU.mult),
                               sem(f"ev_yoff_{l}"))
                        do.run(v.tensor_tensor(y[:, t, :], y[:, t, :], yo, ALU.add))
                        ny += 1
                    if s < 3:
                        dve.wait_ge(*stage(f"mm_state_{l}", ns + 1))
                        bank = 2 + 2 * (ns % 2)
                        add = ps[:, bank:bank + 2, :].rearrange("p a n -> p (a n)")
                        if s == 0:
                            do.run(v.tensor_copy(st[:, d, :], add), sem(f"state_{l}"))
                        else:
                            if ny and t < nt:
                                dve.wait_ge(*stage(f"mm_yoff_{l}", ny))
                            do.run(v.tensor_tensor(perhead(st[:, d, :]), perhead(st[:, d, :]), hb(edec[:, d, t, :]), ALU.mult))
                            do.run(v.tensor_tensor(st[:, d, :], st[:, d, :], add, ALU.add), sem(f"state_{l}"))
                        ns += 1
                do.run(v.memset(stat[:, 6, 0:1], 0.0), sem(f"scan_done_{l}"))

                def decayed(q):
                    u, d = q // 2, q % 2
                    t, g = u // SG, u % SG
                    dve.wait_ge(*stage(f"expd_{l}", q + 1))
                    for h in range(8):
                        ins = v.scalar_tensor_tensor(mt[:, q % 3, h, :], mt[:, q % 3, h, :], dt[:, d, t, g * 8 + h:g * 8 + h + 1], cbm[:, d, :], ALU.mult, ALU.mult)
                        do.mark(ins, sem(f"m_ready_{l}")) if h == 7 else None

                def add_y(u):
                    t, g = u // SG, u % SG
                    dve.wait_ge(*stage(f"mm_y_{l}", u + 1))
                    yy = y[:, t, g * NCH:(g + 1) * NCH]
                    do.run(v.tensor_tensor(yy, yy, ps[:, 5 + u % 2, :], ALU.add), sem(f"ev_y_{l}"))

                NQ = 2 * SG * nt
                for q in range(NQ + 1):
                    if q == 3:
                        modulation(2 * l + 1)
                        if l + 1 < DEPTH:
                            dve.wait_ge(sem("mod_written"), 16 * (2 * l + 2))
                            clear_gains()
                    if q < NQ:
                        u, d = q // 2, q % 2
                        t, g = u // SG, u % SG
                        dve.wait_ge(*stage(f"mm_r_{l}", q + 1))
                        if q >= 3:
                            dve.wait_ge(*stage(f"mm_y_{l}", (q - 3) // 2 + 1))
                        for h in range(8):
                            ins = v.tensor_scalar(mt[:, q % 3, h, :], ps[:, 1 + 2 * (q % 2) + h // 4, (h % 4) * P:(h % 4 + 1) * P],
                                                  cum[:, d, t, g * 8 + h:g * 8 + h + 1], 0.0, ALU.subtract, ALU.min)
                        do.mark(ins, sem(f"diff_{l}"))
                    if q >= 1:
                        if (q - 1) % 2 == 0:
                            pu = (q - 1) // 2
                            dve.wait_ge(*stage(f"mm_cb_{l}", pu + 1))
                            for dd in range(2):
                                do.run(v.tensor_tensor(cbm[:, dd, :], ps[:, 0, 0:P], tri[dd], ALU.mult), sem(f"cbm_{l}"))
                        decayed(q - 1)
                        if (q - 1) % 2 == 1:
                            add_y((q - 1) // 2)
                end()

                dve.wait_ge(phase, phase_start(l, "gn"))
                dve.wait_ge(*stage(f"silu_z_{l}", nt))
                for t in range(nt):
                    do.run(v.tensor_tensor(y[:, t, :], y[:, t, :], zs[:, t, :], ALU.mult), sem(f"yz_{l}"))
                dve.wait_ge(*stage(f"sq_gn_{l}", SG * nt))
                inverse_ms(SG * nt, NCH, sem(f"inv_gn_{l}"))
                dve.wait_ge(*stage(f"rstd_gn_{l}", 1))
                for t in range(nt):
                    for g in range(SG):
                        yy = y[:, t, g * NCH:(g + 1) * NCH]
                        ins = v.scalar_tensor_tensor(yy, yy, stat[:, 2, 2 * t + g:2 * t + g + 1], nw[:, g * NCH:(g + 1) * NCH], ALU.mult, ALU.mult)
                    do.run(ins, sem(f"gn_rows_{l}"))
                if l + 1 < DEPTH:
                    modulation(2 * l + 2)
                end()

                dve.wait_ge(phase, phase_start(l, "merge"))
                for u in range(6 * nt):
                    bn, t = u // nt, u % nt
                    b, n = bn // 2, bn % 2
                    dve.wait_ge(*stage(f"gate_{l}", u + 1))
                    dve.wait_ge(*stage(f"mm_br_{l}", u + 1))
                    dst = acc[:, t, n * NCH:(n + 1) * NCH]
                    if b == 0:
                        do.run(v.tensor_tensor(dst, ps[:, 2 + u % 2, :], gs[:, u % 2, :], ALU.mult), sem(f"gated_{l}"))
                    else:
                        do.run(v.tensor_tensor(tmp[:, 0:NCH], ps[:, 2 + u % 2, :], gs[:, u % 2, :], ALU.mult), sem(f"gated_{l}"))
                        do.run(v.tensor_tensor(dst, dst, tmp[:, 0:NCH], ALU.add), sem(f"mg_rows_{l}") if bn == 5 else None)
                end()

                def post(name, src):
                    dve.wait_ge(phase, phase_start(l, name))
                    dve.wait_ge(*stage(f"sq_{name}_{l}", nt))
                    inverse_ms(nt, D, sem(f"inv_{name}_{l}"))
                    dve.wait_ge(*stage(f"rstd_{name}_{l}", 1))
                    dve.wait_ge(sem("gate_loaded"), 16 * (2 * l + 1 + (name == "post")))
                    for t in range(nt):
                        s = 0 if t < LAT_TILES else 1
                        do.run(v.scalar_tensor_tensor(tmp[:, :], src[:, t, :], stat[:, 2, t:t + 1], bc[:, 2, s, :], ALU.mult, ALU.mult))
                        do.run(v.tensor_tensor(x[:, t, :], x[:, t, :], tmp[:, :], ALU.add), sem(f"xup_{name}_{l}"))
                    end()

                post("out", ml)
                norm(1, nt)

                dve.wait_ge(phase, phase_start(l, "router"))
                do.run(v.memset(nor[:, :], NOROW), sem(f"norow_{l}"))
                dve.wait_ge(*stage(f"scores_{l}", 1))
                for t in range(nt):
                    R = lambda i: rtr[:, i, t, :]
                    do.run(v.tensor_tensor(R(1), R(0), brt[:, :], ALU.add))
                    for g in range(8):
                        do.mark(v.max(R(2)[:, g * 8:(g + 1) * 8], R(1)[:, g * 8:(g + 1) * 8]))
                    dve.wait_ge(do.own, do.n[do.own.name])
                    top2 = R(2).rearrange("p (g e) -> p g e", e=8)
                    gsum = R(3)[:, 0:8]
                    do.run(v.tensor_tensor(gsum.unsqueeze(2), top2[:, :, 0:1], top2[:, :, 1:2], ALU.add))
                    mine = gsum.unsqueeze(2).to_broadcast([P, 8, 8])
                    other = gsum.unsqueeze(1).to_broadcast([P, 8, 8])
                    g88 = lambda i: R(i).rearrange("p (g e) -> p g e", e=8)
                    do.run(v.tensor_tensor(g88(4), other, mine, ALU.is_equal))
                    do.run(v.tensor_tensor(R(4), R(4), cst[:, C_TRI8:C_TRI8 + 64], ALU.mult))
                    do.run(v.tensor_tensor(g88(5), other, mine, ALU.is_gt))
                    do.run(v.tensor_tensor(R(5), R(5), R(4), ALU.add))
                    do.run(v.tensor_reduce(R(3)[:, 8:16], g88(5), AX.X, ALU.add))
                    do.run(v.tensor_scalar(R(3)[:, 16:24], R(3)[:, 8:16], 3.5, None, ALU.is_lt))
                    gm = R(3)[:, 16:24].unsqueeze(2).to_broadcast([P, 8, 8])
                    do.run(v.tensor_tensor(g88(6), g88(1), gm, ALU.mult))
                    do.run(v.tensor_scalar(R(3)[:, 24:32], R(3)[:, 16:24], 1.0, -NEG, ALU.subtract, ALU.mult))
                    do.run(v.tensor_tensor(g88(6), g88(6), R(3)[:, 24:32].unsqueeze(2).to_broadcast([P, 8, 8]), ALU.add))
                    do.run(v.max(R(7)[:, 0:8], R(6)))
                    do.run(v.max_index(eiu[:, t, :], R(7)[:, 0:8], R(6)))
                    do.run(v.tensor_copy(eif[:, t, :], eiu[:, t, :]))
                    do.run(v.match_replace(R(8), R(7)[:, 0:8], R(6), 3 * NEG))
                    do.run(v.tensor_tensor(R(8), R(8), R(6), ALU.not_equal))
                    do.run(v.tensor_tensor(R(9), R(8), R(0), ALU.mult))
                    do.run(v.tensor_reduce(R(7)[:, 8:9], R(9), AX.X, ALU.add))
                    do.run(v.reciprocal(R(7)[:, 9:10], R(7)[:, 8:9]))
                    do.run(v.tensor_scalar(R(10), R(9), R(7)[:, 9:10], ROUTED_SCALE, ALU.mult, ALU.mult))
                do.run(v.memset(stat[:, 6, 0:1], 0.0), sem(f"masks_{l}"))
                for t in range(nt):
                    dve.wait_ge(*stage(f"ssilu_{l}", t + 1))
                    do.run(v.tensor_tensor(shs[:, t, :], shs[:, t, :], ps[:, 4 + t, D_EXP:2 * D_EXP], ALU.mult), sem(f"shid_{l}"))
                dve.wait_ge(*stage(f"mm_rank_{l}", 1))
                for t in range(nt):
                    over_e = lambda z: z.unsqueeze(1).to_broadcast([P, TOP_K, N_EXP])
                    do.run(v.tensor_tensor(oneh[:, :, :], over_e(cst[:, C_IOTA:C_IOTA + N_EXP]),
                                           eif[:, t, :].unsqueeze(2).to_broadcast([P, TOP_K, N_EXP]), ALU.is_equal))
                    do.run(v.tensor_tensor(onet[:, :, :], oneh[:, :, :], over_e(ps[:, 1, t * N_EXP:(t + 1) * N_EXP]), ALU.mult))
                    do.run(v.tensor_reduce(rnk[:, t, :], onet[:, :, :], AX.X, ALU.add))
                    do.run(v.tensor_tensor(onet[:, :, :], oneh[:, :, :], over_e(rtr[:, 10, t, :]), ALU.mult))
                    do.run(v.tensor_reduce(wk[:, t, :], onet[:, :, :], AX.X, ALU.add))
                    do.run(v.scalar_tensor_tensor(rnk[:, t, :], eif[:, t, :], float(CAP), rnk[:, t, :], ALU.mult, ALU.add))
                    do.run(v.tensor_scalar(dst_i[:, t, :], rnk[:, t, :], -1.0, None, ALU.add), sem(f"dest_{l}"))
                e64 = slice(0, N_EXP)
                do.run(v.tensor_copy(stat[e64, 1, 0:1], ps[e64, 0, 0:1]))
                do.run(v.tensor_tensor(stat[e64, 0, 0:3], stat[e64, 1, 0:1].to_broadcast([N_EXP, 3]), cst[e64, C_THR:C_THR + 3], ALU.is_gt))
                for i in range(2):
                    dve.wait_ge(*stage(f"h_written{i}_{l}", 16 * nt // 2))
                for i in range(EXP_SLOTS):
                    do.run(v.memset(xg[i][:, :], 0.0))
                end()

                dve.wait_ge(phase, phase_start(l, "moe"))

                dve.wait_ge(*stage(f"mm_tab_{l}", 1))
                do.run(v.tensor_copy(si[:, :], ps[:, 0, 0:BLOCKS * N_EXP]))
                do.run(v.tensor_single_scalar(gi[:, :], si[:, :], 3, ALU.arith_shift_right), sem(f"flags_{l}"))

                def stage_gather(e, slot):
                    v.tensor_copy(gstg[:, slot:slot + 1], gi[:, bass.ds(e, 1)]).then_inc(sem(f"staged_{l}"), 1)

                for e in range(EXP_SLOTS):
                    stage_gather(e, e)
                dve.wait_ge(*stage(f"mm_pos_{l}", 1))
                do.run(v.tensor_copy(stat[e64, 1, 0:6], ps[e64, 1, 0:6]))
                do.run(v.tensor_tensor(stat[e64, 1, 1:3], stat[e64, 1, 1:3], stat[e64, 1, 3:4].to_broadcast([N_EXP, 2]), ALU.add))
                do.run(v.tensor_tensor(stat[e64, 1, 2:3], stat[e64, 1, 2:3], stat[e64, 1, 4:5], ALU.add))
                do.run(v.tensor_tensor(stat[e64, 1, 0:3], stat[e64, 1, 0:3], stat[e64, 0, 0:3], ALU.mult))
                xoh = stat[e64, 4:6, :].rearrange("p a n -> p (a n)")
                for b in range(BLOCKS - 1):
                    do.run(v.tensor_scalar(xoh[:, b * 32:(b + 1) * 32], cst[e64, C_IOTA + 1:C_IOTA + 33], stat[e64, 1, b:b + 1], None, ALU.is_equal))
                do.run(v.tensor_reduce(stat[e64, 2, 0:1], stat[e64, 1, 3:6], AX.X, ALU.add), sem(f"places_{l}"))
                dve.wait_ge(*stage(f"mm_list_{l}", 1))
                do.run(v.tensor_copy(xl[0:1, 0:64], ps[0:1, 2, 0:64]))
                dve.sem_inc(sem(f"x_step_{l}"), X0)
                do.run(v.tensor_copy(xl[0:1, 64:65], stat[0:1, 2, 0:1]), sem(f"list_ready_{l}"))

                def ev_x(e, par):
                    dve.wait_ge(*stage(f"mm_xT_{l}", e + 1))
                    v.tensor_copy(xgT[:, par, 4:8, :], ps[:, 1, :].rearrange("p (k n) -> p k n", n=P)).then_inc(sem(f"ev_xv_{l}"), 1)

                def ev_y(e, j, scat):
                    dve.wait_ge(*stage(f"mm_down_{l}", e + 1))
                    if scat is not None:
                        dve.wait_ge(*stage(f"scat{j}_{l}", scat))
                    v.tensor_copy(sstg[:, j:j + 1], si[:, bass.ds(e, 1)])
                    v.tensor_copy(ysb[j][:, NCH:], ps[:, 5, :]).then_inc(sem(f"ev_yv_{l}"), 1)

                def step(e, r, j):
                    dve.wait_ge(*stage(f"silu_{l}", e + 1))
                    v.tensor_tensor(hsg[:, j % 2, :], hsg[:, j % 2, :], ps[:, 2, D_EXP:2 * D_EXP], ALU.mult).then_inc(sem(f"hidden_{l}"), 1)
                    static = isinstance(e, int)
                    if not (static and e == N_EXP - 1):
                        ev_x(e + 1, (j + 1) % 2)
                    if not (static and e == 0):
                        ev_y(e - 1, (j + 3) % 4, None if static and e < 5 else r * 16 + 16 * ((j - 5) // 4 + 1))
                    if not (static and e >= N_EXP - 4):
                        stage_gather(e + EXP_SLOTS, j % 4)

                ev_x(0, 0)
                for e in range(5):
                    step(e, 0, e)
                with dve.Fori(1, N_EXP // 4 - 2) as r:
                    for j in range(1, 5):
                        step(r * 4 + j, r, j)
                for e in range(N_EXP - 7, N_EXP):
                    step(e, e // 4, e % 4)
                ev_y(N_EXP - 1, 3, 16 * ((N_EXP - 5) // 4 + 1))

                for i in range(EXP_SLOTS):
                    dve.wait_ge(*stage(f"scat{i}_{l}", 16 * N_EXP // EXP_SLOTS))
                n = dve.value_load(xl[0:1, 64:65], min_val=0, max_val=max_extra(l))
                with dve.Fori(0, extra_groups(l)) as o:
                    with dve.If(o * XG < n):
                        with dve.Fori(0, XG) as k:
                            i = o * XG + k
                            with dve.If(i < n):
                                xstep = sem(f"x_step_{l}")
                                col = dve.value_load(xl[0:1, bass.ds(i + 32, 1)], min_val=0, max_val=BLOCKS * N_EXP - 1)
                                dve.wait_ge(xstep, i * XSTEPS + X0)
                                v.tensor_copy(gstg[:, 0:1], gi[:, bass.ds(col, 1)])
                                v.tensor_copy(sstg[:, 0:1], si[:, bass.ds(col, 1)]).then_inc(xstep, 1)
                                dve.wait_ge(xstep, i * XSTEPS + (X0 + 5))
                                v.tensor_tensor(hsg[:, 0, :], hsg[:, 0, :], ps[:, 2, D_EXP:2 * D_EXP], ALU.mult).then_inc(xstep, 1)

                for u in range(nt * 4):
                    t, kp = u // 4, u % 4
                    dve.wait_ge(*stage(f"comb{kp}_{l}", 16 * (t + 1)))
                    for i in range(2):
                        ins = v.scalar_tensor_tensor(acc[:, t, :], comb[:, kp, i, :], wk[:, t, 2 * kp + i:2 * kp + i + 1], acc[:, t, :], ALU.mult, ALU.add)
                        do.run(ins, sem(f"combined_{l}") if i == 1 else None)
                end()
                post("post", acc)


SHARED = {"x_updated": (("xup_out", (TILES, LAT_TILES)), ("xup_post", (TILES, LAT_TILES))),
          "rows_transposed": (("mm_gn", (2 * TILES, 2 * LAT_TILES)), ("mm_mg", (2 * TILES, 2 * LAT_TILES))),
          "transposed_rows_read": (("ev_gn", (2 * TILES, 2 * LAT_TILES)), ("ev_mg", (2 * TILES, 2 * LAT_TILES))),
          "route_products": tuple((f"mm_{n}", (1, 1)) for n in ("router", "rank", "tab", "pos", "list")),
          "route_steps": (("norow", (1, 1)), ("masks", (1, 1)), ("dest", (TILES, LAT_TILES)), ("flags", (1, 1)), ("places", (1, 1)), ("list_ready", (1, 1))),
          "decay_steps": tuple((n, (1, 1)) for n in ("nabs", "onep", "a_ready", "cum")),
          "decay_functions": tuple((n, (1, 1)) for n in ("expA", "softexp", "softln", "decays")),
          "squares_summed": (("sq_gn", (2 * TILES, 2 * LAT_TILES)), ("sq_out", (TILES, LAT_TILES)), ("sq_post", (TILES, LAT_TILES))),
          "rstd_found": tuple((f"rstd_{n}", (TILES, TILES) if n == "qk" else (1, 1)) for n in ("qk", "gn", "out", "post")),
          "inv_found": tuple((f"inv_{n}", (TILES, TILES) if n == "qk" else (1, 1)) for n in ("qk", "gn", "out", "post"))}

BEFORE = {'x_loaded': 32,
 'h_written0': 32,
 'h_written1': 32,
 'tab_cleared': 16,
 'tab_written': 512,
 'tab_read': 16,
 'comb0': 64,
 'comb1': 64,
 'comb2': 64,
 'comb3': 64,
 'mm_ccol': 1,
 'mm_norm': 16,
 'mm_xbc': 12,
 'mm_uT': 10,
 'mm_dt': 1,
 'mm_qkv': 12,
 'mm_cum': 1,
 'mm_qT': 16,
 'mm_score': 64,
 'mm_pT': 64,
 'mm_pv': 64,
 'mm_z': 8,
 'mm_oT': 8,
 'mm_state': 6,
 'mm_yoff': 6,
 'mm_cb': 8,
 'mm_r': 16,
 'mm_y': 8,
 'rows_transposed': 16,
 'mm_gate': 24,
 'mm_br': 24,
 'mm_out': 8,
 'route_products': 5,
 'mm_sgu': 4,
 'mm_shT': 4,
 'mm_sdown': 4,
 'sq_norm': 8,
 'rstd_norm': 2,
 'ev_norm': 16,
 'conv_in': 12,
 'conv_u': 12,
 'decay_functions': 4,
 'ev_proj': 12,
 'rstd_found': 7,
 'ev_qT': 16,
 'prob': 64,
 'ev_pT': 64,
 'ev_z': 8,
 'sinkexp': 4,
 'ev_oT': 8,
 'silu_z': 4,
 'expd': 16,
 'squares_summed': 16,
 'transposed_rows_read': 16,
 'gate': 24,
 'ev_out': 8,
 'scores': 1,
 'ssilu': 4,
 'ev_shT': 4,
 'ev_sy': 4,
 'inv_norm': 2,
 'hn_norm': 8,
 'xp_zero': 2,
 'conv': 12,
 'ev_uT': 10,
 'decay_steps': 4,
 'inv_found': 7,
 'roped': 8,
 'negmax': 64,
 'ev_o': 8,
 'sinkarg': 4,
 'xw': 6,
 'state': 6,
 'ev_yoff': 6,
 'scan_done': 1,
 'diff': 16,
 'cbm': 16,
 'm_ready': 16,
 'ev_y': 8,
 'yz': 4,
 'gn_rows': 4,
 'gated': 24,
 'mg_rows': 4,
 'x_updated': 8,
 'route_steps': 9,
 'shid': 4,
 'combined': 16}
EACH_EXPERT = ("mm_xT", "mm_gu", "mm_hT", "mm_down", "ev_xa", "ev_xv", "ev_hT", "ev_ya", "ev_yv", "silu", "hidden", "staged")
BEFORE.update({n: N_EXP for n in EACH_EXPERT})
BEFORE.update({f"{n}{i}": 16 * N_EXP // EXP_SLOTS for n in ("gath", "scat") for i in range(EXP_SLOTS)})
BEFORE.update({f"weights{i}": 48 * (N_EXP // EXP_SLOTS + (i == 2)) for i in range(EXP_SLOTS)})

_NAMES = ['x', 'c', 'ctx', 'c_ctx', 'w_ada', 'b_ada', 'g_mix_pre', 'g_mix_post', 'g_ffn_pre', 'g_ffn_post', 'w_in', 'g_q_a', 'g_k_a',
          'sink_w', 'ssm_conv_w', 'ssm_conv_b', 'ssm_dt_bias', 'ssm_a_log', 'ssm_d', 'ssm_norm', 'w_br_a', 'w_br_w', 'w_br_s', 'w_out',
          'w_router', 'b_router', 'we_gate', 'we_up', 'we_down', 'ws_gate', 'ws_up', 'ws_down']


def kernel(**inputs):
    import concourse.bacc as bacc
    from concourse.bass_utils import run_bass_kernel_spmd

    nc = bacc.Bacc("TRN2", target_bir_lowering=False, num_devices=1)
    arrays, aps = {}, {}
    for name in _NAMES:
        v = np.ascontiguousarray(inputs[name])
        arrays[f"in_{name}"] = v
        aps[name] = nc.dram_tensor(f"in_{name}", v.shape, mybir.dt.from_np(v.dtype), kind="ExternalInput").ap()
    arrays["in_constants"] = constants()
    cst_d = nc.dram_tensor("in_constants", (P, C_END), F32, kind="ExternalInput").ap()
    out = nc.dram_tensor("out", (1, SEG, D), F32, kind="ExternalOutput").ap()
    build(nc, aps, cst_d, out)
    r = run_bass_kernel_spmd(nc, [arrays], core_ids=[0])
    return r.results[0]["out"]
```
